# Optimizing a Trainium2 kernel written in Bass

```python
import math
import jax, jax.numpy as jnp
from jax import lax
import numpy as np

D_MODEL = 1024
BATCH = 1
SEQ = 512
DEPTH = 2

HEAD_DIM = 64
RET_HEADS = 4
RET_DK = 64
RET_DV = 128
DIL_HEADS = 4
SB_HEADS = 4
MIX_WIDTH = RET_HEADS * RET_DV + DIL_HEADS * HEAD_DIM + SB_HEADS * HEAD_DIM
IN_SIZES = (RET_HEADS * RET_DK, RET_HEADS * RET_DK, RET_HEADS * RET_DV, RET_HEADS * RET_DV,
            DIL_HEADS * HEAD_DIM, DIL_HEADS * HEAD_DIM, DIL_HEADS * HEAD_DIM,
            SB_HEADS * HEAD_DIM, SB_HEADS * HEAD_DIM, SB_HEADS * HEAD_DIM)
IN_WIDTH = sum(IN_SIZES)
D_FF = 2816
BLOCK = 128
RET_CHUNK = 128
WINDOWS = (128, 512, 2048)
DILATIONS = (1, 4, 16)
ROPE_THETA = 10000.0
ALPHA = (2.0 * DEPTH) ** 0.25
BETA = (8.0 * DEPTH) ** -0.25
LN_EPS = 1e-5
GN_EPS = 1e-6
FFN_RES = 0.5
N_MOD = 9


def _layer_norm(x, gain, bias):
    xf = x.astype(jnp.float32)
    mu = jnp.mean(xf, -1, keepdims=True)
    var = jnp.mean(jnp.square(xf - mu), -1, keepdims=True)
    y = (xf - mu) * lax.rsqrt(var + LN_EPS)
    return (y * gain.astype(jnp.float32) + bias.astype(jnp.float32)).astype(x.dtype)

def _modulate(x, shift, scale):
    return x * (1.0 + scale) + shift

def _post_norm(x, y, gate, res_w, gain, bias):
    return _layer_norm(ALPHA * x + res_w * (1.0 + gate) * y, gain, bias)

def _swiglu(h, w_gate, w_up, w_down):
    return (jax.nn.silu(h @ w_gate) * (h @ w_up)) @ w_down

def _split_heads(x, n_heads):
    b, s, _ = x.shape
    return x.reshape(b, s, n_heads, -1).transpose(0, 2, 1, 3)

def _merge_heads(x):
    b, h, s, d = x.shape
    return x.transpose(0, 2, 1, 3).reshape(b, s, h * d)

def _rotate(x, inv_freq):
    s, d = x.shape[2], x.shape[3]
    ang = jnp.arange(s, dtype=jnp.float32)[:, None] * inv_freq[None, :]
    cos, sin = jnp.cos(ang), jnp.sin(ang)
    xf = x.astype(jnp.float32)
    x1, x2 = xf[..., : d // 2], xf[..., d // 2:]
    return jnp.concatenate([x1 * cos - x2 * sin, x1 * sin + x2 * cos], -1).astype(x.dtype)

def _retention(q, k, v, g):
    b, h, s, dk = q.shape
    dv = v.shape[-1]
    c = RET_CHUNK
    n = s // c
    log_gamma = jnp.log1p(-jnp.exp2(-5.0 - jnp.arange(h, dtype=jnp.float32)))
    i = jnp.arange(c, dtype=jnp.float32)
    diff = i[:, None] - i[None, :]
    decay_in = jnp.where(diff >= 0, jnp.exp(log_gamma[:, None, None] * jnp.maximum(diff, 0.0)), 0.0)
    xi = jnp.exp(log_gamma[:, None] * (i + 1.0))
    zeta = jnp.exp(log_gamma[:, None] * (c - 1.0 - i))
    gamma_c = jnp.exp(log_gamma * c)
    qc = q.astype(jnp.float32).reshape(b, h, n, c, dk)
    kc = (k.astype(jnp.float32) * dk ** -0.5).reshape(b, h, n, c, dk)
    vc = v.astype(jnp.float32).reshape(b, h, n, c, dv)
    scores = jnp.einsum('bhncd,bhnmd->bhncm', qc, kc) * decay_in[None, :, None]
    o_inner = jnp.einsum('bhncm,bhnme->bhnce', scores, vc)
    kv = jnp.einsum('bhncd,bhnce->bhnde', kc * zeta[None, :, None, :, None], vc)

    def step(state, kv_n):
        return state * gamma_c[None, :, None, None] + kv_n, state

    init = jnp.zeros((b, h, dk, dv), jnp.float32)
    _, prev = lax.scan(step, init, jnp.moveaxis(kv, 2, 0))
    prev = jnp.moveaxis(prev, 0, 2)
    o_cross = jnp.einsum('bhncd,bhnde->bhnce', qc, prev) * xi[None, :, None, :, None]
    o = (o_inner + o_cross).reshape(b, h, s, dv)
    mu = jnp.mean(o, -1, keepdims=True)
    var = jnp.mean(jnp.square(o - mu), -1, keepdims=True)
    o = (o - mu) * lax.rsqrt(var + GN_EPS)
    return jax.nn.silu(g.astype(jnp.float32)) * _merge_heads(o)

def _dilated_attention(q, k, v):
    b, h, s, d = q.shape
    nb = s // BLOCK
    n_keys = max(w // dl for w, dl in zip(WINDOWS, DILATIONS)) + 1
    dist = jnp.array(DILATIONS, jnp.int32)[:, None] * jnp.arange(n_keys, dtype=jnp.int32)[None, :]
    in_win = dist <= jnp.array(WINDOWS, jnp.int32)[:, None]
    qb = (q.astype(jnp.float32) * d ** -0.5).reshape(b, h, nb, BLOCK, d).transpose(2, 0, 1, 3, 4)
    kf = k.astype(jnp.float32)
    vf = v.astype(jnp.float32)

    def block(args):
        q_blk, start = args
        t = start + jnp.arange(BLOCK, dtype=jnp.int32)
        idx = t[:, None, None] - dist[None]
        valid = (idx >= 0) & in_win[None]
        idx = jnp.maximum(idx, 0)
        k_g = jnp.take(kf, idx, axis=2)
        v_g = jnp.take(vf, idx, axis=2)
        sc = jnp.einsum('bhqd,bhqpjd->bhqpj', q_blk, k_g)
        sc = jnp.where(valid, sc, -jnp.inf)
        m = jnp.max(sc, -1)
        e = jnp.exp(sc - m[..., None])
        den = jnp.sum(e, -1)
        o_p = jnp.einsum('bhqpj,bhqpjd->bhqpd', e, v_g) / den[..., None]
        wgt = den * jnp.exp(m - jnp.max(m, -1, keepdims=True))
        wgt = wgt / jnp.sum(wgt, -1, keepdims=True)
        return jnp.einsum('bhqp,bhqpd->bhqd', wgt, o_p)

    out = lax.map(block, (qb, jnp.arange(nb, dtype=jnp.int32) * BLOCK))
    return out.transpose(1, 2, 0, 3, 4).reshape(b, h, s, d)

def _stick_breaking(q, k, v):
    b, h, s, d = q.shape
    nb = s // BLOCK
    qb = (q.astype(jnp.float32) * d ** -0.5).reshape(b, h, nb, BLOCK, d).transpose(2, 0, 1, 3, 4)
    kf = k.astype(jnp.float32)
    vf = v.astype(jnp.float32)
    key_pos = jnp.arange(s, dtype=jnp.int32)

    def block(args):
        q_blk, start = args
        t = start + jnp.arange(BLOCK, dtype=jnp.int32)
        z = jnp.einsum('bhqd,bhsd->bhqs', q_blk, kf)
        causal = key_pos[None, :] < t[:, None]
        log_beta = jax.nn.log_sigmoid(z)
        log_keep = jnp.where(causal, jax.nn.log_sigmoid(-z), 0.0)
        between = lax.cumsum(log_keep, axis=3, reverse=True) - log_keep
        a = jnp.where(causal, jnp.exp(log_beta + between), 0.0)
        return jnp.einsum('bhqs,bhsd->bhqd', a, vf)

    out = lax.map(block, (qb, jnp.arange(nb, dtype=jnp.int32) * BLOCK))
    return out.transpose(1, 2, 0, 3, 4).reshape(b, h, s, d)

def _token_mixer(h, w_in, w_out):
    proj = h @ w_in
    points, acc = [], 0
    for size in IN_SIZES[:-1]:
        acc += size
        points.append(acc)
    rq, rk, rv, rg, dq, dk, dv, sq, sk, sv = jnp.split(proj, points, axis=-1)
    ret_freq = 1.0 / (ROPE_THETA ** jnp.linspace(0.0, 1.0, RET_DK // 2, dtype=jnp.float32))
    rope_freq = 1.0 / (ROPE_THETA ** (jnp.arange(0, HEAD_DIM, 2, dtype=jnp.float32) / HEAD_DIM))
    y_ret = _retention(_rotate(_split_heads(rq, RET_HEADS), ret_freq),
                       _rotate(_split_heads(rk, RET_HEADS), ret_freq),
                       _split_heads(rv, RET_HEADS), rg)
    y_dil = _merge_heads(_dilated_attention(_rotate(_split_heads(dq, DIL_HEADS), rope_freq),
                                            _rotate(_split_heads(dk, DIL_HEADS), rope_freq),
                                            _split_heads(dv, DIL_HEADS)))
    y_sb = _merge_heads(_stick_breaking(_split_heads(sq, SB_HEADS), _split_heads(sk, SB_HEADS),
                                        _split_heads(sv, SB_HEADS)))
    y = jnp.concatenate([y_ret, y_dil, y_sb], -1).astype(h.dtype)
    return y @ w_out

def first_inputs(seed: int = 0) -> dict:
    key = jax.random.key(seed)
    ks = jax.random.split(key, 16)
    f32 = jnp.float32
    nrm = lambda k, shape, scale: jax.random.normal(k, shape, f32) * scale
    return {
        'x': nrm(ks[0], (BATCH, SEQ, D_MODEL), 1.0),
        'c': nrm(ks[1], (BATCH, D_MODEL), 1.0),
        'w_ada': nrm(ks[2], (DEPTH, D_MODEL, N_MOD * D_MODEL), 0.3 * D_MODEL ** -0.5),
        'b_ada': nrm(ks[3], (DEPTH, N_MOD * D_MODEL), 0.01),
        'ln_gain': 1.0 + nrm(ks[4], (DEPTH, 3, D_MODEL), 0.01),
        'ln_bias': nrm(ks[5], (DEPTH, 3, D_MODEL), 0.01),
        'ffn1_w_gate': nrm(ks[6], (DEPTH, D_MODEL, D_FF), D_MODEL ** -0.5),
        'ffn1_w_up': nrm(ks[7], (DEPTH, D_MODEL, D_FF), D_MODEL ** -0.5),
        'ffn1_w_down': nrm(ks[8], (DEPTH, D_FF, D_MODEL), BETA * D_FF ** -0.5),
        'w_in': nrm(ks[9], (DEPTH, D_MODEL, IN_WIDTH), D_MODEL ** -0.5),
        'w_out': nrm(ks[10], (DEPTH, MIX_WIDTH, D_MODEL), BETA * MIX_WIDTH ** -0.5),
        'ffn2_w_gate': nrm(ks[11], (DEPTH, D_MODEL, D_FF), D_MODEL ** -0.5),
        'ffn2_w_up': nrm(ks[12], (DEPTH, D_MODEL, D_FF), D_MODEL ** -0.5),
        'ffn2_w_down': nrm(ks[13], (DEPTH, D_FF, D_MODEL), BETA * D_FF ** -0.5),
    }

def first_block(x, c, w_ada, b_ada, ln_gain, ln_bias, ffn1_w_gate, ffn1_w_up, ffn1_w_down,
              w_in, w_out, ffn2_w_gate, ffn2_w_up, ffn2_w_down):
    cond = jax.nn.silu(c)
    for l in range(DEPTH):
        mod = cond @ w_ada[l] + b_ada[l]
        sh1, sc1, g1, sh2, sc2, g2, sh3, sc3, g3 = jnp.split(mod[:, None, :].astype(x.dtype), N_MOD, axis=-1)
        y = _swiglu(_modulate(x, sh1, sc1), ffn1_w_gate[l], ffn1_w_up[l], ffn1_w_down[l])
        x = _post_norm(x, y, g1, FFN_RES, ln_gain[l, 0], ln_bias[l, 0])
        y = _token_mixer(_modulate(x, sh2, sc2), w_in[l], w_out[l])
        x = _post_norm(x, y, g2, 1.0, ln_gain[l, 1], ln_bias[l, 1])
        y = _swiglu(_modulate(x, sh3, sc3), ffn2_w_gate[l], ffn2_w_up[l], ffn2_w_down[l])
        x = _post_norm(x, y, g3, FFN_RES, ln_gain[l, 2], ln_bias[l, 2])
    return x


ROT_DIM = HEAD_DIM // 4
ROPE_THETA_2 = 500000.0
A_HEADS = (D_MODEL // 2) // (2 * HEAD_DIM)
B_HEADS = (D_MODEL // 2) // HEAD_DIM
KV_LORA = D_MODEL // 4
IDX_HEADS = 4
IDX_DIM = 64
TOPK_MAX = 256
QBLOCK = 128
C_WIDTH = D_MODEL // 2
CONV_W = 3
POOL_WINDOWS = (2, 4, 8, 16)
POOL_WIDTH = D_MODEL // 2
POOL_GROUP = POOL_WIDTH // len(POOL_WINDOWS)
MEM_LEN = 256
X_HEADS = 4
X_HEAD_DIM = D_MODEL // 8
D_FF_2 = 4 * D_MODEL
EPS = 1e-6
N_EVEN = (DEPTH + 1) // 2
N_ODD = DEPTH // 2
EVEN_SPLITS = (A_HEADS * 2 * HEAD_DIM, A_HEADS * 2 * HEAD_DIM, A_HEADS * 2 * HEAD_DIM,
               B_HEADS * HEAD_DIM, KV_LORA, IDX_HEADS * IDX_DIM, IDX_DIM, IDX_HEADS)
EVEN_IN = sum(EVEN_SPLITS)
ODD_SPLITS = (C_WIDTH, C_WIDTH, C_WIDTH, POOL_WIDTH)
ODD_IN = sum(ODD_SPLITS)


def rmsnorm(x, g):
    xf = x.astype(jnp.float32)
    y = xf * lax.rsqrt(jnp.mean(xf * xf, axis=-1, keepdims=True) + EPS)
    return (y * g.astype(jnp.float32)).astype(x.dtype)

def _split(a, sizes):
    return jnp.split(a, np.cumsum(sizes)[:-1].tolist(), axis=-1)

def rope_tables(positions):
    inv = ROPE_THETA_2 ** (-jnp.arange(0, ROT_DIM, 2, dtype=jnp.float32) / ROT_DIM)
    ang = positions.astype(jnp.float32)[..., None] * inv
    return jnp.cos(ang)[:, :, None, :], jnp.sin(ang)[:, :, None, :]

def rope(x, cos, sin):
    half = ROT_DIM // 2
    xr, xp = x[..., :ROT_DIM], x[..., ROT_DIM:]
    x1, x2 = xr[..., :half], xr[..., half:]
    rot = jnp.concatenate([x1 * cos - x2 * sin, x2 * cos + x1 * sin], axis=-1)
    return jnp.concatenate([rot.astype(x.dtype), xp], axis=-1)

def even_mixer(h, cos, sin, w_in, gq_a, gk_a, lam, lam_init, g_sub_a,
               g_kv_b, w_kv_up_b, gq_b, gk_b, g_kidx, w_out, k_sel):
    B, S, _ = h.shape
    nb = S // QBLOCK

    def to_blocks(a):
        return jnp.moveaxis(a.reshape((B, nb, QBLOCK) + a.shape[2:]), 1, 0)

    def from_blocks(o):
        return jnp.moveaxis(o, 0, 1).reshape((B, S) + o.shape[3:])

    qa, ka, va, qb, ckv, qi, ki, wi = _split(h @ w_in, EVEN_SPLITS)

    qa = rope(rmsnorm(qa.reshape(B, S, 2 * A_HEADS, HEAD_DIM), gq_a), cos, sin)
    qa = qa.reshape(B, S, A_HEADS, 2, HEAD_DIM)
    ka = rope(rmsnorm(ka.reshape(B, S, 2 * A_HEADS, HEAD_DIM), gk_a), cos, sin)
    ka = ka.reshape(B, S, A_HEADS, 2, HEAD_DIM)
    va = va.reshape(B, S, A_HEADS, 2 * HEAD_DIM)

    kb, vb = jnp.split(rmsnorm(ckv, g_kv_b) @ w_kv_up_b, 2, axis=-1)
    qb = rope(rmsnorm(qb.reshape(B, S, B_HEADS, HEAD_DIM), gq_b), cos, sin)
    kb = rope(rmsnorm(kb.reshape(B, S, B_HEADS, HEAD_DIM), gk_b), cos, sin)
    vb = vb.reshape(B, S, B_HEADS, HEAD_DIM)
    qi = rope(qi.reshape(B, S, IDX_HEADS, IDX_DIM), cos, sin)
    ki = rope(rmsnorm(ki, g_kidx)[:, :, None, :], cos, sin)[:, :, 0, :]
    wi = wi.astype(jnp.float32) * (IDX_HEADS ** -0.5 * IDX_DIM ** -0.5)

    kpos = jnp.arange(S)
    scale = HEAD_DIM ** -0.5

    def a_block(args):
        q, t0 = args
        qpos = t0 + jnp.arange(QBLOCK)
        causal = kpos[None, :] <= qpos[:, None]
        logits = jnp.einsum('bqhcd,bkhcd->bhcqk', q, ka).astype(jnp.float32) * scale
        p = jax.nn.softmax(jnp.where(causal, logits, -jnp.inf), axis=-1)
        attn = p[:, :, 0] - lam * p[:, :, 1]
        return jnp.einsum('bhqk,bkhe->bqhe', attn.astype(va.dtype), va)

    def b_block(args):
        q, qidx, widx, t0 = args
        qpos = t0 + jnp.arange(QBLOCK)
        causal = kpos[None, :] <= qpos[:, None]
        isc = jax.nn.relu(jnp.einsum('bqhd,bkd->bqhk', qidx, ki).astype(jnp.float32))
        isc = jnp.einsum('bqhk,bqh->bqk', isc, widx)
        isc = jnp.where(causal[None], isc, -jnp.inf)
        _, idx = lax.top_k(isc, k_sel)
        k_g = jax.vmap(lambda a, i: a[i])(kb, idx)
        v_g = jax.vmap(lambda a, i: a[i])(vb, idx)
        logits = jnp.einsum('bqhd,bqkhd->bhqk', q, k_g).astype(jnp.float32) * scale
        valid = (idx <= qpos[None, :, None])[:, None]
        p = jax.nn.softmax(jnp.where(valid, logits, -jnp.inf), axis=-1)
        return jnp.einsum('bhqk,bqkhd->bqhd', p.astype(vb.dtype), v_g)

    starts = jnp.arange(nb, dtype=jnp.int32) * QBLOCK
    out_a = from_blocks(lax.map(a_block, (to_blocks(qa), starts)))
    out_a = rmsnorm(out_a, g_sub_a) * (1.0 - lam_init)
    out_b = from_blocks(lax.map(b_block, (to_blocks(qb), to_blocks(qi), to_blocks(wi), starts)))
    y = jnp.concatenate([out_a.reshape(B, S, -1), out_b.reshape(B, S, -1)], axis=-1)
    return y @ w_out

def pool_mixer(z, w_pool, pool_scale):
    B, S, _ = z.shape
    zf = z.astype(jnp.float32).reshape(B, S, len(POOL_WINDOWS), POOL_GROUP)
    csp = jnp.pad(jnp.cumsum(zf, axis=1), ((0, 0), (1, 0), (0, 0), (0, 0)))
    t = jnp.arange(S)
    outs = []
    for g, w in enumerate(POOL_WINDOWS):
        lo = jnp.maximum(t + 1 - w, 0)
        win_sum = csp[:, 1:, g] - csp[:, lo, g]
        cnt = jnp.minimum(t + 1, w).astype(jnp.float32)
        outs.append(win_sum / cnt[None, :, None] - zf[:, :, g])
    pooled = jnp.stack(outs, axis=2).astype(z.dtype)
    y = jnp.einsum('bsgc,gcd->bsgd', pooled, w_pool).reshape(B, S, POOL_WIDTH)
    return y * pool_scale

def odd_mixer(h, w_in, conv_w, w_pool, pool_scale, w_out):
    gb, gc, hc, zd = _split(h @ w_in, ODD_SPLITS)
    u = gc * hc
    conv = lax.conv_general_dilated(
        u, conv_w[:, None, :].astype(u.dtype), window_strides=(1,),
        padding=[(CONV_W - 1, 0)], dimension_numbers=('NWC', 'WIO', 'NWC'),
        feature_group_count=C_WIDTH)
    yc = gb * conv
    yd = pool_mixer(zd, w_pool, pool_scale)
    return jnp.concatenate([yc, yd], axis=-1) @ w_out

def cross_attn(h, m, wq, wkv, gq, gk, wo):
    B, S, _ = h.shape
    q = rmsnorm((h @ wq).reshape(B, S, X_HEADS, X_HEAD_DIM), gq)
    k, v = jnp.split(m @ wkv, 2, axis=-1)
    k = rmsnorm(k.reshape(B, -1, X_HEADS, X_HEAD_DIM), gk)
    v = v.reshape(B, -1, X_HEADS, X_HEAD_DIM)
    logits = jnp.einsum('bqhd,bkhd->bhqk', q, k).astype(jnp.float32) * X_HEAD_DIM ** -0.5
    p = jax.nn.softmax(logits, axis=-1)
    o = jnp.einsum('bhqk,bkhd->bqhd', p.astype(v.dtype), v).reshape(B, S, -1)
    return o @ wo

def mlp(h, w_up, w_down):
    return jnp.square(jax.nn.relu(h @ w_up)) @ w_down

def second_inputs(seed: int = 0) -> dict:
    key = jax.random.key(seed)
    ks = iter(jax.random.split(key, 48))

    def nrm(shape, scale):
        return scale * jax.random.normal(next(ks), shape, jnp.float32)

    def gain(shape):
        return 1.0 + 0.05 * jax.random.normal(next(ks), shape, jnp.float32)

    d = D_MODEL
    return {
        'x': nrm((BATCH, SEQ, d), 1.0),
        'mem': nrm((BATCH, MEM_LEN, d), 1.0),
        'positions': jnp.tile(jnp.arange(SEQ, dtype=jnp.int32)[None, :], (BATCH, 1)),
        'g_mix': gain((DEPTH, d)),
        'g_xattn': gain((DEPTH, d)),
        'g_mem': gain((DEPTH, d)),
        'g_mlp': gain((DEPTH, d)),
        'wq_x': nrm((DEPTH, d, X_HEADS * X_HEAD_DIM), d ** -0.5),
        'wkv_x': nrm((DEPTH, d, 2 * X_HEADS * X_HEAD_DIM), d ** -0.5),
        'gq_x': gain((DEPTH, X_HEAD_DIM)),
        'gk_x': gain((DEPTH, X_HEAD_DIM)),
        'wo_x': nrm((DEPTH, X_HEADS * X_HEAD_DIM, d), (X_HEADS * X_HEAD_DIM) ** -0.5),
        'w_up': nrm((DEPTH, d, D_FF_2), d ** -0.5),
        'w_down': nrm((DEPTH, D_FF_2, d), D_FF_2 ** -0.5),
        'w_in_e': nrm((N_EVEN, d, EVEN_IN), d ** -0.5),
        'gq_a': gain((N_EVEN, HEAD_DIM)),
        'gk_a': gain((N_EVEN, HEAD_DIM)),
        'lam_q1': nrm((N_EVEN, HEAD_DIM), 0.1),
        'lam_k1': nrm((N_EVEN, HEAD_DIM), 0.1),
        'lam_q2': nrm((N_EVEN, HEAD_DIM), 0.1),
        'lam_k2': nrm((N_EVEN, HEAD_DIM), 0.1),
        'g_sub_a': gain((N_EVEN, 2 * HEAD_DIM)),
        'g_kv_b': gain((N_EVEN, KV_LORA)),
        'w_kv_up_b': nrm((N_EVEN, KV_LORA, 2 * B_HEADS * HEAD_DIM), KV_LORA ** -0.5),
        'gq_b': gain((N_EVEN, HEAD_DIM)),
        'gk_b': gain((N_EVEN, HEAD_DIM)),
        'g_kidx': gain((N_EVEN, IDX_DIM)),
        'w_out_e': nrm((N_EVEN, d, d), d ** -0.5),
        'w_in_o': nrm((N_ODD, d, ODD_IN), d ** -0.5),
        'conv_w': nrm((N_ODD, CONV_W, C_WIDTH), CONV_W ** -0.5),
        'w_pool': nrm((N_ODD, len(POOL_WINDOWS), POOL_GROUP, POOL_GROUP), POOL_GROUP ** -0.5),
        'pool_scale': gain((N_ODD, POOL_WIDTH)),
        'w_out_o': nrm((N_ODD, d, d), d ** -0.5),
    }

def second_block(x, mem, positions, g_mix, g_xattn, g_mem, g_mlp, wq_x, wkv_x, gq_x, gk_x,
              wo_x, w_up, w_down, w_in_e, gq_a, gk_a, lam_q1, lam_k1, lam_q2, lam_k2,
              g_sub_a, g_kv_b, w_kv_up_b, gq_b, gk_b, g_kidx, w_out_e, w_in_o, conv_w,
              w_pool, pool_scale, w_out_o):
    S = x.shape[1]
    k_sel = min(TOPK_MAX, S // 4)
    cos, sin = rope_tables(positions)
    for i in range(DEPTH):
        j = i // 2
        h = rmsnorm(x, g_mix[i])
        if i % 2 == 0:
            lam_init = 0.8 - 0.6 * float(np.exp(-0.3 * i))
            f32 = jnp.float32
            lam = (jnp.exp(jnp.sum(lam_q1[j].astype(f32) * lam_k1[j].astype(f32)))
                   - jnp.exp(jnp.sum(lam_q2[j].astype(f32) * lam_k2[j].astype(f32)))
                   + lam_init)
            mix = even_mixer(h, cos, sin, w_in_e[j], gq_a[j], gk_a[j], lam, lam_init,
                             g_sub_a[j], g_kv_b[j], w_kv_up_b[j], gq_b[j], gk_b[j],
                             g_kidx[j], w_out_e[j], k_sel)
        else:
            mix = odd_mixer(h, w_in_o[j], conv_w[j], w_pool[j], pool_scale[j], w_out_o[j])
        x = x + mix
        x = x + cross_attn(rmsnorm(x, g_xattn[i]), rmsnorm(mem, g_mem[i]),
                           wq_x[i], wkv_x[i], gq_x[i], gk_x[i], wo_x[i])
        x = x + mlp(rmsnorm(x, g_mlp[i]), w_up[i], w_down[i])
    return x


def setup_inputs(seed=0):
    out = dict(first_inputs(seed))
    for name, value in second_inputs(seed + 1).items():
        if name != "x":
            out[name + "_2"] = value
    return out


def reference(
    x, c, w_ada, b_ada, ln_gain, ln_bias, ffn1_w_gate, ffn1_w_up, ffn1_w_down, w_in, w_out,
    ffn2_w_gate, ffn2_w_up, ffn2_w_down, mem_2, positions_2, g_mix_2, g_xattn_2, g_mem_2,
    g_mlp_2, wq_x_2, wkv_x_2, gq_x_2, gk_x_2, wo_x_2, w_up_2, w_down_2, w_in_e_2, gq_a_2,
    gk_a_2, lam_q1_2, lam_k1_2, lam_q2_2, lam_k2_2, g_sub_a_2, g_kv_b_2, w_kv_up_b_2, gq_b_2,
    gk_b_2, g_kidx_2, w_out_e_2, w_in_o_2, conv_w_2, w_pool_2, pool_scale_2, w_out_o_2,
):
    x = first_block(
        x, c, w_ada, b_ada, ln_gain, ln_bias, ffn1_w_gate, ffn1_w_up, ffn1_w_down, w_in, w_out,
        ffn2_w_gate, ffn2_w_up, ffn2_w_down,
    )
    return second_block(
        x, mem_2, positions_2, g_mix_2, g_xattn_2, g_mem_2, g_mlp_2, wq_x_2, wkv_x_2, gq_x_2,
        gk_x_2, wo_x_2, w_up_2, w_down_2, w_in_e_2, gq_a_2, gk_a_2, lam_q1_2, lam_k1_2,
        lam_q2_2, lam_k2_2, g_sub_a_2, g_kv_b_2, w_kv_up_b_2, gq_b_2, gk_b_2, g_kidx_2,
        w_out_e_2, w_in_o_2, conv_w_2, w_pool_2, pool_scale_2, w_out_o_2,
    )


_drawn_inputs = setup_inputs


def setup_inputs(seed=0):
    import zlib

    import numpy as np

    out = dict(_drawn_inputs(seed))
    spreads = {}
    factors = {'g_xattn_2': 8.0,
     'g_mem_2': 5.845,
     'gq_x_2': 8.0,
     'gk_x_2': 8.0,
     'lam_q1_2': 6.734,
     'lam_q2_2': 6.533,
     'g_kv_b_2': 5.274,
     'gq_b_2': 8.0,
     'gk_b_2': 8.0,
     'g_kidx_2': 3.614,
     'pool_scale_2': 3.533}
    for name, (base, spread) in spreads.items():
        noise = np.random.default_rng([zlib.crc32(name.encode()), seed]).standard_normal(out[name].shape)
        drawn = base * np.exp(spread * noise) if base else spread * noise
        out[name] = __import__('jax').numpy.asarray(drawn.astype(out[name].dtype))
    for name, factor in factors.items():
        out[name] = (out[name] * factor).astype(out[name].dtype)
    return out
```

```python
from contextlib import ExitStack

import numpy as np

import concourse.bass as bass
from concourse import mybir

F32 = mybir.dt.float32
F32R = mybir.dt.float32r
I32 = mybir.dt.int32
ALU = mybir.AluOpType
ACT = mybir.ActivationFunctionType
AXX = mybir.AxisListType.X

P = 128
S = 512
D = 1024
NT = D // P
ALPHA = 4.0 ** 0.25
NEG = -1e30
TAKEN = -3e38
MAGIC = 12582912.0
TWO_PI = 6.283185307179586
C1 = 6.28125
C2 = float(np.float32(TWO_PI - C1))
C3 = float(np.float32(TWO_PI - C1 - C2))
PI_LOW = float(np.nextafter(np.float32(np.pi), np.float32(0)))
FFN_GROUPS = [(0, 8), (8, 8), (16, 6)]
MLP_GROUPS = [(0, 8), (8, 8), (16, 8), (24, 8)]

VEC = {}


def _vec_layout():
    at = 0
    for name, n in (("c", 8), ("b_ada", 144), ("ln_gain", 48), ("ln_bias", 48), ("g_mix", 16),
                    ("g_xattn", 16), ("g_mem", 16), ("g_mlp", 16), ("gq_x", 2), ("gk_x", 2),
                    ("gq_a", 1), ("gk_a", 1), ("gq_b", 1), ("gk_b", 1), ("g_kidx", 1),
                    ("g_sub_a", 1), ("g_kv_b", 2), ("conv_w", 12), ("pool_scale", 4),
                    ("lam", 4)):
        VEC[name] = (at, n)
        at += n
    return at


NVEC = _vec_layout()
SEMS = ["pe", "act", "dve", "pool", "st0", "st1", "st2", "cc", "vec", "x", "c1", "c2", "misc", "mem", "out"]


def flat(ws):
    for w in ws:
        if w is None:
            continue
        if isinstance(w, list):
            yield from flat(w)
        else:
            yield w


class Queue:

    def __init__(self, key, eng, sems):
        self.key, self.eng, self.sems = key, eng, sems
        self.n, self.seen = 0, {}

    def __call__(self, waits, fn, sig=True, sem=None):
        need = []
        for k, v in flat(waits):
            if self.seen.get(k, 0) < v:
                self.seen[k] = v
                need = [x for x in need if x[0] != k] + [(k, v)]
        if sig and sem is None:
            self.n += 1
        if self.eng is not None:
            for k, v in need:
                self.eng.wait_ge(self.sems[k], v)
            ins = fn(self.eng)
            if sem is not None:
                ins.then_inc(self.sems[sem], 16)
            elif sig:
                ins.then_inc(self.sems[self.key], 1)
        return (self.key, self.n)


class Slot:

    def __init__(self, ap):
        self.ap, self.w, self.busy = ap, [], False

    def done(self, *tokens):
        self.w = list(tokens)
        self.busy = False


class Ring:
    def __init__(self, aps):
        self.slots, self.i = [Slot(a) for a in aps], 0

    def get(self):
        for _ in self.slots:
            s = self.slots[self.i % len(self.slots)]
            self.i += 1
            if not s.busy:
                break
        assert not s.busy
        s.busy = True
        return s


class Prog:
    def __init__(self, nc, dram, out, plan, mem, tag):
        self.nc, self.dram, self.out, self.plan, self.tag = nc, dram, out, plan, tag
        live = plan is not None
        sems = mem["sems"]
        self.pe = Queue("pe", nc.tensor if live else None, sems)
        self.act = Queue("act", nc.scalar if live else None, sems)
        self.dve = Queue("dve", nc.vector if live else None, sems)
        self.pool = Queue("pool", nc.gpsimd if live else None, sems)
        self.sp = Queue("sp", nc.sync if live else None, sems)
        self.psum = mem["psum"]
        self.XR = mem["XR"]
        self.HH = mem["HH"]
        self.HL = mem["HL"]
        self.STAGE = mem["STAGE"]
        self.WH = mem["WH"]
        self.WL = mem["WL"]
        self.TMP = mem["TMP"]
        self.CC = mem["CC"]
        self.C = mem["C"]
        self.VEC = mem["VEC"]
        self.MOD = mem["MOD"]
        self.COND = mem["COND"]
        self.SM = mem["SM"]
        self.NY = mem["NY"]
        self.NV = mem["NV"]
        self.NA = mem["NA"]
        self.NU = mem["NU"]
        self.NG = mem["NG"]
        self.LAM = mem["LAM"]
        self.POSI = mem["POSI"]
        self.COS2 = mem["COS2"]
        self.SIN2 = mem["SIN2"]
        self.c1 = mem["c1"]
        self.c2 = mem["c2"]
        self.c2n = mem["c2n"]
        self.NS = mem["NS"]
        self.NW = mem["NW"]
        self.ident = mem["ident"]
        self.one = mem["one"]
        self.later = mem["later"]
        self.perm1 = mem["perm1"]
        self.perm2 = mem["perm2"]
        self.causal = mem["causal"]
        self.strict = mem["strict"]
        self.blk = mem["blk"]
        self.col1024 = mem["col1024"]
        self.col256 = mem["col256"]
        self.col128 = mem["col128"]
        self.inv = mem["inv"]
        self.nalloc = 0
        self.order = []
        self.banks = Ring([b[:, :] for b in self.psum[0:6]])
        self.held = Ring([b[:, :] for b in self.psum[6:8]])
        self.tmp = Ring([self.TMP[:, i, :] for i in range(self.TMP.shape[1])])
        self.small = Ring([self.SM[:, i, :] for i in range(self.SM.shape[1])])
        self.newt = Slot(None)
        self.yr = Ring([self.NY[:, i, :] for i in range(2)])
        self.ndma = {}
        self.taken = 0
        self.nload = 0
        self.nsplit = 0
        self.stage_w = {}
        self.landed = {}
        self.split_of = {}
        self.wslot = [[], []]
        self.nw = 0
        self.base = []
        self.fill = []
        self.hfree = []
        self.ada_acc = None
        self.bg, self.active, self.depth = [], [], 5

    def alloc(self, ctx, name, shape, dt=F32):
        self.nalloc += 1
        return ctx.enter_context(self.nc.sbuf_tensor(f"{name}_{self.tag}{self.nalloc}", shape, dt))

    def more_tmp(self, ctx, n):
        t = self.alloc(ctx, "xt", [P, n, S])
        new = [Slot(t[:, i, :]) for i in range(n)]
        for x in new:
            x.w = self.base
        self.tmp.slots.extend(new)
        return new

    def less_tmp(self, new):
        assert not any(x.busy for x in new)
        self.tmp.slots = [x for x in self.tmp.slots if x not in new]

    def barrier(self):
        self.base = [(q.key, q.n) for q in (self.pe, self.act, self.dve, self.pool) if q.n]

    def load(self, key, dst, src, waits=()):
        n = self.ndma.get(key, 0) + 1
        self.ndma[key] = n
        self.sp(list(waits), lambda e: e.dma_start(dst, src), sem=key)
        return (key, 16 * n)

    def issue(self, j):
        if j >= len(self.plan):
            return
        name, idx, raw = self.plan[j]
        src = self.dram[name][idx]
        n = src.shape[-1]
        slot = j % self.NS
        self.landed[j] = self.load(f"st{slot}", self.STAGE[:, slot, 0:n], src,
                                   self.stage_w.get(j - self.NS, []))

    def split(self, j):
        name, idx, raw = self.plan[j]
        n = self.dram[name][idx].shape[-1]
        slot, ws = j % self.NS, self.nw % self.NW
        self.nw += 1
        src, wh, wl = self.STAGE[:, slot, 0:n], self.WH[:, ws, 0:n], self.WL[:, ws, 0:n]
        free = self.wslot[ws]
        th = self.act([self.landed[j], free], lambda e: e.activation(wh, src, ACT.Copy))
        cut = n * 5 // 8
        t1 = self.pool([self.landed[j], th, free], lambda e: e.tensor_tensor(
            wl[:, 0:cut], src[:, 0:cut], wh[:, 0:cut].bitcast(F32), ALU.subtract))
        t2 = self.dve([self.landed[j], th, free], lambda e: e.tensor_tensor(
            wl[:, cut:n], src[:, cut:n], wh[:, cut:n].bitcast(F32), ALU.subtract))
        self.stage_w[j] = [t1, t2]
        self.split_of[j] = (wh, wl, [th, t1, t2], ws)
        self.issue(j + self.NS)

    def take(self, name, idx, raw=False):
        j = self.taken
        self.taken += 1
        self.order.append((name, idx, raw))
        if self.plan is None:
            a = self.WH[:, 0, :]
            return (j, self.STAGE[:, 0, :], [], 0) if raw else (j, a, a, [], 0)
        assert self.plan[j] == (name, idx, raw)
        if j == 0:
            for i in range(self.NS):
                self.issue(i)
        if raw:
            return j, self.STAGE[:, j % self.NS, :], self.landed[j], 0
        done = 0
        for i in range(max(j, self.nsplit), len(self.plan)):
            if i > j:
                done += 1
            if done > self.NW - 1 or i >= j + self.NS:
                break
            if self.plan[i][2]:
                if i > j:
                    done -= 1
                continue
            if i > j and (i not in self.landed):
                break
            if i >= self.nsplit:
                self.split(i)
                self.nsplit = i + 1
        wh, wl, toks, ws = self.split_of[j]
        return j, wh, wl, toks, ws

    def release(self, ch, token):
        if self.plan is not None:
            self.wslot[ch[-1]] = [token]

    def release_raw(self, ch, token):
        if self.plan is not None:
            self.stage_w[ch[0]] = [token]
            self.issue(ch[0] + self.NS)

    def mm(self, waits, out, lhsT, rhs, start=True, stop=True, sig=False):
        return self.pe(waits, lambda e: e.matmul(out, lhsT, rhs, start=start, stop=stop,
                                                 skip_group_check=True), sig=sig)

    def mm3(self, waits, out, ah, al, bh, bl, start, stop, sig=False):
        self.mm(waits, out, ah, bh, start, False)
        self.mm([], out, ah, bl, False, False)
        return self.mm([], out, al, bh, False, stop, sig)

    def feat(self, ch, kt, nc_, t, X, xt, N=S, M=P, off=None):
        _, wh, wl, toks, _ = ch
        whv = wh[:, 0:kt * nc_].rearrange("p (k n) -> p k n", k=kt)
        wlv = wl[:, 0:kt * nc_].rearrange("p (k n) -> p k n", k=kt)
        a = t * P if off is None else off
        b = self.banks.get()
        for k in range(kt):
            tok = self.mm3([toks, xt[k], b.w], b.ap[0:M, 0:N], whv[:, k, a:a + M], wlv[:, k, a:a + M],
                           X[0][:, k, 0:N], X[1][:, k, 0:N], k == 0, k == kt - 1, sig=(k == kt - 1))
            if k % 4 == 3:
                self.tick()
        return b, tok

    def feat2(self, ch, kt, X, xt, eager=False, N=S):
        if not eager:
            for t in range(2):
                yield self.feat(ch, kt, 256, t, X, xt, N)
            return
        _, wh, wl, toks, _ = ch
        whv = wh[:, 0:kt * 256].rearrange("p (k n) -> p k n", k=kt)
        wlv = wl[:, 0:kt * 256].rearrange("p (k n) -> p k n", k=kt)
        bs = [self.banks.get(), self.banks.get()]
        tok = [None, None]
        for k in range(kt):
            for t in range(2):
                tok[t] = self.mm3([toks, xt[k], bs[t].w], bs[t].ap[:, 0:N], whv[:, k, t * P:(t + 1) * P],
                                  wlv[:, k, t * P:(t + 1) * P], X[0][:, k, 0:N], X[1][:, k, 0:N],
                                  k == 0, k == kt - 1, sig=(k == kt - 1))
            if k % 2 == 1:
                self.tick()
        yield bs[0], tok[0]
        yield bs[1], tok[1]

    def toks(self, ch, kt, nc_, tiles, X, xt, cols=None, n=None, view=None):
        _, wh, wl, toks, _ = ch
        whv = wh[:, 0:kt * nc_].rearrange("p (k n) -> p k n", k=kt)
        wlv = wl[:, 0:kt * nc_].rearrange("p (k n) -> p k n", k=kt)
        c0, n = (0, nc_) if cols is None else cols
        b = self.banks.get()
        for q, i in enumerate(tiles):
            for k in range(kt):
                tok = self.mm3([toks, xt[k], b.w], b.ap[:, q * n:(q + 1) * n],
                               X[0][:, k, i * P:(i + 1) * P], X[1][:, k, i * P:(i + 1) * P],
                               whv[:, k, c0:c0 + n], wlv[:, k, c0:c0 + n],
                               k == 0, k == kt - 1, sig=(k == kt - 1 and i == tiles[-1]))
            if n == 256:
                self.tick()
        return b, tok

    def parts(self, hi, lo, src, waits, lo_on=None, free=()):
        th = self.act([waits, list(free)], lambda e: e.activation(hi, src, ACT.Copy))
        q = lo_on or self.pool
        tl = q([waits, th, list(free)], lambda e: e.tensor_tensor(lo, src, hi.bitcast(F32), ALU.subtract))
        return [th, tl]

    def stat(self, b, col, step, src, tok, rhs, start, stop, n=1, tiles=4):
        for i in range(tiles):
            t = self.mm([tok, b.w], b.ap[:, i * step + col:i * step + col + n], src[:, i * P:(i + 1) * P],
                        rhs, start if i == 0 else False, stop, sig=(i == tiles - 1))
        return t

    def rsqrt(self, src, n, eps, waits):
        y = self.yr.get()
        d, v, u, a, g, yy = self.dve, self.NV[:, 0:n], self.NU[:, 0:n], self.NA[:, 0:n], self.NG[:, 0:n], y.ap[:, 0:n]
        t = d([waits, (d.key, d.n)], lambda e: e.tensor_scalar(v, src, eps, None, ALU.add))
        read = t
        t = d([t], lambda e: e.tensor_scalar(u, v.bitcast(I32), 1, None, ALU.logical_shift_right))
        t = d([t, y.w], lambda e: e.tensor_scalar(yy.bitcast(I32), u, -1.0, float(0x5F3759DF), ALU.mult, ALU.add))
        for _ in range(3):
            t = d([t], lambda e: e.tensor_tensor(a, yy, yy, ALU.mult))
            t = d([t], lambda e: e.scalar_tensor_tensor(g, a, -0.5, v, ALU.mult, ALU.mult))
            t = d([t], lambda e: e.scalar_tensor_tensor(yy, g, 1.5, yy, ALU.add, ALU.mult))
        return y, t, read

    def spread(self, y, cols, tok, ring=None, tiles=4):
        b = (ring or self.banks).get()
        for i in range(tiles):
            c = cols[i]
            t = self.mm([tok, b.w], b.ap[:, i * P:(i + 1) * P], y[:, c:c + 1].to_broadcast([P, P]),
                        self.ident, sig=(i == tiles - 1))
        return b, t

    def ada(self):
        if not self.fill:
            return
        l, c = self.fill.pop(0)
        ch = self.take("w_ada", l * 36 + c, raw=True)
        w = ch[1].rearrange("p (k n) -> p k n", k=8)
        if self.ada_acc is None:
            self.ada_acc = self.tmp.get()
        acc, q = self.ada_acc, self.tmp.get()
        a0, a1 = acc.ap[:, (c % 2) * 256:(c % 2) * 256 + 256], q.ap[:, 0:256]
        t = [None, None]
        for k in range(8):
            dst, cond = (a0, a1)[k % 2], self.COND[:, k:k + 1]
            if k < 2:
                t[k] = self.dve([ch[2], self.cond_t, acc.w, q.w], lambda e: e.tensor_scalar(
                    dst, w[:, k, :], cond, None, ALU.mult))
            else:
                t[k % 2] = self.dve([t[k % 2]], lambda e: e.scalar_tensor_tensor(
                    dst, w[:, k, :], cond, dst, ALU.mult, ALU.add))
        self.release_raw(ch, t[1])
        ts = self.dve(t, lambda e: e.tensor_tensor(a0, a0, a1, ALU.add))
        q.done(ts)
        if c % 2 == 0:
            return
        b = self.banks.get()
        for j in range(4):
            tok = self.mm([ts, b.w], b.ap[:, j:j + 1], acc.ap[:, j * P:(j + 1) * P], self.one, sig=(j == 3))
        acc.done(tok)
        self.ada_acc = None
        at = l * 72 + 2 * c - 2
        dst, bias = self.MOD[:, at:at + 4], self.vec("b_ada", at, 4)
        tm = self.dve([tok, self.vec_t], lambda e: e.tensor_tensor(dst, b.ap[:, 0:4], bias, ALU.add))
        b.done(tm)
        self.mod_t[l, c - 1] = self.mod_t[l, c] = tm

    def vec(self, name, i=0, n=1):
        at = VEC[name][0] + i
        return self.VEC[:, at:at + n]

    def mod(self, l, which):
        return (self.MOD[:, l * 72 + which * 8:l * 72 + which * 8 + 8],
                [self.mod_t[l, which * 4 + c] for c in range(4)])

    def modulate_first(self):
        sc, tsc = self.mod(0, 1)
        sh, tsh = self.mod(0, 0)
        s = self.small.get()
        t = self.dve([tsc, tsh, s.w], lambda e: e.tensor_scalar(s.ap[:, 0:8], sc, 1.0, None, ALU.add))
        ht = []
        for n in range(NT):
            ht.append(self.to_h(n, s.ap[:, n:n + 1], sh[:, n:n + 1], [t, tsh, self.x_t[n]]))
            x = self.XR[:, n, :]
            self.x_t[n] = self.dve([ht[n]], lambda e: e.tensor_scalar(x, x, ALPHA, None, ALU.mult))
        s.done(*flat(ht))
        self.ht = ht

    def to_h(self, n, a, b, waits):
        x, hi, lo = self.XR[:, n, :], self.HH[:, n, :], self.HL[:, n, :]
        h = self.tmp.get()
        t1 = self.dve([waits, self.hfree], lambda e: e.tensor_scalar(hi, x, a, b, ALU.mult, ALU.add))
        t2 = self.act([waits, h.w], lambda e: e.activation(h.ap, x, ACT.Identity, bias=b, scale=a))
        q = self.pool
        t3 = q([t1, t2, self.hfree], lambda e: e.tensor_tensor(lo, h.ap, hi.bitcast(F32), ALU.subtract))
        h.done(t3)
        return [t1, t2, t3]

    def gate(self, l, which, w):
        g, tg = self.mod(l, which)
        s = self.small.get()
        t = self.dve([tg, s.w], lambda e: e.tensor_scalar(s.ap[:, 0:8], g, w, w, ALU.mult, ALU.add))
        return s, t

    def update_gated(self, n, b, tok, s, ts):
        x, c = self.XR[:, n, :], s.ap[:, n:n + 1]
        t = self.dve([tok, ts, self.x_t[n]], lambda e: e.scalar_tensor_tensor(x, b.ap, c, x, ALU.mult, ALU.add))
        b.done(t)
        self.x_t[n] = t

    def update_plain(self, n, b, tok):
        x = self.XR[:, n, :]
        t = self.dve([tok, self.x_t[n]], lambda e: e.tensor_tensor(x, b.ap, x, ALU.add))
        b.done(t)
        self.x_t[n] = t

    def layer_norm(self, l, idx, mean, nxt):
        gain, beta = self.vec("ln_gain", l * 24 + idx * 8, 8), self.vec("ln_bias", l * 24 + idx * 8, 8)
        s = self.small.get()
        A, B, AG, AB = (s.ap[:, 8 * i:8 * i + 8] for i in range(4))
        if nxt is not None:
            sc, tsc = self.mod(nxt[0], nxt[2])
            sh, tsh = self.mod(nxt[0], nxt[1])
            t = self.dve([tsc, s.w, self.vec_t], lambda e: e.tensor_scalar(AG, sc, 1.0, None, ALU.add))
            ta = self.dve([t], lambda e: e.tensor_tensor(A, gain, AG, ALU.mult))
            tb = self.dve([t], lambda e: e.tensor_tensor(AB, beta, AG, ALU.mult))
            tb = self.dve([tb, tsh], lambda e: e.tensor_tensor(B, AB, sh, ALU.add))
            t1 = self.dve([ta, tb], lambda e: e.tensor_scalar(AG, gain, ALPHA, None, ALU.mult))
            t2 = self.dve([tb], lambda e: e.tensor_scalar(AB, beta, ALPHA, None, ALU.mult))
            small = [ta, tb, t1, t2]
        mb, tm = mean
        y = self.yr.get()
        t = self.dve([tm, y.w], lambda e: e.tensor_copy(y.ap[:, 0:4], mb.ap[:, 0:4]))
        mb.done(t)
        b, tb_ = self.spread(y.ap, range(4), t)
        y.done(tb_)
        var = self.held.get()
        rd = []
        for n in range(NT):
            x = self.XR[:, n, :]
            td = self.dve([tb_, tm, self.x_t[n]], lambda e: e.tensor_tensor(x, x, b.ap, ALU.subtract))
            q = self.tmp.get()
            ts = self.act([td, q.w], lambda e: e.activation(q.ap, x, ACT.Square))
            tv = self.stat(var, 0, 1, q.ap, ts, self.col1024, n == 0, n == NT - 1)
            q.done(tv)
            rd.append([td, ts])
        b.done(td)
        y, t, read = self.rsqrt(var.ap[:, 0:4], 4, 1e-5, [tv])
        var.done(read)
        b, tb_ = self.spread(y.ap, range(4), t)
        y.done(tb_)
        self.ht = []
        last = []
        for n in range(NT):
            x = self.XR[:, n, :]
            t = self.dve([tb_, rd[n]], lambda e: e.tensor_tensor(x, x, b.ap, ALU.mult))
            if nxt is not None:
                self.ht.append(self.to_h(n, A[:, n:n + 1], B[:, n:n + 1], [t, small]))
            else:
                g, c = gain[:, n:n + 1], beta[:, n:n + 1]
                self.x_t[n] = self.act([t], lambda e: e.activation(x, x, ACT.Identity, bias=c, scale=g))
            last.append(self.x_t[n])
        b.done(t)
        if nxt is not None:
            for n in range(NT):
                x, g, c = self.XR[:, n, :], AG[:, n:n + 1], AB[:, n:n + 1]
                self.x_t[n] = self.act([self.ht[n], small], lambda e: e.activation(x, x, ACT.Identity, bias=c, scale=g))
                last.append(self.x_t[n])
        s.done(*last)

    def square_of(self, stats, tiles):
        tv = None
        for n in tiles:
            x, q = self.XR[:, n, :], self.tmp.get()
            ts = self.act([self.x_t[n], q.w], lambda e: e.activation(q.ap, x, ACT.Square))
            tv = self.stat(stats, 0, 1, q.ap, ts, self.col1024, n == 0, n == NT - 1)
            q.done(tv)
        return tv

    def rms_norm(self, name, l, stats=None, meanwhile=None):
        st, tv = stats or (self.held.get(), None)
        if tv is None:
            tv = self.square_of(st, range(NT))
        y, t, read = self.rsqrt(st.ap[:, 0:4], 4, 1e-6, [tv])
        st.done(read)
        if meanwhile:
            meanwhile[0]()
        b, tb = self.spread(y.ap, range(4), t)
        y.done(tb)
        self.ht = []
        for n in range(NT):
            x, g, q = self.XR[:, n, :], self.vec(name, l * 8 + n), self.tmp.get()
            t = self.dve([tb, q.w, self.x_t[n], self.vec_t], lambda e: e.scalar_tensor_tensor(q.ap, x, g, b.ap, ALU.mult, ALU.mult))
            self.ht.append(self.parts(self.HH[:, n, :], self.HL[:, n, :], q.ap, [t],
                                      self.dve if n % 2 else self.pool, self.hfree))
            q.done(*self.ht[n])
        b.done(t)
        if meanwhile:
            meanwhile[1]()

    def ffn(self, kind, names, l, groups, update, mean):
        H = (self.HH, self.HL)
        self.barrier()
        base = self.base
        stats, tm = None, None
        with ExitStack() as ctx:
            A = [(self.alloc(ctx, "ah", [P, 8, S], F32R), self.alloc(ctx, "al", [P, 8, S], F32R)) for _ in range(2)]
            afree = [base, base]
            up_n = names["n_up"]
            for gi, (g0, G) in enumerate(groups):
                AH, AL = A[gi % 2]
                at = []
                for m in range(G // 2):
                    idx = l * up_n + g0 // 2 + m
                    if kind == "swiglu":
                        ch = self.take(names["gate"], idx)
                        sl = []
                        for b, tok in self.feat2(ch, 8, H, self.ht, gi == 0 and m == 0):
                            q = self.tmp.get()
                            ts = self.act([tok, q.w], lambda e, q=q, b=b: e.activation(q.ap, b.ap, ACT.Silu))
                            b.done(ts)
                            sl.append((q, ts))
                        self.release(ch, tok)
                        self.ada()
                        ch = self.take(names["up"], idx)
                        for t in range(2):
                            b, tok = self.feat(ch, 8, 256, t, H, self.ht)
                            q, ts = sl[t]
                            ta = self.dve([tok, ts], lambda e, q=q, b=b: e.tensor_tensor(q.ap, q.ap, b.ap, ALU.mult))
                            b.done(ta)
                            k = 2 * m + t
                            at.append(self.parts(AH[:, k, :], AL[:, k, :], q.ap, [ta], free=afree[gi % 2]))
                            q.done(*at[k])
                        self.release(ch, tok)
                        self.ada()
                    else:
                        ch = self.take(names["up"], idx)
                        for t, (b, tok) in enumerate(self.feat2(ch, 8, H, self.ht, gi == 0 and m == 0)):
                            q = self.tmp.get()
                            ts = self.act([tok, q.w], lambda e, q=q, b=b: e.activation(q.ap, b.ap, ACT.Relu))
                            b.done(ts)
                            ta = self.dve([ts], lambda e, q=q: e.tensor_tensor(q.ap, q.ap, q.ap, ALU.mult))
                            k = 2 * m + t
                            at.append(self.parts(AH[:, k, :], AL[:, k, :], q.ap, [ta], free=afree[gi % 2]))
                            q.done(*at[k])
                        self.release(ch, tok)
                if gi == len(groups) - 1:
                    self.hfree = [tok]
                final = gi == len(groups) - 1 and mean
                if final:
                    stats = self.held.get()
                done = []
                for c in range(4):
                    ch = self.take(names["down"][gi], l * 4 + c)
                    for t in range(2):
                        b, tok = self.feat(ch, G, 256, t, (AH, AL), at)
                        update(2 * c + t, b, tok)
                        done.append(2 * c + t)
                    self.release(ch, tok)
                    afree[gi % 2] = [tok]
                    if final:
                        f = self.mean_of if mean == "ln" else self.square_of
                        tm = f(stats, done[:-2] if c < 3 else done) or tm
                        done = done[-2:] if c < 3 else []
                    self.ada()
        self.barrier()
        return stats, tm

    def mean_of(self, stats, tiles):
        tm = None
        for n in tiles:
            tm = self.stat(stats, 0, 1, self.XR[:, n, :], self.x_t[n], self.col1024, n == 0, n == NT - 1)
        return tm

    def project_out(self, name, idx0, kt, nc_, Y, yt, update, mean):
        stats = self.held.get() if mean else None
        tm, done = None, []
        per = nc_ // P
        for c in range(NT // per):
            ch = self.take(name, idx0 + c)
            for t in range(per):
                b, tok = self.feat(ch, kt, nc_, t, Y, yt)
                update(per * c + t, b, tok)
                done.append(per * c + t)
            self.release(ch, tok)
            if mean:
                last = c == NT // per - 1
                f = self.mean_of if mean == "ln" else self.square_of
                tm = f(stats, done if last else done[:-2]) or tm
                done = done[-2:]
        self.hfree = [tok]
        return stats, tm

    def copy_out(self, dst, b, tok, waits=(), scale=None, q=None, src=None):
        src = b.ap if src is None else src
        q = q or self.act
        if q is self.act:
            if scale is None:
                t = q([tok, list(waits)], lambda e: e.activation(dst, src, ACT.Copy))
            else:
                t = q([tok, list(waits)], lambda e: e.activation(dst, src, ACT.Copy, scale=scale))
        else:
            t = q([tok, list(waits)], lambda e: e.tensor_copy(dst, src))
        return t

    def rope(self, x, tok, perm, cos, sin, ctok=()):
        b = self.banks.get()
        tp = self.mm([tok, b.w, list(ctok)], b.ap, perm, x, sig=True)
        q = self.tmp.get()
        t1 = self.dve([tp, q.w, list(ctok)], lambda e: e.tensor_tensor(q.ap, b.ap, sin, ALU.mult))
        b.done(t1)
        t2 = self.pool([tok, tp, list(ctok)], lambda e: e.tensor_tensor(x, x, cos, ALU.mult))
        t3 = self.dve([t1, t2], lambda e: e.tensor_tensor(x, x, q.ap, ALU.add))
        q.done(t3)
        return t3

    def tick(self):
        if self.bg and len(self.active) < self.depth:
            self.active.append(self.bg.pop(0))
        keep = []
        for u in self.active:
            if next(u, "end") != "end":
                keep.append(u)
        self.active = keep

    def pipeline(self, units=()):
        self.bg.extend(units)
        while self.bg or self.active:
            self.tick()

    def softmax_rows(self, src, n, bias, tok, extra=(), mask_from=None):
        q, sm = self.tmp.get(), self.small.get()
        e_, mx, nm, sm_, rc = q.ap[:, 0:n], sm.ap[:, 0:1], sm.ap[:, 1:2], sm.ap[:, 2:3], sm.ap[:, 3:4]
        if bias is not None:
            t = self.dve([tok, q.w, sm.w, list(extra)], lambda e: e.tensor_tensor_reduce(
                e_, src.ap[:, 0:n], bias, 1.0, -3e38, ALU.add, ALU.max, mx))
            src.done(t)
            t = self.dve([t], lambda e: e.tensor_scalar(nm, mx, -1.0, None, ALU.mult))
            t = self.act([t], lambda e: e.activation(e_, e_, ACT.Exp, bias=nm, accum_out=sm_))
        else:
            t = self.dve([tok, sm.w], lambda e: e.tensor_reduce(mx, src.ap[:, 0:n], AXX, ALU.max))
            t = self.dve([t], lambda e: e.tensor_scalar(nm, mx, -1.0, None, ALU.mult))
            t = self.act([t, q.w], lambda e: e.activation(e_, src.ap[:, 0:n], ACT.Exp, bias=nm, accum_out=sm_))
            src.done(t)
        return q, sm, t

    def attend(self, Q, K, V, lo, i, n, bias, extra, out, osl, first, last, finish):
        b = self.banks.get()
        tok = self.mm([extra, b.w], b.ap[:, 0:n], Q, K, sig=True)
        q, sm, t = self.softmax_rows(b, n, bias, tok, extra)
        yield
        e_, rc = q.ap[:, 0:n], sm.ap[:, 3:4]
        t = self.dve([t], lambda e: e.reciprocal(rc, sm.ap[:, 2:3]))
        t = self.dve([t], lambda e: e.tensor_scalar(e_, e_, rc, None, ALU.mult))
        sm.done(t)
        yield
        b = self.banks.get()
        for j in range(n // P):
            tt = self.pe([t, b.w], lambda e, j=j: e.transpose(b.ap[:, j * P:(j + 1) * P], e_[:, j * P:(j + 1) * P], self.ident),
                         sig=(j == n // P - 1))
        q.done(tt)
        p = self.tmp.get()
        t = self.act([tt, p.w], lambda e: e.activation(p.ap[:, 0:n], b.ap[:, 0:n], ACT.Copy))
        b.done(t)
        yield
        o = out()
        for j in range(n // P):
            to = self.mm([t, o.w, extra], osl(o), V(j), p.ap[:, j * P:(j + 1) * P], j == 0, j == n // P - 1,
                         sig=(j == n // P - 1))
        p.done(to)
        if last:
            finish(o, to)


def consts():
    f = np.float32
    i = np.arange(P)
    cc = {}
    cc["ident"] = np.eye(P, dtype=f)
    cc["one"] = np.ones((P, 1), f)
    cc["later"] = (i[:, None] > i[None, :]).astype(f)

    def perm(half, width):
        m = np.zeros((P, P), f)
        for a in range(0, P, 64):
            for r in range(half):
                m[a + half + r, a + r] = -1.0
                m[a + r, a + half + r] = 1.0
        return m

    cc["perm1"] = perm(32, 64)
    cc["perm2"] = perm(8, 16)
    w = np.arange(S)
    diff = i[:, None] + 384 - w[None, :]
    cc["causal"] = np.where(diff >= 0, 0.0, NEG).astype(f)
    cc["strict"] = (i[:, None] < i[None, :]).astype(f)
    blk = np.zeros((P, 2), f)
    blk[0:64, 0] = blk[64:, 1] = 1.0 / 64
    cc["blk"] = blk
    cc["col1024"] = np.full((P, 1), 1.0 / 1024, f)
    cc["col256"] = np.full((P, 1), 1.0 / 256, f)
    cc["col128"] = np.full((P, 1), 1.0 / 128, f)
    inv = (np.float64(500000.0) ** (-np.arange(0, 16, 2, dtype=np.float64) / 16)).astype(f)
    col = np.zeros((P, 1), f)
    for a in (0, 64):
        col[a:a + 8, 0] = inv
        col[a + 8:a + 16, 0] = inv
    cc["inv"] = col
    c1 = {}
    t = np.arange(S, dtype=f)
    for name, freq in (("ret", 1.0 / (10000.0 ** np.linspace(0.0, 1.0, 32))),
                       ("dil", 1.0 / (10000.0 ** (np.arange(0, 64, 2) / 64)))):
        ang = (t[None, :] * freq.astype(f)[:, None]).astype(f).astype(np.float64)
        c1[name + "_cos"] = np.tile(np.cos(ang), (4, 1)).astype(f)
        c1[name + "_sin"] = np.tile(np.sin(ang), (4, 1)).astype(f)
    for h in range(4):
        lg = np.log1p(-(2.0 ** (-5.0 - h)))
        d = w[None, :] - i[:, None]
        c1[f"decay{h}"] = (np.where(d >= 0, np.exp(lg * np.maximum(d, 0)), 0.0) * 0.125).astype(f)
    cnt = (diff >= 0).astype(np.int64) * ((diff <= 128).astype(np.int64) + (diff % 4 == 0) + (diff % 16 == 0))
    c1["dil_mask"] = np.where(cnt > 0, np.log(np.maximum(cnt, 1)), NEG).astype(f)
    sel = np.zeros((P, 13 * P), f)
    for v in range(13 * P):
        sel[v // 64, v] = 1.0
    ct = np.zeros((P, 64), f)
    for g, wd in enumerate((2, 4, 8, 16)):
        ct[:, g * 16:(g + 1) * 16] = 1.0 / np.minimum(np.arange(16) + 1, wd)
    c2 = {"sel": sel, "count": ct}
    out = []
    for d in (cc, c1, c2):
        at, where = 0, {}
        for k, v in d.items():
            where[k] = (at, v.shape[1])
            at += v.shape[1]
        out.append((np.ascontiguousarray(np.concatenate(list(d.values()), 1)), where))
    return out


def first_mixer(p, l):
    H = (p.HH, p.HL)
    p.barrier()
    base = p.base
    with ExitStack() as ctx:
        RQ, RK = p.alloc(ctx, "rq", [P, 2, S]), p.alloc(ctx, "rk", [P, 2, S])
        RV, RG = p.alloc(ctx, "rv", [P, 4, S]), p.alloc(ctx, "rg", [P, 4, S])
        DQ, DK, DV = p.alloc(ctx, "dq", [P, 2, S]), p.alloc(ctx, "dk", [P, 2, S]), p.alloc(ctx, "dv", [P, 4, 256])
        SQ, SK, SV = p.alloc(ctx, "sq", [P, 2, S]), p.alloc(ctx, "sk", [P, 2, S]), p.alloc(ctx, "sv", [P, 4, 256])
        NK = p.alloc(ctx, "nk", [P, 2, 1280])
        extra = p.more_tmp(ctx, 3)
        yt = [None] * 8
        kept = {}
        tk = {}

        def fproj(idx, dst, key, scale=None, eager=False, after=None):
            ch = p.take("w_in", l * 12 + idx)
            r = []
            for t, (b, tok) in enumerate(p.feat2(ch, 8, H, p.ht, eager)):
                r.append(p.copy_out(dst[:, t, :], b, tok, base, scale))
                b.done(r[-1])
            p.release(ch, tok)
            tk[key] = r
            p.ada()

        def tproj(idx, dst, c0, key):
            ch = p.take("w_in", l * 12 + idx)
            for i in (0, 2):
                b, tok = p.toks(ch, 8, 256, [i, i + 1], H, p.ht)
                tk.setdefault(key, []).append(p.copy_out(dst[:, i:i + 2, c0:c0 + 256], b, tok, base,
                                                         src=b.ap.rearrange("p (a n) -> p a n", a=2)))
                b.done(tk[key][-1])
            p.release(ch, tok)
            p.ada()
            return tok

        def roped(X, key, kind):
            tk[key] = [p.rope(X[:, t, :], tk[key][t], p.perm1, p.c1(kind + "_cos"), p.c1(kind + "_sin"), [p.c1_t])
                       for t in range(2)]

        def keep(n, o, to, dst, waits=()):
            t = p.copy_out(dst, o, to, waits)
            o.done(t)
            kept[n] = (dst, t)

        offs = [0, 512, 896, 1152]
        nk_t = {}
        nkfree = [[], []]
        sb_last = []

        def sb_unit(h, j, cell):
            r = slice(64 * (h % 2), 64 * (h % 2) + 64)
            n = S - j * P
            nk = NK[:, h % 2, offs[j]:offs[j] + n]
            b = p.banks.get()
            tok = p.mm([tk["sq"], tk["sk"], b.w], b.ap[:, 0:n], SK[r, h // 2, j * P:(j + 1) * P], SQ[r, h // 2, j * P:S], sig=True)
            z = b.ap[:, 0:n]
            q = p.tmp.get()
            a = q.ap[:, 0:n]
            t = p.dve([tok, q.w], lambda e: e.tensor_scalar(a, z, 0.0, -2.0, ALU.max, ALU.mult))
            t = p.dve([t], lambda e: e.tensor_tensor(a, z, a, ALU.add))
            t = p.act([t], lambda e: e.activation(a, a, ACT.Exp))
            t = p.act([t], lambda e: e.activation(a, a, ACT.Ln, bias=1.0))
            yield
            t1 = p.dve([t, base, nkfree[h % 2]], lambda e: e.scalar_tensor_tensor(nk, z, 0.0, a, ALU.max, ALU.add))
            t2 = p.dve([t1], lambda e: e.tensor_tensor(a, z, nk, ALU.subtract))
            b.done(t2)
            nk_t[h, j] = p.dve([t2], lambda e: e.tensor_tensor(nk[:, 0:P], nk[:, 0:P], p.strict, ALU.mult))
            yield
            b = p.banks.get()
            bt = p.mm([nk_t[h, j], b.w], b.ap[:, 0:n], p.later, nk, True, j == 3, sig=(j == 3))
            for jj in range(j + 1, 4):
                m = S - jj * P
                bt = p.mm([nk_t[h, jj]], b.ap[:, n - m:n], p.one.to_broadcast([P, P]), NK[:, h % 2, offs[jj]:offs[jj] + m],
                          False, jj == 3, sig=(jj == 3))
            if j == 0:
                nkfree[h % 2] = [bt]
            t = p.dve([bt, t2], lambda e: e.tensor_tensor(a, a, b.ap[:, 0:n], ALU.subtract))
            b.done(t)
            t = p.act([t], lambda e: e.activation(a, a, ACT.Exp))
            yield
            t = p.dve([t], lambda e: e.tensor_tensor(a[:, 0:P], a[:, 0:P], p.strict, ALU.mult))
            if not cell:
                cell.append(p.held.get())
            o = cell[0]
            to = p.mm([t, o.w, tk["sv"]], o.ap[r, j * P:S], SV[:, j, 64 * h:64 * h + 64], a, j == 3, j == 0, sig=True)
            q.done(to)
            if j == 0 and h % 2 == 1:
                keep(6 + h // 2, o, to, SQ[:, h // 2, :])
                sb_last.append(to)

        def sb_units():
            for h in range(4):
                if h % 2 == 0:
                    cell = []
                for j in (3, 2, 1, 0):
                    yield sb_unit(h, j, cell)

        NKF = NK[:, :, :].rearrange("p a n -> p (a n)")
        oh = {}

        def ret_unit(h, j, cell):
            r = slice(64 * (h % 2), 64 * (h % 2) + 64)
            n = S - j * P
            b = p.banks.get()
            tok = p.mm([tk["rq"], tk["rk"], b.w], b.ap[:, 0:n], RK[r, h // 2, j * P:(j + 1) * P], RQ[r, h // 2, j * P:S], sig=True)
            q = p.tmp.get()
            t = p.dve([tok, q.w], lambda e: e.tensor_tensor(q.ap[:, 0:n], b.ap[:, 0:n], p.c1(f"decay{h}")[:, 0:n], ALU.mult))
            b.done(t)
            yield
            if j == 0:
                cell.append(p.held.get())
            o = cell[0]
            to = p.mm([t, o.w, tk["rv"]], o.ap[:, j * P:S], RV[:, j, h * P:(h + 1) * P], q.ap[:, 0:n], j == 0, j == 3, sig=True)
            q.done(to)
            if j == 3:
                dst = NKF[:, h * S:(h + 1) * S]
                t = p.copy_out(dst, o, to, sb_last)
                o.done(t)
                oh[h] = (dst, t)

        def ret_norm():
            yield
            yield
            st = p.held.get()
            for h in range(4):
                dst, t = oh[h]
                tm = p.stat(st, h, 4, dst, t, p.col128, True, True)
            yield
            y = p.yr.get()
            t = p.dve([tm, y.w], lambda e: e.tensor_copy(y.ap[:, 0:16], st.ap[:, 0:16]))
            st.done(t)
            st = p.held.get()
            prev = None
            for h in range(5):
                if h < 4:
                    dst, to = oh[h]
                    b, tb = p.spread(y.ap, [4 * i + h for i in range(4)], t)
                    td = p.dve([tb, to], lambda e: e.tensor_tensor(dst, dst, b.ap, ALU.subtract))
                    b.done(td)
                    q = p.tmp.get()
                    ts = p.act([td, q.w], lambda e: e.activation(q.ap, dst, ACT.Square))
                    oh[h] = (dst, [td, ts])
                if prev is not None:
                    q0, ts0 = prev
                    tv = p.stat(st, h - 1, 4, q0.ap, ts0, p.col128, True, True)
                    q0.done(tv)
                prev = (q, ts)
                yield
            y.done(tb)
            y, t, read = p.rsqrt(st.ap[:, 0:16], 16, 1e-6, [tv])
            st.done(read)
            yield
            for h in range(4):
                dst, to = oh[h]
                b, tb = p.spread(y.ap, [4 * i + h for i in range(4)], t)
                g = RG[:, h, :]
                tg = p.pool([tk["rg"][h], to], lambda e: e.tensor_tensor(g, dst, g, ALU.mult))
                td = p.dve([tb, tg], lambda e: e.tensor_tensor(g, g, b.ap, ALU.mult))
                b.done(td)
                kept[h] = (g, td)
                yield
            y.done(tb)

        def ret_units():
            for h in range(4):
                cell = []
                for j in range(4):
                    yield ret_unit(h, j, cell)
            yield ret_norm()

        def dil_units():
            for pr in range(2):
                cell = []

                def out(cell=cell):
                    if not cell:
                        cell.append(p.held.get())
                    return cell[0]

                for i in range(4):
                    for c in range(2):
                        n = (i + 1) * P
                        r = slice(64 * c, 64 * c + 64)
                        yield p.attend(
                            DQ[r, pr, i * P:(i + 1) * P], DK[r, pr, 0:n],
                            lambda j, pr=pr, c=c: DV[:, j, 64 * (2 * pr + c):64 * (2 * pr + c) + 64],
                            0, i, n, p.c1("dil_mask")[:, 384 - i * P:S], [tk["dq"], tk["dk"], tk["dv"], p.c1_t], out,
                            lambda o, r=r, i=i: o.ap[r, i * P:(i + 1) * P], i == 0, i == 3 and c == 1,
                            lambda o, to, pr=pr: keep(4 + pr, o, to, DQ[:, pr, :]))

        fproj(9, SQ, "sq", 0.125, eager=True)
        fproj(10, SK, "sk")
        tproj(11, SV, 0, "sv")
        p.bg.extend(sb_units())
        fproj(0, RQ, "rq")
        fproj(1, RK, "rk")
        roped(RQ, "rq", "ret")
        roped(RK, "rk", "ret")
        tproj(2, RV, 0, "rv")
        tproj(3, RV, 256, "rv")
        p.bg.extend(ret_units())
        tk["rg"] = []
        for c in range(2):
            ch = p.take("w_in", l * 12 + 4 + c)
            for t, (b, tok) in enumerate(p.feat2(ch, 8, H, p.ht)):
                dst = RG[:, 2 * c + t, :]
                tk["rg"].append(p.act([tok, base], lambda e: e.activation(dst, b.ap, ACT.Silu)))
                b.done(tk["rg"][-1])
            p.release(ch, tok)
            p.ada()
        fproj(6, DQ, "dq", 0.125)
        fproj(7, DK, "dk")
        roped(DQ, "dq", "dil")
        roped(DK, "dk", "dil")
        last = tproj(8, DV, 0, "dv")
        p.hfree = [last]
        p.pipeline(dil_units())
        for i, n in enumerate((6, 7, 0, 1, 2, 3, 4, 5)):
            src, t = kept[n]
            yt[n] = p.parts(p.HH[:, n, :], p.HL[:, n, :], src, [t], (p.pool, p.dve)[i % 2], p.hfree)
        s, ts = p.gate(l, 5, 1.0)
        r = p.project_out("w_out", l * 4, 8, 256, H, yt, lambda n, b, tok: p.update_gated(n, b, tok, s, ts), "ln")
        s.done(p.x_t[7])
        p.less_tmp(extra)
    p.barrier()
    return r


def head_norms(p, st, ncols, tok, seln):
    y, t, read = p.rsqrt(st.ap[:, 0:4 * ncols], 4 * ncols, 1e-6, [tok])
    st.done(read)
    b = p.banks.get()
    for i in range(4):
        tt = p.pe([t, b.w], lambda e, i=i: e.transpose(b.ap[0:seln, i * P:(i + 1) * P],
                                                       y.ap[:, i * ncols:i * ncols + seln], p.ident), sig=(i == 3))
    return y, t, b, tt


def even_mixer(p):
    H = (p.HH, p.HL)
    p.barrier()
    base = p.base
    with ExitStack() as ctx:
        QA, KA, VA = (p.alloc(ctx, n, [P, 4, S]) for n in ("qa", "ka", "va"))
        QB, KB, VB = (p.alloc(ctx, n, [P, 4, S]) for n in ("qb", "kb", "vb"))
        QI, KI = p.alloc(ctx, "qi", [P, 2, S]), p.alloc(ctx, "ki", [P, S])
        BM = p.alloc(ctx, "bm", [P, 1152])
        RT = p.alloc(ctx, "rt", [32, S])
        WI = p.alloc(ctx, "wi", [P, 4, 4])
        CK = BM[:, 0:1024].rearrange("p (a n) -> p a n", a=2)
        NC = 27
        st = p.held.get()
        raw = {}

        def fproj(idx, dst, key, col, stat=True, waits=()):
            ch = p.take("w_in_e", idx)
            for t in range(2):
                b, tok = p.feat(ch, 8, 256, t, H, p.ht)
                d = dst[t]
                tc_ = p.copy_out(d, b, tok, base)
                last = tc_
                if stat:
                    q = p.tmp.get()
                    ts = p.act([tok, q.w], lambda e, q=q, b=b: e.activation(q.ap, b.ap, ACT.Square))
                    last = ts
                    if stat == "ckv":
                        sts.append((q, ts))
                    else:
                        pend.append((q, ts, col + 2 * t))
                b.done(last)
                raw[key, t] = tc_
            p.release(ch, tok)
            return tok

        pend, sts = [], []
        last_stat = [None]

        def flush():
            while pend:
                q, ts, col = pend.pop(0)
                tv = p.stat(st, col, NC, q.ap, ts, p.blk, True, True, n=2)
                q.done(tv)
                last_stat[0] = tv

        for i, (X, key, c0) in enumerate(((QA, "qa", 0), (KA, "ka", 8), (QB, "qb", 16))):
            for c in range(2):
                fproj(2 * i + c, [X[:, 2 * c, :], X[:, 2 * c + 1, :]], (key, c), c0 + 4 * c)
                if c:
                    flush()
        fproj(6, [CK[:, 0, :], CK[:, 1, :]], ("ckv", 0), 26, "ckv")
        flush()
        for i in range(4):
            for k in range(2):
                tv = p.mm([sts[k][1], st.w], st.ap[:, i * NC + 26:i * NC + 27], sts[k][0].ap[:, i * P:(i + 1) * P],
                          p.col256, k == 0, k == 1, sig=(i == 3 and k == 1))
        for k in range(2):
            sts[k][0].done(tv)
        fproj(7, [QI[:, 0, :], QI[:, 1, :]], ("qi", 0), 0, False)
        ch = p.take("w_kiwi", 0)
        b, tok = p.feat(ch, 8, 132, 0, H, p.ht)
        t_ki = p.copy_out(KI[:, :], b, tok, base)
        q = p.tmp.get()
        ts = p.act([tok, q.w], lambda e, q=q, b=b: e.activation(q.ap, b.ap, ACT.Square))
        b.done(ts)
        pend.append((q, ts, 24))
        b, tok = p.toks(ch, 8, 132, [0, 1, 2, 3], H, p.ht, cols=(128, 4))
        t_wi = p.dve([tok, base], lambda e, b=b: e.tensor_scalar(
            WI[:, :, :], b.ap[:, 0:16].rearrange("p (a n) -> p a n", a=4), 1.0 / 16, None, ALU.mult))
        b.done(t_wi)
        p.release(ch, tok)
        flush()
        y, ty, b, tt = head_norms(p, st, NC, [last_stat[0], tv], 26)
        t_rt = p.dve([tt, base], lambda e, b=b: e.tensor_copy(RT[0:26, :], b.ap[0:26, :]))
        b.done(t_rt)
        va = []
        hlast = None
        for c in range(2):
            ch = p.take("w_in_e", 8 + c)
            for i in (0, 2):
                b, tok = p.toks(ch, 8, 256, [i, i + 1], H, p.ht)
                va.append(p.copy_out(VA[:, i:i + 2, 256 * c:256 * c + 256], b, tok, base,
                                     src=b.ap.rearrange("p (a n) -> p a n", a=2)))
                b.done(va[-1])
            p.release(ch, tok)
        p.hfree = [tok]
        b, tb = p.spread(y.ap, [NC * i + 26 for i in range(4)], ty)
        y.done(tb, tt)
        ct = []
        for k in range(2):
            q = p.tmp.get()
            g = p.vec("g_kv_b", k)
            t = p.dve([tb, q.w, raw[("ckv", 0), k]], lambda e, q=q, g=g, k=k, b=b: e.scalar_tensor_tensor(
                q.ap, CK[:, k, :], g, b.ap, ALU.mult, ALU.mult))
            ck_read = t
            ct.append(p.parts(p.HH[:, k, :], p.HL[:, k, :], q.ap, [t], p.dve, p.hfree))
            q.done(*ct[k])
        b.done(t)

        def normed(X, rowtile, g, tok, rt_t, rt=RT, rows=26):
            b = p.banks.get()
            tb = p.mm([rt_t, b.w, p.c2_t], b.ap, p.c2("sel")[0:rows, rowtile * P:(rowtile + 1) * P], rt[0:rows, :], sig=True)
            t = p.dve([tb, tok], lambda e: e.scalar_tensor_tensor(X, X, g, b.ap, ALU.mult, ALU.mult))
            b.done(t)
            return p.rope(X, t, p.perm2, p.COS2, p.SIN2, [p.rope_t]), tb

        small = p.small.get()
        g8 = small.ap[:, 0:2]
        tg = p.dve([small.w, p.vec_t], lambda e: e.tensor_scalar(small.ap[:, 0:1], p.vec("gq_a"), 0.125, None, ALU.mult))
        tg = p.dve([tg], lambda e: e.tensor_scalar(small.ap[:, 1:2], p.vec("gq_b"), 0.125, None, ALU.mult))
        qa = [normed(QA[:, n, :], n, small.ap[:, 0:1], [raw[("qa", n // 2), n % 2], tg], t_rt)[0] for n in range(4)]
        ka = [normed(KA[:, n, :], 4 + n, p.vec("gk_a"), raw[("ka", n // 2), n % 2], t_rt)[0] for n in range(4)]
        ch = p.take("w_kv_up", 0)
        stb = p.held.get()
        for n in range(4):
            b, tok = p.feat(ch, 2, 1024, n, H, ct)
            raw["kb", n] = p.copy_out(KB[:, n, :], b, tok, base)
            q = p.tmp.get()
            ts = p.act([tok, q.w], lambda e, q=q, b=b: e.activation(q.ap, b.ap, ACT.Square))
            b.done(ts)
            tvb = p.stat(stb, 2 * n, 8, q.ap, ts, p.blk, True, True, n=2)
            q.done(tvb)
        vb = []
        for i in range(4):
            b, tok = p.toks(ch, 2, 1024, [i], H, ct, cols=(512, 512))
            vb.append(p.copy_out(VB[:, i, :], b, tok, base))
            b.done(vb[-1])
        p.release(ch, tok)
        p.hfree = [tok]
        ki, tlast = normed(KI[:, :], 12, p.vec("g_kidx"), t_ki, t_rt)
        qi = [p.rope(QI[:, t, :], raw[("qi", 0), t], p.perm2, p.COS2, p.SIN2, [p.rope_t]) for t in range(2)]

        bm_at = [None, 0, 256, 640]
        bm_t = [None] * 4
        qb = [None] * 4

        def index(i):
            n = (i + 1) * P
            w = p.tmp.get()
            tw = None
            for h in range(4):
                r = slice(64 * (h % 2), 64 * (h % 2) + 64)
                b = p.banks.get()
                tok = p.mm([qi, ki, b.w], b.ap[:, 0:n], QI[r, h // 2, i * P:(i + 1) * P], KI[r, 0:n], sig=True)
                q = p.tmp.get()
                t = p.act([tok, q.w], lambda e, q=q, b=b: e.activation(q.ap[:, 0:n], b.ap[:, 0:n], ACT.Relu))
                b.done(t)
                s = WI[:, i, h:h + 1]
                if h == 0:
                    tw = p.dve([t, w.w, t_wi], lambda e, q=q, s=s: e.tensor_scalar(w.ap[:, 0:n], q.ap[:, 0:n], s, None, ALU.mult))
                else:
                    tw = p.dve([t, tw], lambda e, q=q, s=s: e.scalar_tensor_tensor(
                        w.ap[:, 0:n], q.ap[:, 0:n], s, w.ap[:, 0:n], ALU.mult, ALU.add))
                q.done(tw)
            tw = p.dve([tw], lambda e: e.tensor_tensor(w.ap[:, 0:n], w.ap[:, 0:n], p.causal[:, 384 - i * P:S], ALU.add))
            yield
            s = p.small.get()
            for r in range(16):
                tm = p.dve([tw, s.w], lambda e: e.max(s.ap[:, 0:8], w.ap[:, 0:n]))
                tw = p.dve([tm], lambda e: e.match_replace(w.ap[:, 0:n], s.ap[:, 0:8], w.ap[:, 0:n], TAKEN))
                if r % 4 == 3:
                    yield
            s.done(tw)
            bm = BM[:, bm_at[i]:bm_at[i] + n]
            bm_t[i] = p.dve([tw, ck_read], lambda e: e.tensor_scalar(bm, w.ap[:, 0:n], -2e38, NEG, ALU.is_gt, ALU.mult))
            w.done(bm_t[i])

        lam = p.LAM[:, 0:1]
        o_raw = {}

        def a_unit(h, i, cell):
            n = (i + 1) * P
            sub = []
            for c in range(2):
                r = slice(64 * c, 64 * c + 64)
                b = p.banks.get()
                tok = p.mm([qa[h], ka[h], b.w], b.ap[:, 0:n], QA[r, h, i * P:(i + 1) * P], KA[r, h, 0:n], sig=True)
                sub.append(p.softmax_rows(b, n, p.causal[:, 384 - i * P:S], tok))
            yield
            (q0, s0, t0), (q1, s1, t1) = sub
            e0, e1 = q0.ap[:, 0:n], q1.ap[:, 0:n]
            t0 = p.dve([t0], lambda e: e.reciprocal(s0.ap[:, 3:4], s0.ap[:, 2:3]))
            t1 = p.dve([t1], lambda e: e.reciprocal(s1.ap[:, 3:4], s1.ap[:, 2:3]))
            t0 = p.dve([t0], lambda e: e.tensor_scalar(e0, e0, s0.ap[:, 3:4], None, ALU.mult))
            t1 = p.dve([t1, p.lam_t], lambda e: e.tensor_tensor(s1.ap[:, 4:5], s1.ap[:, 3:4], lam, ALU.mult))
            t = p.dve([t0, t1], lambda e: e.scalar_tensor_tensor(e0, e1, s1.ap[:, 4:5], e0, ALU.mult, ALU.add))
            q1.done(t)
            s0.done(t)
            s1.done(t)
            yield
            b = p.banks.get()
            for j in range(i + 1):
                tt = p.pe([t, b.w], lambda e, j=j: e.transpose(b.ap[:, j * P:(j + 1) * P], e0[:, j * P:(j + 1) * P], p.ident),
                          sig=(j == i))
            q0.done(tt)
            pt = p.tmp.get()
            t = p.act([tt, pt.w], lambda e: e.activation(pt.ap[:, 0:n], b.ap[:, 0:n], ACT.Copy))
            b.done(t)
            yield
            if not cell:
                cell.append(p.held.get())
            o = cell[0]
            for j in range(i + 1):
                to = p.mm([t, o.w, va], o.ap[:, i * P:(i + 1) * P], VA[:, j, h * P:(h + 1) * P], pt.ap[:, j * P:(j + 1) * P],
                          j == 0, j == i, sig=(j == i))
            pt.done(to)
            if i == 3:
                dst = QA[:, h, :]
                t = p.copy_out(dst, o, to)
                o.done(t)
                o_raw[h] = (dst, t)

        qb = [normed(QB[:, n, :], 8 + n, small.ap[:, 1:2], [raw[("qb", n // 2), n % 2], tg], t_rt)[0] for n in range(4)]
        small.done(qb[3])
        y, ty, b, tt = head_norms(p, stb, 8, [tvb], 8)
        t_rt2 = p.dve([tt, (p.pe.key, p.pe.n)], lambda e, b=b: e.tensor_copy(RT[0:8, :], b.ap[0:8, :]))
        b.done(t_rt2)
        y.done(tt)
        kb = [normed(KB[:, n, :], n, p.vec("gk_b"), raw["kb", n], t_rt2, rows=8)[0] for n in range(4)]

        def spaced(g, k):
            for _ in g:
                for _ in range(k):
                    yield

        def units():
            for h in range(4):
                cell = []
                if h < 3:
                    yield spaced(index(h + 1), 1)
                for i in range(4):
                    yield a_unit(h, i, cell)

        p.pipeline(units())
        yt = [None] * 8
        st = p.held.get()
        for h in range(4):
            dst, t = o_raw[h]
            q = p.tmp.get()
            ts = p.act([t, q.w], lambda e, dst=dst, q=q: e.activation(q.ap, dst, ACT.Square))
            tv = p.stat(st, h, 4, q.ap, ts, p.col128, True, True)
            q.done(tv)
        y, t, read = p.rsqrt(st.ap[:, 0:16], 16, 1e-6, [tv])
        st.done(read)
        sg = p.small.get()
        tg = p.dve([sg.w], lambda e: e.tensor_scalar(sg.ap[:, 0:1], p.vec("g_sub_a"), 0.8, None, ALU.mult))
        for h in range(4):
            dst, to = o_raw[h]
            b, tb = p.spread(y.ap, [4 * i + h for i in range(4)], t)
            td = p.dve([tb, to, tg, tv], lambda e, dst=dst, b=b: e.scalar_tensor_tensor(dst, dst, sg.ap[:, 0:1], b.ap, ALU.mult, ALU.mult))
            b.done(td)
            yt[h] = p.parts(p.HH[:, h, :], p.HL[:, h, :], dst, [td], p.pool, p.hfree)
        y.done(tb)
        sg.done(td)

        def emit(n, o, to):
            yt[n] = p.parts(p.HH[:, n, :], p.HL[:, n, :], o.ap, [to], p.dve, p.hfree)
            o.done(*yt[n])

        def b_units():
            for pr in range(4):
                cell = []

                def out(cell=cell):
                    if not cell:
                        cell.append(p.held.get())
                    return cell[0]

                for i in range(4):
                    for c in range(2):
                        n = (i + 1) * P
                        r = slice(64 * c, 64 * c + 64)
                        bias = p.causal[:, 384:S] if i == 0 else BM[:, bm_at[i]:bm_at[i] + n]
                        yield p.attend(
                            QB[r, pr, i * P:(i + 1) * P], KB[r, pr, 0:n],
                            lambda j, pr=pr, c=c: VB[:, j, 64 * (2 * pr + c):64 * (2 * pr + c) + 64],
                            0, i, n, bias, [qb[pr], kb[pr], vb, bm_t[i]], out,
                            lambda o, r=r, i=i: o.ap[r, i * P:(i + 1) * P], i == 0, i == 3 and c == 1,
                            lambda o, to, pr=pr: emit(4 + pr, o, to))

        p.pipeline(b_units())
        p.project_out("w_out_e", 0, 8, 256, H, yt, p.update_plain, False)
    p.barrier()


def odd_mixer(p):
    H = (p.HH, p.HL)
    p.barrier()
    base = p.base
    with ExitStack() as ctx:
        GB, GC = p.alloc(ctx, "gb", [P, 4, S]), p.alloc(ctx, "gc", [P, 4, S])
        U = p.alloc(ctx, "u", [P, 4, S + 2])
        Z = p.alloc(ctx, "z", [P, 4, S + 16])
        SA, SB = p.alloc(ctx, "sa", [P, S + 16]), p.alloc(ctx, "sbb", [P, S + 16])
        tz = p.pool([base], lambda e: e.memset(U[:, :, 0:2], 0.0))
        tz2 = p.pool([base], lambda e: e.memset(Z[:, :, 0:16], 0.0))
        tz3 = p.pool([base], lambda e: e.memset(SA[:, 0:16], 0.0))
        tz4 = p.pool([base], lambda e: e.memset(SB[:, 0:16], 0.0))
        zt = [tz, tz2, tz3, tz4]
        gb, gc, u, zd = [], [], [], []
        for i in range(8):
            ch = p.take("w_in_o", i)
            for t in range(2):
                n = 2 * (i % 2) + t
                b, tok = p.feat(ch, 8, 256, t, H, p.ht)
                if i < 2:
                    gb.append(p.copy_out(GB[:, n, :], b, tok, base))
                    b.done(gb[-1])
                elif i < 4:
                    gc.append(p.copy_out(GC[:, n, :], b, tok, base))
                    b.done(gc[-1])
                elif i < 6:
                    u.append(p.dve([tok, gc[n], zt], lambda e, n=n, b=b: e.tensor_tensor(U[:, n, 2:S + 2], GC[:, n, :], b.ap, ALU.mult)))
                    b.done(u[-1])
                else:
                    zd.append(p.copy_out(Z[:, n, 16:S + 16], b, tok, [zt]))
                    b.done(zd[-1])
            p.release(ch, tok)
        p.hfree = [tok]
        yt = [None] * 8
        for n in range(4):
            acc = GC[:, n, :]
            w = [p.vec("conv_w", 4 * k + n) for k in range(3)]
            t = p.dve([u[n]], lambda e, n=n, w=w, acc=acc: e.tensor_scalar(acc, U[:, n, 0:S], w[0], None, ALU.mult))
            for k in (1, 2):
                t = p.dve([t], lambda e, n=n, w=w, acc=acc, k=k: e.scalar_tensor_tensor(acc, U[:, n, k:k + S], w[k], acc, ALU.mult, ALU.add))
            t = p.dve([t, gb[n]], lambda e, n=n, acc=acc: e.tensor_tensor(acc, acc, GB[:, n, :], ALU.mult))
            yt[n] = p.parts(p.HH[:, n, :], p.HL[:, n, :], acc, [t], p.pool, p.hfree)
        ch = p.take("w_pool", 0)
        pv = []
        prev = list(zt)
        for g, wd in enumerate((2, 4, 8, 16)):
            src, t, k = Z[:, g, :], zd[g], 1
            bufs = [SA[:, :], SB[:, :]]
            while k < wd:
                dst = bufs[0]
                t = p.dve([t, prev], lambda e, dst=dst, src=src, k=k: e.tensor_tensor(
                    dst[:, 16:S + 16], src[:, 16:S + 16], src[:, 16 - k:S + 16 - k], ALU.add))
                src, bufs, k = dst, bufs[::-1], 2 * k
            q = p.tmp.get()
            t1 = p.dve([t, q.w], lambda e, q=q, src=src, wd=wd: e.tensor_scalar(q.ap, src[:, 16:S + 16], 1.0 / wd, None, ALU.mult))
            t1 = p.dve([t1, p.c2_t], lambda e, q=q, src=src, g=g: e.tensor_tensor(
                q.ap[:, 0:16], src[:, 16:32], p.c2("count")[:, g * 16:(g + 1) * 16], ALU.mult))
            prev = [t1]
            t1 = p.dve([t1], lambda e, q=q, g=g: e.tensor_tensor(q.ap, q.ap, Z[:, g, 16:S + 16], ALU.subtract))
            hi, lo = p.HH[:, 4 + g, :], p.HL[:, 4 + g, :]
            pt = p.parts(hi, lo, q.ap, [t1], p.dve, p.hfree)
            q.done(*pt)
            _, wh, wl, toks, _ = ch
            b = p.banks.get()
            tok = p.mm3([toks, pt, b.w], b.ap, wh[:, g * P:(g + 1) * P], wl[:, g * P:(g + 1) * P], hi, lo, True, True, sig=True)
            q = p.tmp.get()
            t = p.act([tok, q.w], lambda e, q=q, b=b, g=g: e.activation(q.ap, b.ap, ACT.Identity, scale=p.vec("pool_scale", g)))
            b.done(t)
            yt[4 + g] = p.parts(hi, lo, q.ap, [t], p.dve)
            q.done(*yt[4 + g])
        p.release(ch, tok)
        p.project_out("w_out_o", 0, 8, 256, H, yt, p.update_plain, False)
    p.barrier()


def cross(p, l):
    H = (p.HH, p.HL)
    p.barrier()
    base = p.base
    M = 256
    with ExitStack() as ctx:
        MT = p.alloc(ctx, "mt", [P, 8, M])
        MH, ML = p.alloc(ctx, "mh", [P, 8, M], F32R), p.alloc(ctx, "ml", [P, 8, M], F32R)
        QX, KX, VX = p.alloc(ctx, "qx", [P, 4, S]), p.alloc(ctx, "kx", [P, 4, M]), p.alloc(ctx, "vx", [P, 2, S])
        tl = p.load("mem", MT[:, :, :], p.dram["memT"], base)
        st = p.held.get()
        for k in range(8):
            q = p.tmp.get()
            ts = p.act([tl, q.w], lambda e, q=q, k=k: e.activation(q.ap[:, 0:M], MT[:, k, :], ACT.Square))
            tv = p.stat(st, 0, 1, q.ap, ts, p.col1024, k == 0, k == 7, tiles=2)
            q.done(tv)
        y, t, read = p.rsqrt(st.ap[:, 0:2], 2, 1e-6, [tv])
        st.done(read)
        b, tb = p.spread(y.ap, range(2), t, tiles=2)
        y.done(tb)
        mt = []
        for k in range(8):
            g = p.vec("g_mem", l * 8 + k)
            q = p.tmp.get()
            t = p.dve([tb, tl, q.w], lambda e, k=k, g=g, q=q, b=b: e.scalar_tensor_tensor(
                q.ap[:, 0:M], MT[:, k, :], g, b.ap[:, 0:M], ALU.mult, ALU.mult))
            mt.append(p.parts(MH[:, k, :], ML[:, k, :], q.ap[:, 0:M], [t], p.pool if k % 2 else p.dve, base))
            q.done(*mt[k])
        b.done(t)
        stk = p.held.get()
        kr = []
        for c in range(2):
            ch = p.take("wkv_x", l * 4 + c)
            for t in range(2):
                n = 2 * c + t
                b, tok = p.feat(ch, 8, 256, t, (MH, ML), mt, N=M)
                kr.append(p.copy_out(KX[:, n, :], b, tok, base, src=b.ap[:, 0:M]))
                q = p.tmp.get()
                ts = p.act([tok, q.w], lambda e, q=q, b=b: e.activation(q.ap[:, 0:M], b.ap[:, 0:M], ACT.Square))
                b.done(ts)
                tvk = p.stat(stk, n, 4, q.ap, ts, p.col128, True, True, tiles=2)
                q.done(tvk)
            p.release(ch, tok)
        vx = []
        for c in range(2):
            ch = p.take("wkv_x", l * 4 + 2 + c)
            b, tok = p.toks(ch, 8, 256, [0, 1], (MH, ML), mt)
            vx.append(p.copy_out(VX[:, :, 256 * c:256 * c + 256], b, tok, base, src=b.ap.rearrange("p (a n) -> p a n", a=2)))
            b.done(vx[-1])
            p.release(ch, tok)
        y, t, read = p.rsqrt(stk.ap[:, 0:8], 8, 1e-6, [tvk])
        stk.done(read)
        kx = []
        for n in range(4):
            b, tb = p.spread(y.ap, [n, 4 + n], t, tiles=2)
            kx.append(p.dve([tb, kr[n]], lambda e, n=n, b=b: e.scalar_tensor_tensor(
                KX[:, n, :], KX[:, n, :], p.vec("gk_x", l), b.ap[:, 0:M], ALU.mult, ALU.mult)))
            b.done(kx[-1])
        y.done(tb)
        p.rms_norm("g_xattn", l)
        stq = p.held.get()
        qr = []
        pend = []
        for c in range(2):
            ch = p.take("wq_x", l * 2 + c)
            for t in range(2):
                n = 2 * c + t
                b, tok = p.feat(ch, 8, 256, t, H, p.ht)
                qr.append(p.copy_out(QX[:, n, :], b, tok, base))
                q = p.tmp.get()
                ts = p.act([tok, q.w], lambda e, q=q, b=b: e.activation(q.ap, b.ap, ACT.Square))
                b.done(ts)
                pend.append((n, q, ts))
            p.release(ch, tok)
        p.hfree = [tok]
        for n, q, ts in pend:
            tvq = p.stat(stq, n, 4, q.ap, ts, p.col128, True, True)
            q.done(tvq)
        y, t, read = p.rsqrt(stq.ap[:, 0:16], 16, 1e-6, [tvq])
        stq.done(read)
        sg = p.small.get()
        tg = p.dve([sg.w], lambda e: e.tensor_scalar(sg.ap[:, 0:1], p.vec("gq_x", l), 128.0 ** -0.5, None, ALU.mult))
        qx = []
        for n in range(4):
            b, tb = p.spread(y.ap, [4 * i + n for i in range(4)], t)
            qx.append(p.dve([tb, qr[n], tg], lambda e, n=n, b=b: e.scalar_tensor_tensor(
                QX[:, n, :], QX[:, n, :], sg.ap[:, 0:1], b.ap, ALU.mult, ALU.mult)))
            b.done(qx[-1])
        y.done(tb)
        sg.done(qx[-1])
        yt = [None] * 4

        def emit(n, o, to):
            yt[n] = p.parts(p.HH[:, n, :], p.HL[:, n, :], o.ap, [to], p.dve, p.hfree)
            o.done(*yt[n])

        def units():
            for h in range(4):
                cell = []

                def out(cell=cell):
                    if not cell:
                        cell.append(p.held.get())
                    return cell[0]

                for i in range(4):
                    yield p.attend(QX[:, h, i * P:(i + 1) * P], KX[:, h, :],
                                   lambda j, h=h: VX[:, j, h * P:(h + 1) * P], 0, i, M, None, [qx[h], kx[h], vx], out,
                                   lambda o, i=i: o.ap[:, i * P:(i + 1) * P], i == 0, i == 3,
                                   lambda o, to, h=h: emit(h, o, to))

        p.pipeline(units())
        p.project_out("wo_x", l * 2, 4, 512, H, yt, p.update_plain, False)
    p.barrier()


def rope_tables(p):
    q = [p.tmp.get() for _ in range(3)]
    ang, n, r = (x.ap for x in q)
    w = [x.w for x in q]
    tr = p.load("misc", p.POSI, p.dram["positions"], p.base)
    t = p.dve([tr, w], lambda e: e.tensor_copy(r[0:1, :], p.POSI))
    b = p.banks.get()
    tb = p.mm([t, b.w, p.cc_t], b.ap, p.one[0:1, :].to_broadcast([1, P]), r[0:1, :], sig=True)
    ta = p.dve([tb], lambda e: e.tensor_scalar(ang, b.ap, p.inv, None, ALU.mult))
    b.done(ta)
    toks = []
    t = ta
    for dst, shift in ((p.SIN2, 0.0), (p.COS2, 0.25)):
        t = p.dve([t], lambda e: e.tensor_scalar(n, ang, 1.0 / TWO_PI, shift, ALU.mult, ALU.add))
        t = p.dve([t], lambda e: e.tensor_scalar(n, n, MAGIC, None, ALU.add))
        t = p.dve([t], lambda e: e.tensor_scalar(n, n, -MAGIC, None, ALU.add))
        t = p.dve([t] + toks, lambda e: e.scalar_tensor_tensor(r, n, -C1, ang, ALU.mult, ALU.add))
        t = p.dve([t], lambda e: e.scalar_tensor_tensor(r, n, -C2, r, ALU.mult, ALU.add))
        t = p.dve([t], lambda e: e.scalar_tensor_tensor(r, n, -C3, r, ALU.mult, ALU.add))
        t = p.dve([t], lambda e, shift=shift: e.tensor_scalar(r, r, shift * TWO_PI, PI_LOW, ALU.add, ALU.min))
        t = p.dve([t], lambda e: e.tensor_scalar(r, r, -PI_LOW, None, ALU.max))
        ts = p.act([t, p.base], lambda e, dst=dst: e.activation(dst, r, ACT.Sin))
        toks.append(ts)
    for x in q:
        x.done(*toks)
    p.rope_t = toks
    s = p.small.get()
    lv = p.vec("lam", 0, 4)
    t = p.dve([s.w], lambda e: e.tensor_tensor(s.ap[0:64, 0:2], lv[0:64, 0:2], lv[0:64, 2:4], ALU.mult))
    b = p.banks.get()
    tb = p.mm([t, b.w], b.ap[:, 0:2], p.one[0:64, :].to_broadcast([64, P]), s.ap[0:64, 0:2], sig=True)
    t = p.act([tb], lambda e: e.activation(s.ap[:, 2:4], b.ap[:, 0:2], ACT.Exp))
    b.done(t)
    t = p.dve([t], lambda e: e.tensor_tensor(s.ap[:, 4:5], s.ap[:, 3:4], s.ap[:, 2:3], ALU.subtract))
    p.lam_t = p.dve([t], lambda e: e.tensor_scalar(p.LAM[:, 0:1], s.ap[:, 4:5], -(0.8 - 0.6), None, ALU.add))
    s.done(p.lam_t)


def whole(p):
    p.cc_t = p.load("cc", p.CC[:, :], p.dram["cc"])
    p.vec_t = p.load("vec", p.VEC[:, :], p.dram["vecs"])
    p.cond_t = p.act([p.vec_t], lambda e: e.activation(p.COND[:, :], p.vec("c", 0, 8), ACT.Silu))
    p.mod_t = {}
    p.fill = [(0, c) for c in range(8)]
    for _ in range(8):
        p.ada()
        if len(p.fill) == 6:
            tx = p.load("x", p.XR[:, :, :], p.dram["xT"])
            p.c1_t = p.load("c1", p.C[:, :], p.dram["c1"])
    p.pe([p.cc_t], lambda e: e.nop(), sig=False)
    p.dve([p.cc_t, p.c1_t, p.vec_t], lambda e: e.nop(), sig=False)
    p.x_t = [tx] * NT
    p.fill = [(0, c) for c in range(8, 36)] + [(1, c) for c in range(36)]
    p.modulate_first()
    ffn1 = {"gate": "ffn1_w_gate", "up": "ffn1_w_up", "down": ["ffn1_down0", "ffn1_down1", "ffn1_down2"], "n_up": 11}
    ffn2 = {"gate": "ffn2_w_gate", "up": "ffn2_w_up", "down": ["ffn2_down0", "ffn2_down1", "ffn2_down2"], "n_up": 11}
    for l in range(2):
        gt = {}

        def gated(which):
            def update(n, b, tok):
                if which not in gt:
                    gt[which] = p.gate(l, which, 0.5)
                p.update_gated(n, b, tok, *gt[which])
            return update

        mean = p.ffn("swiglu", ffn1, l, FFN_GROUPS, gated(2), "ln")
        gt[2][0].done(p.x_t[7])
        p.layer_norm(l, 0, mean, (l, 3, 4))
        mean = first_mixer(p, l)
        p.layer_norm(l, 1, mean, (l, 6, 7))
        mean = p.ffn("swiglu", ffn2, l, FFN_GROUPS, gated(8), "ln")
        gt[8][0].done(p.x_t[7])
        p.layer_norm(l, 2, mean, (1, 0, 1) if l == 0 else None)
    assert not p.fill
    p.barrier()
    p.c2_t = p.load("c2", p.C[:, 1024:1024 + p.c2n], p.dram["c2"], p.base)
    rope_tables(p)
    mlp = {"up": "w_up", "down": ["down_m0", "down_m1", "down_m2", "down_m3"], "n_up": 16}
    for l in range(2):
        p.rms_norm("g_mix", l)
        if l == 0:
            even_mixer(p)
        else:
            odd_mixer(p)
        cross(p, l)
        p.rms_norm("g_mlp", l)
        p.ffn("relu2", mlp, l, MLP_GROUPS, p.update_plain, False)
    for n in range(NT):
        p.load("out", p.out[:, n, :], p.XR[:, n, :], [p.x_t[n]])
    p.sp([("out", 16 * NT)], lambda e: e.nop(), sig=False)


def build(nc, dram, out, tables):
    ctx = ExitStack()
    with ctx:
        def sb(name, shape, dt=F32):
            return ctx.enter_context(nc.sbuf_tensor("s_" + name, shape, dt))

        (cc, ccw), (c1, c1w), (c2, c2w) = tables
        mem = {"NS": 3, "NW": 2}
        mem["psum"] = [ctx.enter_context(nc.psum_tensor(f"ps{i}", [P, S], F32)) for i in range(8)]
        mem["XR"] = sb("xr", [P, NT, S])
        mem["HH"], mem["HL"] = sb("hh", [P, NT, S], F32R), sb("hl", [P, NT, S], F32R)
        mem["STAGE"] = sb("stage", [P, 3, 2048])
        mem["WH"], mem["WL"] = sb("wh", [P, 2, 2048], F32R), sb("wl", [P, 2, 2048], F32R)
        mem["TMP"] = sb("tmp", [P, 6, S])
        mem["CC"] = CC = sb("cc", [P, cc.shape[1]])
        mem["C"] = C = sb("c", [P, c1.shape[1]])
        mem["VEC"] = sb("vec", [P, NVEC])
        mem["MOD"] = sb("mod", [P, 144])
        mem["COND"] = sb("cond", [P, 8])
        mem["SM"] = sb("sm", [P, 8, 32])
        mem["NY"] = sb("ny", [P, 2, 112])
        mem["NV"], mem["NA"] = sb("nv", [P, 112]), sb("na", [P, 112])
        mem["NU"] = sb("nu", [P, 112], I32)
        mem["NG"] = mem["NU"][:, :].bitcast(F32)
        mem["LAM"] = sb("lam", [P, 1])
        for k, (at, n) in ccw.items():
            mem[k] = CC[:, at:at + n]
        mem["c1"] = lambda k: C[:, c1w[k][0]:c1w[k][0] + c1w[k][1]]
        mem["COS2"], mem["SIN2"] = C[:, 0:512], C[:, 512:1024]
        mem["c2"] = lambda k: C[:, 1024 + c2w[k][0]:1024 + c2w[k][0] + c2w[k][1]]
        mem["POSI"] = C[0:1, 4096:4608].bitcast(I32)
        mem["c2n"] = c2.shape[1]
        mem["sems"] = {k: ctx.enter_context(nc.semaphore("q_" + k)) for k in SEMS}
        dry = Prog(nc, dram, out, None, mem, "a")
        whole(dry)
        p = Prog(nc, dram, out, dry.order, mem, "b")
        whole(p)
        assert p.taken == len(p.plan)


def _tiles(w, nc_):
    k, n = w.shape
    a = w.reshape(k // P, P, n // nc_, nc_).transpose(2, 1, 0, 3)
    return a.reshape(n // nc_, P, (k // P) * nc_)


def _cols(v):
    return v.reshape(-1, P).T


def kernel(**inputs):
    import concourse.bacc as _bacc
    from concourse import mybir as _mybir
    from concourse.bass_utils import run_bass_kernel_spmd as _run

    a = {k: np.asarray(v) for k, v in inputs.items()}
    arr = {}

    def put(name, parts):
        arr[name] = np.ascontiguousarray(np.concatenate(parts, 0))

    put("w_ada", [_tiles(a["w_ada"][l], 256) for l in range(2)])
    for f in ("ffn1", "ffn2"):
        for g in ("gate", "up"):
            put(f"{f}_w_{g}", [_tiles(a[f"{f}_w_{g}"][l], 256) for l in range(2)])
        for gi, (g0, G) in enumerate(FFN_GROUPS):
            put(f"{f}_down{gi}", [_tiles(a[f"{f}_w_down"][l][g0 * P:(g0 + G) * P], 256) for l in range(2)])
    put("w_in", [_tiles(a["w_in"][l], 256) for l in range(2)])
    put("w_out", [_tiles(a["w_out"][l], 256) for l in range(2)])
    e = a["w_in_e_2"][0]
    order = [e[:, 0:1024], e[:, 1536:2048], e[:, 2048:2560], e[:, 1024:1536]]
    put("w_in_e", [_tiles(w, 256) for w in order])
    ki, wi = e[:, 2560:2624], e[:, 2624:2628]
    put("w_kiwi", [_tiles(np.concatenate([ki, ki, wi], 1), 132)])
    put("w_kv_up", [_tiles(a["w_kv_up_b_2"][0], 1024)])
    put("w_out_e", [_tiles(a["w_out_e_2"][0], 256)])
    put("w_in_o", [_tiles(a["w_in_o_2"][0], 256)])
    put("w_pool", [a["w_pool_2"][0].transpose(1, 0, 2).reshape(1, P, 512)])
    put("w_out_o", [_tiles(a["w_out_o_2"][0], 256)])
    put("wq_x", [_tiles(a["wq_x_2"][l], 256) for l in range(2)])
    put("wkv_x", [_tiles(a["wkv_x_2"][l], 256) for l in range(2)])
    put("wo_x", [_tiles(a["wo_x_2"][l], 512) for l in range(2)])
    put("w_up", [_tiles(a["w_up_2"][l], 256) for l in range(2)])
    for gi, (g0, G) in enumerate(MLP_GROUPS):
        put(f"down_m{gi}", [_tiles(a["w_down_2"][l][g0 * P:(g0 + G) * P], 256) for l in range(2)])
    arr["xT"] = np.ascontiguousarray(a["x"][0].T.reshape(NT, P, S).transpose(1, 0, 2))
    arr["memT"] = np.ascontiguousarray(a["mem_2"][0].T.reshape(8, P, 256).transpose(1, 0, 2))
    arr["positions"] = np.ascontiguousarray(a["positions_2"])
    two = lambda v: np.concatenate([v, v])[:, None]
    lam = np.zeros((P, 4), np.float32)
    for i, n in enumerate(("lam_q1_2", "lam_q2_2", "lam_k1_2", "lam_k2_2")):
        lam[0:64, i] = a[n][0]
    arr["vecs"] = np.ascontiguousarray(np.concatenate([
        _cols(a["c"][0]), _cols(a["b_ada"].reshape(-1)), _cols(a["ln_gain"].reshape(-1)),
        _cols(a["ln_bias"].reshape(-1)), _cols(a["g_mix_2"].reshape(-1)), _cols(a["g_xattn_2"].reshape(-1)),
        _cols(a["g_mem_2"].reshape(-1)), _cols(a["g_mlp_2"].reshape(-1)), _cols(a["gq_x_2"].reshape(-1)),
        _cols(a["gk_x_2"].reshape(-1)), two(a["gq_a_2"][0]), two(a["gk_a_2"][0]), two(a["gq_b_2"][0]),
        two(a["gk_b_2"][0]), two(a["g_kidx_2"][0]), _cols(a["g_sub_a_2"].reshape(-1)),
        _cols(a["g_kv_b_2"].reshape(-1)), _cols(a["conv_w_2"].reshape(-1)),
        _cols(a["pool_scale_2"].reshape(-1)), lam], 1))
    tables = consts()
    arr["cc"], arr["c1"], arr["c2"] = (t[0] for t in tables)

    nc = _bacc.Bacc("TRN2", target_bir_lowering=False, num_devices=1)
    dram = {}
    for name, v in arr.items():
        dram[name] = nc.dram_tensor(f"in_{name}", v.shape, _mybir.dt.from_np(v.dtype), kind="ExternalInput").ap()
    out = nc.dram_tensor("out_0", (P, NT, S), F32, kind="ExternalOutput").ap()
    build(nc, dram, out, tables)
    r = _run(nc, [{f"in_{k}": v for k, v in arr.items()}], core_ids=[0])
    got = r.results[0]["out_0"]
    return np.ascontiguousarray(got.transpose(1, 0, 2).reshape(D, S).T).reshape(1, S, D)
```

```python
from contextlib import ExitStack

import numpy as np

import concourse.bass as bass
from concourse import mybir

F32 = mybir.dt.float32
F32R = mybir.dt.float32r
I32 = mybir.dt.int32
ALU = mybir.AluOpType
ACT = mybir.ActivationFunctionType
AXX = mybir.AxisListType.X

P = 128
S = 512
D = 1024
NT = D // P
ALPHA = 4.0 ** 0.25
NEG = -1e30
TAKEN = -3e38
MAGIC = 12582912.0
TWO_PI = 6.283185307179586
C1 = 6.28125
C2 = float(np.float32(TWO_PI - C1))
C3 = float(np.float32(TWO_PI - C1 - C2))
PI_LOW = float(np.nextafter(np.float32(np.pi), np.float32(0)))
FFN_GROUPS = [(0, 8), (8, 8), (16, 6)]
MLP_GROUPS = [(0, 8), (8, 8), (16, 8), (24, 8)]

VEC = {}


def _vec_layout():
    at = 0
    for name, n in (("c", 8), ("b_ada", 144), ("ln_gain", 48), ("ln_bias", 48), ("g_mix", 16),
                    ("g_xattn", 16), ("g_mem", 16), ("g_mlp", 16), ("gq_x", 2), ("gk_x", 2),
                    ("gq_a", 1), ("gk_a", 1), ("gq_b", 1), ("gk_b", 1), ("g_kidx", 1),
                    ("g_sub_a", 1), ("g_kv_b", 2), ("conv_w", 12), ("pool_scale", 4),
                    ("lam", 4)):
        VEC[name] = (at, n)
        at += n
    return at


NVEC = _vec_layout()
SEMS = ["pe", "act", "dve", "pool", "st0", "st1", "st2", "cc", "vec", "x", "c1", "c2", "a0", "a1", "a2", "a3", "a4", "a5", "a6", "a7", "misc", "mem", "out"]


def flat(ws):
    for w in ws:
        if w is None:
            continue
        if isinstance(w, list):
            yield from flat(w)
        else:
            yield w


class Queue:

    def __init__(self, key, eng, sems):
        self.key, self.eng, self.sems = key, eng, sems
        self.n, self.seen = 0, {}

    def __call__(self, waits, fn, sig=True, sem=None):
        need = []
        for k, v in flat(waits):
            if self.seen.get(k, 0) < v:
                self.seen[k] = v
                need = [x for x in need if x[0] != k] + [(k, v)]
        if sig and sem is None:
            self.n += 1
        if self.eng is not None:
            for k, v in need:
                self.eng.wait_ge(self.sems[k], v)
            ins = fn(self.eng)
            if sem is not None:
                ins.then_inc(self.sems[sem], 16)
            elif sig:
                ins.then_inc(self.sems[self.key], 1)
        return (self.key, self.n)


class Slot:

    def __init__(self, ap):
        self.ap, self.w, self.busy = ap, [], False

    def done(self, *tokens):
        self.w = list(tokens)
        self.busy = False


class Ring:
    def __init__(self, aps):
        self.slots, self.i = [Slot(a) for a in aps], 0

    def free(self):
        return sum(not s.busy for s in self.slots)

    def get(self, first=None):
        for _ in self.slots:
            i = self.i % len(self.slots)
            s = self.slots[i]
            self.i += 1
            if not s.busy and i < (first or len(self.slots)):
                break
        assert not s.busy
        s.busy = True
        return s


class Prog:
    def __init__(self, nc, dram, out, plan, mem, tag):
        self.nc, self.dram, self.out, self.plan, self.tag = nc, dram, out, plan, tag
        live = plan is not None
        sems = mem["sems"]
        self.pe = Queue("pe", nc.tensor if live else None, sems)
        self.act = Queue("act", nc.scalar if live else None, sems)
        self.dve = Queue("dve", nc.vector if live else None, sems)
        self.pool = Queue("pool", nc.gpsimd if live else None, sems)
        self.sp = Queue("sp", nc.sync if live else None, sems)
        self.psum = mem["psum"]
        self.XR = mem["XR"]
        self.HH = mem["HH"]
        self.HL = mem["HL"]
        self.STAGE = mem["STAGE"]
        self.WH = mem["WH"]
        self.WL = mem["WL"]
        self.TMP = mem["TMP"]
        self.CC = mem["CC"]
        self.C = mem["C"]
        self.VEC = mem["VEC"]
        self.MOD = mem["MOD"]
        self.COND = mem["COND"]
        self.SM = mem["SM"]
        self.NY = mem["NY"]
        self.NV = mem["NV"]
        self.NA = mem["NA"]
        self.NU = mem["NU"]
        self.NG = mem["NG"]
        self.LAM = mem["LAM"]
        self.POSI = mem["POSI"]
        self.COS2 = mem["COS2"]
        self.SIN2 = mem["SIN2"]
        self.c1 = mem["c1"]
        self.c2 = mem["c2"]
        self.c2n = mem["c2n"]
        self.NS = mem["NS"]
        self.NW = mem["NW"]
        self.ident = mem["ident"]
        self.one = mem["one"]
        self.later = mem["later"]
        self.perm1 = mem["perm1"]
        self.perm2 = mem["perm2"]
        self.causal = mem["causal"]
        self.strict = mem["strict"]
        self.blk = mem["blk"]
        self.col1024 = mem["col1024"]
        self.col256 = mem["col256"]
        self.col128 = mem["col128"]
        self.inv = mem["inv"]
        self.nalloc = 0
        self.order = []
        self.banks = Ring([b[:, :] for b in self.psum[0:6]])
        self.held = Ring([b[:, :] for b in self.psum[6:8]])
        self.tmp = Ring([self.TMP[:, i, :] for i in range(self.TMP.shape[1])])
        self.small = Ring([self.SM[:, i, :] for i in range(self.SM.shape[1])])
        self.newt = Slot(None)
        self.yr = Ring([self.NY[:, i, :] for i in range(2)])
        self.ndma = {}
        self.taken = 0
        self.nload = 0
        self.nsplit = 0
        self.stage_w = {}
        self.landed = {}
        self.split_of = {}
        self.wslot = [[], []]
        self.nw = 0
        self.base = []
        self.fill = []
        self.hfree = []
        self.ada_acc, self.ada_sum = None, None
        self.every, self.since = 0, 0
        self.bg, self.active, self.depth, self.spare = [], [], 5, 0

    def alloc(self, ctx, name, shape, dt=F32):
        self.nalloc += 1
        return ctx.enter_context(self.nc.sbuf_tensor(f"{name}_{self.tag}{self.nalloc}", shape, dt))

    def more_tmp(self, ctx, n):
        t = self.alloc(ctx, "xt", [P, n, S])
        new = [Slot(t[:, i, :]) for i in range(n)]
        for x in new:
            x.w = self.base
        self.tmp.slots.extend(new)
        return new

    def less_tmp(self, new):
        assert not any(x.busy for x in new)
        self.tmp.slots = [x for x in self.tmp.slots if x not in new]

    def barrier(self):
        self.base = [(q.key, q.n) for q in (self.pe, self.act, self.dve, self.pool) if q.n]

    def load(self, key, dst, src, waits=()):
        n = self.ndma.get(key, 0) + 1
        self.ndma[key] = n
        self.sp(list(waits), lambda e: e.dma_start(dst, src), sem=key)
        return (key, 16 * n)

    def issue(self, j):
        if j >= len(self.plan):
            return
        name, idx, raw = self.plan[j]
        src = self.dram[name][idx]
        n = src.shape[-1]
        slot = j % self.NS
        self.landed[j] = self.load(f"st{slot}", self.STAGE[:, slot, 0:n], src,
                                   self.stage_w.get(j - self.NS, []))

    def split(self, j):
        name, idx, raw = self.plan[j]
        n = self.dram[name][idx].shape[-1]
        slot, ws = j % self.NS, self.nw % self.NW
        self.nw += 1
        src, wh, wl = self.STAGE[:, slot, 0:n], self.WH[:, ws, 0:n], self.WL[:, ws, 0:n]
        free = self.wslot[ws]
        th = self.act([self.landed[j], free], lambda e: e.activation(wh, src, ACT.Copy))
        cut = n * 5 // 8
        t1 = self.pool([self.landed[j], th, free], lambda e: e.tensor_tensor(
            wl[:, 0:cut], src[:, 0:cut], wh[:, 0:cut].bitcast(F32), ALU.subtract))
        t2 = self.dve([self.landed[j], th, free], lambda e: e.tensor_tensor(
            wl[:, cut:n], src[:, cut:n], wh[:, cut:n].bitcast(F32), ALU.subtract))
        self.stage_w[j] = [t1, t2]
        self.split_of[j] = (wh, wl, [th, t1, t2], ws)
        self.issue(j + self.NS)

    def take(self, name, idx, raw=False):
        j = self.taken
        self.taken += 1
        self.order.append((name, idx, raw))
        if self.plan is None:
            a = self.WH[:, 0, :]
            if raw:
                return j, self.STAGE[:, 0, :], [], 0
            self.ada_step()
            return j, a, a, [], 0
        assert self.plan[j] == (name, idx, raw)
        if raw:
            return j, self.STAGE[:, j % self.NS, :], self.landed[j], 0
        done = 0
        for i in range(max(j, self.nsplit), len(self.plan)):
            if i > j:
                done += 1
            if done > self.NW - 1 or i >= j + self.NS:
                break
            if self.plan[i][2]:
                if i > j:
                    done -= 1
                continue
            if i > j and (i not in self.landed):
                break
            if i >= self.nsplit:
                self.split(i)
                self.nsplit = i + 1
        wh, wl, toks, ws = self.split_of[j]
        self.ada_step()
        return j, wh, wl, toks, ws

    def release(self, ch, token):
        if self.ada_sum:
            self.ada_sum()
            self.ada_sum = None
        if self.plan is not None:
            self.wslot[ch[-1]] = [token]

    def release_raw(self, ch, token):
        if self.plan is not None:
            self.stage_w[ch[0]] = [token]
            self.issue(ch[0] + self.NS)

    def mm(self, waits, out, lhsT, rhs, start=True, stop=True, sig=False):
        return self.pe(waits, lambda e: e.matmul(out, lhsT, rhs, start=start, stop=stop,
                                                 skip_group_check=True), sig=sig)

    def mm3(self, waits, out, ah, al, bh, bl, start, stop, sig=False):
        self.mm(waits, out, ah, bh, start, False)
        self.mm([], out, ah, bl, False, False)
        return self.mm([], out, al, bh, False, stop, sig)

    def feat(self, ch, kt, nc_, t, X, xt, N=S, M=P, off=None):
        _, wh, wl, toks, _ = ch
        whv = wh[:, 0:kt * nc_].rearrange("p (k n) -> p k n", k=kt)
        wlv = wl[:, 0:kt * nc_].rearrange("p (k n) -> p k n", k=kt)
        a = t * P if off is None else off
        b = self.banks.get()
        for k in range(kt):
            tok = self.mm3([toks, xt[k], b.w], b.ap[0:M, 0:N], whv[:, k, a:a + M], wlv[:, k, a:a + M],
                           X[0][:, k, 0:N], X[1][:, k, 0:N], k == 0, k == kt - 1, sig=(k == kt - 1))
            if k % 4 == 3:
                self.tick()
        return b, tok

    def feat2(self, ch, kt, X, xt, eager=False, N=S):
        if not eager:
            for t in range(2):
                yield self.feat(ch, kt, 256, t, X, xt, N)
            return
        _, wh, wl, toks, _ = ch
        whv = wh[:, 0:kt * 256].rearrange("p (k n) -> p k n", k=kt)
        wlv = wl[:, 0:kt * 256].rearrange("p (k n) -> p k n", k=kt)
        bs = [self.banks.get(), self.banks.get()]
        tok = [None, None]
        for k in range(kt):
            for t in range(2):
                tok[t] = self.mm3([toks, xt[k], bs[t].w], bs[t].ap[:, 0:N], whv[:, k, t * P:(t + 1) * P],
                                  wlv[:, k, t * P:(t + 1) * P], X[0][:, k, 0:N], X[1][:, k, 0:N],
                                  k == 0, k == kt - 1, sig=(k == kt - 1))
            if k % 2 == 1:
                self.tick()
        yield bs[0], tok[0]
        yield bs[1], tok[1]

    def toks(self, ch, kt, nc_, tiles, X, xt, cols=None, n=None, view=None):
        _, wh, wl, toks, _ = ch
        whv = wh[:, 0:kt * nc_].rearrange("p (k n) -> p k n", k=kt)
        wlv = wl[:, 0:kt * nc_].rearrange("p (k n) -> p k n", k=kt)
        c0, n = (0, nc_) if cols is None else cols
        b = self.banks.get()
        for q, i in enumerate(tiles):
            for k in range(kt):
                tok = self.mm3([toks, xt[k], b.w], b.ap[:, q * n:(q + 1) * n],
                               X[0][:, k, i * P:(i + 1) * P], X[1][:, k, i * P:(i + 1) * P],
                               whv[:, k, c0:c0 + n], wlv[:, k, c0:c0 + n],
                               k == 0, k == kt - 1, sig=(k == kt - 1 and i == tiles[-1]))
            if n == 256:
                self.tick()
        return b, tok

    def parts(self, hi, lo, src, waits, lo_on=None, free=()):
        th = self.act([waits, list(free)], lambda e: e.activation(hi, src, ACT.Copy))
        q = lo_on or self.pool
        tl = q([waits, th, list(free)], lambda e: e.tensor_tensor(lo, src, hi.bitcast(F32), ALU.subtract))
        return [th, tl]

    def stat(self, b, col, step, src, tok, rhs, start, stop, n=1, tiles=4):
        for i in range(tiles):
            t = self.mm([tok, b.w], b.ap[:, i * step + col:i * step + col + n], src[:, i * P:(i + 1) * P],
                        rhs, start if i == 0 else False, stop, sig=(i == tiles - 1))
        return t

    def rsqrt(self, src, n, eps, waits):
        y = self.yr.get()
        d, v, u, a, g, yy = self.dve, self.NV[:, 0:n], self.NU[:, 0:n], self.NA[:, 0:n], self.NG[:, 0:n], y.ap[:, 0:n]
        t = d([waits, (d.key, d.n)], lambda e: e.tensor_scalar(v, src, eps, None, ALU.add))
        read = t
        t = d([t], lambda e: e.tensor_scalar(u, v.bitcast(I32), 1, None, ALU.logical_shift_right))
        t = d([t, y.w], lambda e: e.tensor_scalar(yy.bitcast(I32), u, -1.0, float(0x5F3759DF), ALU.mult, ALU.add))
        for _ in range(3):
            t = d([t], lambda e: e.tensor_tensor(a, yy, yy, ALU.mult))
            t = d([t], lambda e: e.scalar_tensor_tensor(g, a, -0.5, v, ALU.mult, ALU.mult))
            t = d([t], lambda e: e.scalar_tensor_tensor(yy, g, 1.5, yy, ALU.add, ALU.mult))
        return y, t, read

    def spread(self, y, cols, tok, ring=None, tiles=4):
        b = (ring or self.banks).get()
        for i in range(tiles):
            c = cols[i]
            t = self.mm([tok, b.w], b.ap[:, i * P:(i + 1) * P], y[:, c:c + 1].to_broadcast([P, P]),
                        self.ident, sig=(i == tiles - 1))
        return b, t

    def ada(self):
        if not self.fill:
            return
        l, c = self.fill.pop(0)
        ch = self.take("w_ada", l * 36 + c, raw=True)
        w = ch[1].rearrange("p (k n) -> p k n", k=8)
        if self.ada_acc is None:
            self.ada_acc = self.tmp.get()
        acc = self.ada_acc
        ts, last = self.ada_rows(w, c, acc, ch[2])
        self.release_raw(ch, last)
        if c % 2 == 0:
            return
        self.ada_acc = None
        self.ada_sum = lambda: self.ada_mod(l, c, acc, ts)

    def ada_rows(self, w, c, acc, loaded):
        q = self.tmp.get()
        a0, a1 = acc.ap[:, (c % 2) * 256:(c % 2) * 256 + 256], q.ap[:, 0:256]
        t = [None, None]
        for k in range(8):
            dst, cond = (a0, a1)[k % 2], self.COND[:, k:k + 1]
            if k < 2:
                t[k] = self.dve([loaded, self.cond_t, acc.w, q.w], lambda e: e.tensor_scalar(
                    dst, w[:, k, :], cond, None, ALU.mult))
            else:
                t[k % 2] = self.dve([t[k % 2]], lambda e: e.scalar_tensor_tensor(
                    dst, w[:, k, :], cond, dst, ALU.mult, ALU.add))
        ts = self.dve(t, lambda e: e.tensor_tensor(a0, a0, a1, ALU.add))
        q.done(ts)
        return ts, t[1]

    def ada_step(self):
        self.since += 1
        if self.every and self.since >= self.every:
            self.since = 0
            self.ada()

    def ada_mod(self, l, c, acc, ts):
        b = self.banks.get()
        for j in range(4):
            tok = self.mm([ts, b.w, self.cc_t], b.ap[:, j:j + 1], acc.ap[:, j * P:(j + 1) * P], self.one, sig=(j == 3))
        acc.done(tok)
        self.add_bias(l, c - 1, 2, b, tok)

    def add_bias(self, l, c, n, b, tok):
        at = l * 72 + 2 * c
        dst, bias = self.MOD[:, at:at + 2 * n], self.vec("b_ada", at, 2 * n)
        tm = self.dve([tok, self.vec_t], lambda e: e.tensor_tensor(dst, b.ap[:, 0:2 * n], bias, ALU.add))
        b.done(tm)
        for i in range(n):
            self.mod_t[l, c + i] = tm

    def ada_first(self, n):
        with ExitStack() as ctx:
            W = self.alloc(ctx, "wa", [P, n, 2048])
            tl = {}
            for c in (0, 2, 1, 3, 4, 6, 5, 7):
                tl[c] = self.load(f"a{c}", W[:, c, :], self.dram["w_ada"][c])
                if c == 3:
                    self.cc_t = self.load("cc", self.CC[:, :], self.dram["cc"])
            tx = self.load("x", self.XR[:, :, :], self.dram["xT"])
            self.begin()
            self.c1_t = self.load("c1", self.C[:, :], self.dram["c1"])
            rows = []
            for c in (2, 3, 6, 7):
                if c % 2 == 0:
                    acc = self.tmp.get()
                ts = self.ada_rows(W[:, c, :].rearrange("p (k n) -> p k n", k=8), c, acc, tl[c])[0]
                if c % 2:
                    rows.append((c, acc, ts))
            for c in (0, 1, 4, 5):
                b = self.banks.get()
                for j in range(2):
                    for k in range(8):
                        tok = self.mm([tl[c], self.cond_t, b.w], b.ap[:, j:j + 1],
                                      W[:, c, k * 256 + j * P:k * 256 + j * P + P], self.COND[:, k:k + 1],
                                      k == 0, k == 7, sig=(j == 1 and k == 7))
                self.add_bias(0, c, 1, b, tok)
            for c, acc, ts in rows:
                self.ada_mod(0, c, acc, ts)
            if self.plan:
                self.split(0)
                self.nsplit = 1
        return tx

    def begin(self):
        for i in range(self.NS if self.plan else 0):
            self.issue(i)

    def vec(self, name, i=0, n=1):
        at = VEC[name][0] + i
        return self.VEC[:, at:at + n]

    def mod(self, l, which):
        return (self.MOD[:, l * 72 + which * 8:l * 72 + which * 8 + 8],
                [self.mod_t[l, which * 4 + c] for c in range(4)])

    def modulate_first(self):
        sc, tsc = self.mod(0, 1)
        sh, tsh = self.mod(0, 0)
        s = self.small.get()
        t = self.dve([tsc, tsh, s.w], lambda e: e.tensor_scalar(s.ap[:, 0:8], sc, 1.0, None, ALU.add))
        self.ht = self.to_h(lambda n: [t, tsh, self.x_t[n]], s.ap, sh)
        for n in range(NT):
            x = self.XR[:, n, :]
            self.x_t[n] = self.act([self.ht[n]], lambda e: e.activation(x, x, ACT.Copy, scale=ALPHA))
        s.done(*flat(self.ht))

    def to_h(self, before, a, b):
        ht, prev = [], None
        for n in range(NT + 1):
            if n < NT:
                x, hi, q = self.XR[:, n, :], self.HH[:, n, :], self.tmp.get()
                w, an, bn = before(n), a[:, n:n + 1], b[:, n:n + 1]
                t1 = self.dve([w, self.hfree], lambda e: e.tensor_scalar(hi, x, an, bn, ALU.mult, ALU.add))
                t2 = self.act([w, q.w], lambda e: e.activation(q.ap, x, ACT.Identity, bias=bn, scale=an))
            if prev:
                m, qm, tm = prev
                him, lom = self.HH[:, m, :], self.HL[:, m, :]
                t3 = (self.pool, self.dve)[m % 2]([tm, self.hfree], lambda e: e.tensor_tensor(
                    lom, qm.ap, him.bitcast(F32), ALU.subtract))
                qm.done(t3)
                ht.append([*tm, t3])
            prev = (n, q, [t1, t2])
        return ht

    def gate(self, l, which, w):
        g, tg = self.mod(l, which)
        s = self.small.get()
        t = self.dve([tg, s.w], lambda e: e.tensor_scalar(s.ap[:, 0:8], g, w, w, ALU.mult, ALU.add))
        return s, t

    def update_gated(self, n, b, tok, s, ts):
        x, c = self.XR[:, n, :], s.ap[:, n:n + 1]
        t = self.dve([tok, ts, self.x_t[n]], lambda e: e.scalar_tensor_tensor(x, b.ap, c, x, ALU.mult, ALU.add))
        b.done(t)
        self.x_t[n] = t

    def update_plain(self, n, b, tok):
        x = self.XR[:, n, :]
        t = self.dve([tok, self.x_t[n]], lambda e: e.tensor_tensor(x, b.ap, x, ALU.add))
        b.done(t)
        self.x_t[n] = t

    def layer_norm(self, l, idx, mean, nxt):
        gain, beta = self.vec("ln_gain", l * 24 + idx * 8, 8), self.vec("ln_bias", l * 24 + idx * 8, 8)
        s = self.small.get()
        A, B, AG, AB = (s.ap[:, 8 * i:8 * i + 8] for i in range(4))
        if nxt is not None:
            sc, tsc = self.mod(nxt[0], nxt[2])
            sh, tsh = self.mod(nxt[0], nxt[1])
            t = self.dve([tsc, s.w, self.vec_t], lambda e: e.tensor_scalar(AG, sc, 1.0, None, ALU.add))
            ta = self.dve([t], lambda e: e.tensor_tensor(A, gain, AG, ALU.mult))
            tb = self.dve([t], lambda e: e.tensor_tensor(AB, beta, AG, ALU.mult))
            tb = self.dve([tb, tsh], lambda e: e.tensor_tensor(B, AB, sh, ALU.add))
            t1 = self.dve([ta, tb], lambda e: e.tensor_scalar(AG, gain, ALPHA, None, ALU.mult))
            t2 = self.dve([tb], lambda e: e.tensor_scalar(AB, beta, ALPHA, None, ALU.mult))
            small = [ta, tb, t1, t2]
        acc, ta = mean.w
        b = self.banks.get()
        tb_ = self.mm([ta, b.w], b.ap, self.col1024.to_broadcast([P, P]), acc.ap, sig=True)
        acc.done(tb_)
        rd, sq = [], []
        for n in range(NT):
            x = self.XR[:, n, :]
            td = self.dve([tb_, self.x_t[n]], lambda e: e.tensor_tensor(x, x, b.ap, ALU.subtract))
            if n == NT - 1:
                b.done(td)
            if n >= 6:
                self.fold(self.dve, sq, n - 1)
            q = self.tmp.get()
            ts = self.act([td, q.w], lambda e: e.activation(q.ap, x, ACT.Square))
            rd.append([td, ts])
            sq.append([q, ts])
            if n in (1, 3):
                self.fold(self.pool, sq, n)
        self.fold(self.dve, sq, 7)
        var = self.held.get()
        for i, n in enumerate((1, 3, 7)):
            q, ts = sq[n]
            tv = self.stat(var, 0, 1, q.ap, ts, self.col1024, i == 0, i == 2)
            q.done(tv)
        y, t, read = self.rsqrt(var.ap[:, 0:4], 4, 1e-5, [tv])
        var.done(read)
        b, tb_ = self.spread(y.ap, range(4), t)
        y.done(tb_)
        last = []

        def scaled(n):
            x = self.XR[:, n, :]
            t = self.dve([tb_, rd[n]], lambda e: e.tensor_tensor(x, x, b.ap, ALU.mult))
            b.done(t)
            return [t, small] if nxt is not None else t

        if nxt is not None:
            self.ht = self.to_h(scaled, A, B)
        else:
            for n in range(NT):
                x, g, c = self.XR[:, n, :], gain[:, n:n + 1], beta[:, n:n + 1]
                t = scaled(n)
                self.x_t[n] = self.act([t], lambda e: e.activation(x, x, ACT.Identity, bias=c, scale=g))
                last.append(self.x_t[n])
        if nxt is not None:
            for n in range(NT):
                x, g, c = self.XR[:, n, :], AG[:, n:n + 1], AB[:, n:n + 1]
                self.x_t[n] = self.act([self.ht[n], small], lambda e: e.activation(x, x, ACT.Identity, bias=c, scale=g))
                last.append(self.x_t[n])
        s.done(*last)

    def square_of(self, stats, tiles):
        tv = None
        for n in tiles:
            x, q = self.XR[:, n, :], self.tmp.get()
            ts = self.act([self.x_t[n], q.w], lambda e: e.activation(q.ap, x, ACT.Square))
            tv = self.stat(stats, 0, 1, q.ap, ts, self.col1024, n == 0, n == NT - 1)
            q.done(tv)
        return tv

    def fold(self, eng, sq, n):
        (q, t), (r, u) = sq[n], sq[n - 1]
        sq[n][1] = eng([t, u], lambda e: e.tensor_tensor(q.ap, q.ap, r.ap, ALU.add))
        r.done(sq[n][1])

    def rms_norm(self, name, l, sums=None, meanwhile=None):
        if sums is None:
            sums = Slot(None)
            self.square_of(sums, range(NT))
        acc, ta = sums.w
        st = self.held.get()
        tv = self.stat(st, 0, 1, acc.ap, ta, self.col1024, True, True)
        acc.done(tv)
        y, t, read = self.rsqrt(st.ap[:, 0:4], 4, 1e-6, [tv])
        st.done(read)
        if meanwhile:
            meanwhile[0]()
        b, tb = self.spread(y.ap, range(4), t)
        y.done(tb)
        self.ht = []
        for n in range(NT):
            x, g, q = self.XR[:, n, :], self.vec(name, l * 8 + n), self.tmp.get()
            t = self.dve([tb, q.w, self.x_t[n], self.vec_t], lambda e: e.scalar_tensor_tensor(q.ap, x, g, b.ap, ALU.mult, ALU.mult))
            self.ht.append(self.parts(self.HH[:, n, :], self.HL[:, n, :], q.ap, [t],
                                      self.dve if n % 2 else self.pool, self.hfree))
            q.done(*self.ht[n])
        b.done(t)
        if meanwhile:
            meanwhile[1]()

    def ffn(self, kind, names, l, groups, update, mean):
        H = (self.HH, self.HL)
        self.barrier()
        base = self.base
        sums = Slot(None)
        with ExitStack() as ctx:
            A = [(self.alloc(ctx, "ah", [P, 8, S], F32R), self.alloc(ctx, "al", [P, 8, S], F32R)) for _ in range(2)]
            afree = [base, base]
            up_n = names["n_up"]
            for gi, (g0, G) in enumerate(groups):
                AH, AL = A[gi % 2]
                at = []
                for m in range(G // 2):
                    idx = l * up_n + g0 // 2 + m
                    if kind == "swiglu":
                        ch = self.take(names["gate"], idx)
                        sl = []
                        for b, tok in self.feat2(ch, 8, H, self.ht, gi == 0 and m == 0):
                            q = self.tmp.get()
                            ts = self.act([tok, q.w], lambda e, q=q, b=b: e.activation(q.ap, b.ap, ACT.Silu))
                            b.done(ts)
                            sl.append((q, ts))
                        self.release(ch, tok)
                        ch = self.take(names["up"], idx)
                        for t in range(2):
                            b, tok = self.feat(ch, 8, 256, t, H, self.ht)
                            q, ts = sl[t]
                            ta = self.dve([tok, ts], lambda e, q=q, b=b: e.tensor_tensor(q.ap, q.ap, b.ap, ALU.mult))
                            b.done(ta)
                            k = 2 * m + t
                            at.append(self.parts(AH[:, k, :], AL[:, k, :], q.ap, [ta], free=afree[gi % 2]))
                            q.done(*at[k])
                        self.release(ch, tok)
                    else:
                        ch = self.take(names["up"], idx)
                        for t, (b, tok) in enumerate(self.feat2(ch, 8, H, self.ht, gi == 0 and m == 0)):
                            q = self.tmp.get()
                            ts = self.act([tok, q.w], lambda e, q=q, b=b: e.activation(q.ap, b.ap, ACT.Relu))
                            b.done(ts)
                            ta = self.dve([ts], lambda e, q=q: e.tensor_tensor(q.ap, q.ap, q.ap, ALU.mult))
                            k = 2 * m + t
                            at.append(self.parts(AH[:, k, :], AL[:, k, :], q.ap, [ta], free=afree[gi % 2]))
                            q.done(*at[k])
                        self.release(ch, tok)
                if gi == len(groups) - 1:
                    self.hfree = [tok]
                final = gi == len(groups) - 1 and mean
                done = []
                for c in range(4):
                    ch = self.take(names["down"][gi], l * 4 + c)
                    for t in range(2):
                        b, tok = self.feat(ch, G, 256, t, (AH, AL), at)
                        update(2 * c + t, b, tok)
                        done.append(2 * c + t)
                    self.release(ch, tok)
                    afree[gi % 2] = [tok]
                    if final:
                        f = self.mean_of if mean == "ln" else self.square_of
                        f(sums, done[:-2] if c < 3 else done)
                        done = done[-2:] if c < 3 else []
        self.barrier()
        return sums

    def mean_of(self, sums, tiles):
        for n in tiles:
            x = self.XR[:, n, :]
            if n == 0:
                sums.w = [self.tmp.get(6)]
            elif n == 1:
                a = sums.w[0]
                sums.w.append(self.pool([self.x_t[0], self.x_t[1], a.w], lambda e: e.tensor_tensor(
                    a.ap, self.XR[:, 0, :], x, ALU.add)))
            else:
                a, t = sums.w
                q = self.dve if n == NT - 1 else self.pool
                sums.w[1] = q([self.x_t[n], t], lambda e: e.tensor_tensor(a.ap, a.ap, x, ALU.add))

    def square_of(self, sums, tiles):
        for n in tiles:
            x, q = self.XR[:, n, :], self.tmp.get()
            ts = self.act([self.x_t[n], q.w], lambda e: e.activation(q.ap, x, ACT.Square))
            if n == 0:
                sums.w = [q, ts]
            else:
                a, t = sums.w
                eng = self.dve if n == NT - 1 else self.pool
                sums.w[1] = eng([ts, t], lambda e: e.tensor_tensor(a.ap, a.ap, q.ap, ALU.add))
                q.done(sums.w[1])

    def project_out(self, name, idx0, kt, nc_, Y, yt, update, mean):
        sums, done = Slot(None), []
        per = nc_ // P
        for c in range(NT // per):
            ch = self.take(name, idx0 + c)
            for t in range(per):
                b, tok = self.feat(ch, kt, nc_, t, Y, yt)
                update(per * c + t, b, tok)
                done.append(per * c + t)
            self.release(ch, tok)
            if mean:
                last = c == NT // per - 1
                f = self.mean_of if mean == "ln" else self.square_of
                f(sums, done if last else done[:-2])
                done = done[-2:]
        self.hfree = [tok]
        return sums

    def copy_out(self, dst, b, tok, waits=(), scale=None, q=None, src=None):
        src = b.ap if src is None else src
        q = q or self.act
        if q is self.act:
            if scale is None:
                t = q([tok, list(waits)], lambda e: e.activation(dst, src, ACT.Copy))
            else:
                t = q([tok, list(waits)], lambda e: e.activation(dst, src, ACT.Copy, scale=scale))
        else:
            t = q([tok, list(waits)], lambda e: e.tensor_copy(dst, src))
        return t

    def rope(self, x, tok, perm, cos, sin, ctok=()):
        b = self.banks.get()
        tp = self.mm([tok, b.w, list(ctok)], b.ap, perm, x, sig=True)
        q = self.tmp.get()
        t1 = self.dve([tp, q.w, list(ctok)], lambda e: e.tensor_tensor(q.ap, b.ap, sin, ALU.mult))
        b.done(t1)
        t2 = self.pool([tok, tp, list(ctok)], lambda e: e.tensor_tensor(x, x, cos, ALU.mult))
        t3 = self.dve([t1, t2], lambda e: e.tensor_tensor(x, x, q.ap, ALU.add))
        q.done(t3)
        return t3

    def tick(self):
        while self.bg and callable(self.bg[0]) and self.bg[0]():
            self.bg.pop(0)
        if (self.bg and not callable(self.bg[0]) and len(self.active) < self.depth
                and self.tmp.free() >= self.spare):
            self.active.append(self.bg.pop(0))
        keep = []
        for u in self.active:
            if next(u, "end") != "end":
                keep.append(u)
        self.active = keep

    def until(self, ready):
        while not ready():
            self.tick()

    def pipeline(self, units=()):
        self.bg.extend(units)
        while self.bg or self.active:
            self.tick()

    def softmax_rows(self, src, n, bias, tok, extra=(), mask_from=None):
        q, sm = self.tmp.get(), self.small.get()
        e_, mx, nm, sm_, rc = q.ap[:, 0:n], sm.ap[:, 0:1], sm.ap[:, 1:2], sm.ap[:, 2:3], sm.ap[:, 3:4]
        if bias is not None:
            t = self.dve([tok, q.w, sm.w, list(extra)], lambda e: e.tensor_tensor_reduce(
                e_, src.ap[:, 0:n], bias, 1.0, -3e38, ALU.add, ALU.max, mx))
            src.done(t)
            t = self.dve([t], lambda e: e.tensor_scalar(nm, mx, -1.0, None, ALU.mult))
            t = self.act([t], lambda e: e.activation(e_, e_, ACT.Exp, bias=nm, accum_out=sm_))
        else:
            t = self.dve([tok, sm.w], lambda e: e.tensor_reduce(mx, src.ap[:, 0:n], AXX, ALU.max))
            t = self.dve([t], lambda e: e.tensor_scalar(nm, mx, -1.0, None, ALU.mult))
            t = self.act([t, q.w], lambda e: e.activation(e_, src.ap[:, 0:n], ACT.Exp, bias=nm, accum_out=sm_))
            src.done(t)
        return q, sm, t

    def attend(self, Q, K, V, lo, i, n, bias, extra, out, osl, first, last, finish):
        b = self.banks.get()
        tok = self.mm([extra, b.w], b.ap[:, 0:n], Q, K, sig=True)
        q, sm, t = self.softmax_rows(b, n, bias, tok, extra)
        yield
        e_, rc = q.ap[:, 0:n], sm.ap[:, 3:4]
        t = self.dve([t], lambda e: e.reciprocal(rc, sm.ap[:, 2:3]))
        t = self.dve([t], lambda e: e.tensor_scalar(e_, e_, rc, None, ALU.mult))
        sm.done(t)
        yield
        b = self.banks.get()
        for j in range(n // P):
            tt = self.pe([t, b.w], lambda e, j=j: e.transpose(b.ap[:, j * P:(j + 1) * P], e_[:, j * P:(j + 1) * P], self.ident),
                         sig=(j == n // P - 1))
        q.done(tt)
        p = self.tmp.get()
        t = self.act([tt, p.w], lambda e: e.activation(p.ap[:, 0:n], b.ap[:, 0:n], ACT.Copy))
        b.done(t)
        yield
        o = out()
        for j in range(n // P):
            to = self.mm([t, o.w, extra], osl(o), V(j), p.ap[:, j * P:(j + 1) * P], j == 0, j == n // P - 1,
                         sig=(j == n // P - 1))
        p.done(to)
        if last:
            finish(o, to)


def consts():
    f = np.float32
    i = np.arange(P)
    cc = {}
    cc["ident"] = np.eye(P, dtype=f)
    cc["one"] = np.ones((P, 1), f)
    cc["later"] = (i[:, None] > i[None, :]).astype(f)

    def perm(half, width):
        m = np.zeros((P, P), f)
        for a in range(0, P, 64):
            for r in range(half):
                m[a + half + r, a + r] = -1.0
                m[a + r, a + half + r] = 1.0
        return m

    cc["perm1"] = perm(32, 64)
    cc["perm2"] = perm(8, 16)
    w = np.arange(S)
    diff = i[:, None] + 384 - w[None, :]
    cc["causal"] = np.where(diff >= 0, 0.0, NEG).astype(f)
    cc["strict"] = (i[:, None] < i[None, :]).astype(f)
    blk = np.zeros((P, 2), f)
    blk[0:64, 0] = blk[64:, 1] = 1.0 / 64
    cc["blk"] = blk
    cc["col1024"] = np.full((P, 1), 1.0 / 1024, f)
    cc["col256"] = np.full((P, 1), 1.0 / 256, f)
    cc["col128"] = np.full((P, 1), 1.0 / 128, f)
    inv = (np.float64(500000.0) ** (-np.arange(0, 16, 2, dtype=np.float64) / 16)).astype(f)
    col = np.zeros((P, 1), f)
    for a in (0, 64):
        col[a:a + 8, 0] = inv
        col[a + 8:a + 16, 0] = inv
    cc["inv"] = col
    c1 = {}
    t = np.arange(S, dtype=f)
    for name, freq in (("ret", 1.0 / (10000.0 ** np.linspace(0.0, 1.0, 32))),
                       ("dil", 1.0 / (10000.0 ** (np.arange(0, 64, 2) / 64)))):
        ang = (t[None, :] * freq.astype(f)[:, None]).astype(f).astype(np.float64)
        c1[name + "_cos"] = np.tile(np.cos(ang), (4, 1)).astype(f)
        c1[name + "_sin"] = np.tile(np.sin(ang), (4, 1)).astype(f)
    for h in range(4):
        lg = np.log1p(-(2.0 ** (-5.0 - h)))
        d = w[None, :] - i[:, None]
        c1[f"decay{h}"] = (np.where(d >= 0, np.exp(lg * np.maximum(d, 0)), 0.0) * 0.125).astype(f)
    cnt = (diff >= 0).astype(np.int64) * ((diff <= 128).astype(np.int64) + (diff % 4 == 0) + (diff % 16 == 0))
    c1["dil_mask"] = np.where(cnt > 0, np.log(np.maximum(cnt, 1)), NEG).astype(f)
    sel = np.zeros((P, 13 * P), f)
    for v in range(13 * P):
        sel[v // 64, v] = 1.0
    ct = np.zeros((P, 64), f)
    for g, wd in enumerate((2, 4, 8, 16)):
        ct[:, g * 16:(g + 1) * 16] = 1.0 / np.minimum(np.arange(16) + 1, wd)
    c2 = {"sel": sel, "count": ct}
    out = []
    for d in (cc, c1, c2):
        at, where = 0, {}
        for k, v in d.items():
            where[k] = (at, v.shape[1])
            at += v.shape[1]
        out.append((np.ascontiguousarray(np.concatenate(list(d.values()), 1)), where))
    return out


def first_mixer(p, l):
    H = (p.HH, p.HL)
    p.barrier()
    base = p.base
    with ExitStack() as ctx:
        RQ, RK = p.alloc(ctx, "rq", [P, 2, S]), p.alloc(ctx, "rk", [P, 2, S])
        RV, RG = p.alloc(ctx, "rv", [P, 4, S]), p.alloc(ctx, "rg", [P, 4, S])
        DQ, DK, DV = p.alloc(ctx, "dq", [P, 2, S]), p.alloc(ctx, "dk", [P, 2, S]), p.alloc(ctx, "dv", [P, 4, 256])
        SQ, SK, SV = p.alloc(ctx, "sq", [P, 2, S]), p.alloc(ctx, "sk", [P, 2, S]), p.alloc(ctx, "sv", [P, 4, 256])
        NK = p.alloc(ctx, "nk", [P, 2, 1280])
        extra = p.more_tmp(ctx, 3)
        yt = [None] * 8
        kept = {}
        tk = {}

        p.dve([p.c1_t], lambda e: e.nop(), sig=False)

        def fproj(idx, dst, key, scale=None, eager=False, after=None):
            ch = p.take("w_in", l * 12 + idx)
            r = []
            for t, (b, tok) in enumerate(p.feat2(ch, 8, H, p.ht, eager)):
                r.append(p.copy_out(dst[:, t, :], b, tok, base, scale))
                b.done(r[-1])
            p.release(ch, tok)
            tk[key] = r

        def tproj(idx, dst, c0, key):
            ch = p.take("w_in", l * 12 + idx)
            for i in (0, 2):
                b, tok = p.toks(ch, 8, 256, [i, i + 1], H, p.ht)
                tk.setdefault(key, []).append(p.copy_out(dst[:, i:i + 2, c0:c0 + 256], b, tok, base,
                                                         src=b.ap.rearrange("p (a n) -> p a n", a=2)))
                b.done(tk[key][-1])
            p.release(ch, tok)
            return tok

        def roped(X, key, kind):
            tk[key] = [p.rope(X[:, t, :], tk[key][t], p.perm1, p.c1(kind + "_cos"), p.c1(kind + "_sin"), [p.c1_t])
                       for t in range(2)]

        def keep(n, o, to, dst, waits=()):
            t = p.copy_out(dst, o, to, waits)
            o.done(t)
            kept[n] = (dst, t)

        offs = [0, 512, 896, 1152]
        nk_t = {}
        nkfree = [[], []]
        sb_last = []

        def sb_unit(h, j, cell):
            r = slice(64 * (h % 2), 64 * (h % 2) + 64)
            n = S - j * P
            nk = NK[:, h % 2, offs[j]:offs[j] + n]
            b = p.banks.get()
            tok = p.mm([tk["sq"], tk["sk"], b.w], b.ap[:, 0:n], SK[r, h // 2, j * P:(j + 1) * P], SQ[r, h // 2, j * P:S], sig=True)
            z = b.ap[:, 0:n]
            q = p.tmp.get()
            a = q.ap[:, 0:n]
            t = p.dve([tok, q.w], lambda e: e.tensor_scalar(a, z, 0.0, -2.0, ALU.max, ALU.mult))
            t = p.dve([t], lambda e: e.tensor_tensor(a, z, a, ALU.add))
            t = p.act([t], lambda e: e.activation(a, a, ACT.Exp))
            t = p.act([t], lambda e: e.activation(a, a, ACT.Ln, bias=1.0))
            yield
            t1 = p.dve([t, base, nkfree[h % 2]], lambda e: e.scalar_tensor_tensor(nk, z, 0.0, a, ALU.max, ALU.add))
            t2 = p.dve([t1], lambda e: e.tensor_tensor(a, z, nk, ALU.subtract))
            b.done(t2)
            nk_t[h, j] = p.dve([t2], lambda e: e.tensor_tensor(nk[:, 0:P], nk[:, 0:P], p.strict, ALU.mult))
            yield
            b = p.banks.get()
            bt = p.mm([nk_t[h, j], b.w], b.ap[:, 0:n], p.later, nk, True, j == 3, sig=(j == 3))
            for jj in range(j + 1, 4):
                m = S - jj * P
                bt = p.mm([nk_t[h, jj]], b.ap[:, n - m:n], p.one.to_broadcast([P, P]), NK[:, h % 2, offs[jj]:offs[jj] + m],
                          False, jj == 3, sig=(jj == 3))
            if j == 0:
                nkfree[h % 2] = [bt]
            t = p.dve([bt, t2], lambda e: e.tensor_tensor(a, a, b.ap[:, 0:n], ALU.subtract))
            b.done(t)
            t = p.act([t], lambda e: e.activation(a, a, ACT.Exp))
            yield
            t = p.dve([t], lambda e: e.tensor_tensor(a[:, 0:P], a[:, 0:P], p.strict, ALU.mult))
            if not cell:
                cell.append(p.held.get())
            o = cell[0]
            to = p.mm([t, o.w, tk["sv"]], o.ap[r, j * P:S], SV[:, j, 64 * h:64 * h + 64], a, j == 3, j == 0, sig=True)
            q.done(to)
            if j == 0 and h % 2 == 1:
                keep(6 + h // 2, o, to, SQ[:, h // 2, :])
                sb_last.append(to)

        def sb_units():
            for h in range(4):
                if h % 2 == 0:
                    cell = []
                for j in (3, 2, 1, 0):
                    yield sb_unit(h, j, cell)

        NKF = NK[:, :, :].rearrange("p a n -> p (a n)")
        oh = {}

        def ret_unit(h, j, cell):
            r = slice(64 * (h % 2), 64 * (h % 2) + 64)
            n = S - j * P
            b = p.banks.get()
            tok = p.mm([tk["rq"], tk["rk"], b.w], b.ap[:, 0:n], RK[r, h // 2, j * P:(j + 1) * P], RQ[r, h // 2, j * P:S], sig=True)
            q = p.tmp.get()
            t = p.dve([tok, q.w], lambda e: e.tensor_tensor(q.ap[:, 0:n], b.ap[:, 0:n], p.c1(f"decay{h}")[:, 0:n], ALU.mult))
            b.done(t)
            yield
            if j == 0:
                cell.append(p.held.get())
            o = cell[0]
            to = p.mm([t, o.w, tk["rv"]], o.ap[:, j * P:S], RV[:, j, h * P:(h + 1) * P], q.ap[:, 0:n], j == 0, j == 3, sig=True)
            q.done(to)
            if j == 3:
                dst = NKF[:, h * S:(h + 1) * S]
                t = p.copy_out(dst, o, to, sb_last)
                o.done(t)
                oh[h] = (dst, t)

        def ret_norm():
            yield
            yield
            st = p.held.get()
            for h in range(4):
                dst, t = oh[h]
                tm = p.stat(st, h, 4, dst, t, p.col128, True, True)
            yield
            y = p.yr.get()
            t = p.dve([tm, y.w], lambda e: e.tensor_copy(y.ap[:, 0:16], st.ap[:, 0:16]))
            st.done(t)
            st = p.held.get()
            prev = None
            for h in range(5):
                if h < 4:
                    dst, to = oh[h]
                    b, tb = p.spread(y.ap, [4 * i + h for i in range(4)], t)
                    td = p.dve([tb, to], lambda e: e.tensor_tensor(dst, dst, b.ap, ALU.subtract))
                    b.done(td)
                    q = p.tmp.get()
                    ts = p.act([td, q.w], lambda e: e.activation(q.ap, dst, ACT.Square))
                    oh[h] = (dst, [td, ts])
                if prev is not None:
                    q0, ts0 = prev
                    tv = p.stat(st, h - 1, 4, q0.ap, ts0, p.col128, True, True)
                    q0.done(tv)
                prev = (q, ts)
                yield
            y.done(tb)
            y, t, read = p.rsqrt(st.ap[:, 0:16], 16, 1e-6, [tv])
            st.done(read)
            yield
            for h in range(4):
                dst, to = oh[h]
                b, tb = p.spread(y.ap, [4 * i + h for i in range(4)], t)
                g = RG[:, h, :]
                tg = p.pool([tk["rg"][h], to], lambda e: e.tensor_tensor(g, dst, g, ALU.mult))
                td = p.dve([tb, tg], lambda e: e.tensor_tensor(g, g, b.ap, ALU.mult))
                b.done(td)
                kept[h] = (g, td)
                yield
            y.done(tb)

        def ret_units():
            for h in range(4):
                cell = []
                for j in range(4):
                    yield ret_unit(h, j, cell)
            yield ret_norm()

        def dil_units():
            for pr in range(2):
                cell = []

                def out(cell=cell):
                    if not cell:
                        cell.append(p.held.get())
                    return cell[0]

                for i in range(4):
                    for c in range(2):
                        n = (i + 1) * P
                        r = slice(64 * c, 64 * c + 64)
                        yield p.attend(
                            DQ[r, pr, i * P:(i + 1) * P], DK[r, pr, 0:n],
                            lambda j, pr=pr, c=c: DV[:, j, 64 * (2 * pr + c):64 * (2 * pr + c) + 64],
                            0, i, n, p.c1("dil_mask")[:, 384 - i * P:S], [tk["dq"], tk["dk"], tk["dv"], p.c1_t], out,
                            lambda o, r=r, i=i: o.ap[r, i * P:(i + 1) * P], i == 0, i == 3 and c == 1,
                            lambda o, to, pr=pr: keep(4 + pr, o, to, DQ[:, pr, :]))

        fproj(9, SQ, "sq", 0.125, eager=True)
        fproj(10, SK, "sk")
        tproj(11, SV, 0, "sv")
        p.bg.extend(sb_units())
        fproj(0, RQ, "rq")
        fproj(1, RK, "rk")
        roped(RQ, "rq", "ret")
        roped(RK, "rk", "ret")
        tproj(2, RV, 0, "rv")
        tproj(3, RV, 256, "rv")
        p.bg.extend(ret_units())
        tk["rg"] = []
        for c in range(2):
            ch = p.take("w_in", l * 12 + 4 + c)
            for t, (b, tok) in enumerate(p.feat2(ch, 8, H, p.ht)):
                dst = RG[:, 2 * c + t, :]
                tk["rg"].append(p.act([tok, base], lambda e: e.activation(dst, b.ap, ACT.Silu)))
                b.done(tk["rg"][-1])
            p.release(ch, tok)
        fproj(6, DQ, "dq", 0.125)
        fproj(7, DK, "dk")
        roped(DQ, "dq", "dil")
        roped(DK, "dk", "dil")
        last = tproj(8, DV, 0, "dv")
        p.hfree = [last]
        p.pipeline(dil_units())
        for i, n in enumerate((6, 7, 0, 1, 2, 3, 4, 5)):
            src, t = kept[n]
            yt[n] = p.parts(p.HH[:, n, :], p.HL[:, n, :], src, [t], (p.pool, p.dve)[i % 2], p.hfree)
        s, ts = p.gate(l, 5, 1.0)
        r = p.project_out("w_out", l * 4, 8, 256, H, yt, lambda n, b, tok: p.update_gated(n, b, tok, s, ts), "ln")
        s.done(p.x_t[7])
        p.less_tmp(extra)
    p.barrier()
    return r


def even_mixer(p):
    H = (p.HH, p.HL)
    p.barrier()
    base = p.base
    with ExitStack() as ctx:
        QA, KA, VA = (p.alloc(ctx, n, [P, 4, S]) for n in ("qa", "ka", "va"))
        QB, KB, VB = (p.alloc(ctx, n, [P, 4, S]) for n in ("qb", "kb", "vb"))
        QI, KI = p.alloc(ctx, "qi", [P, 2, S]), p.alloc(ctx, "ki", [P, S])
        BM = p.alloc(ctx, "bm", [P, 1152])
        RT = p.alloc(ctx, "rt", [32, S])
        WI = p.alloc(ctx, "wi", [P, 4, 4])
        ST = p.alloc(ctx, "stt", [P, 4, 16])
        more = p.more_tmp(ctx, 1)
        p.spare, p.depth = 4, 6
        p.dve([p.c2_t, p.rope_t, p.lam_t], lambda e: e.nop(), sig=False)
        raw = {}
        st_t, st_free = [], []
        rt_free = list(base)
        pend = []

        def flush(col=p.blk, n=2):
            if not pend:
                return
            b = p.banks.get()
            c0 = pend[0][2]
            w = n * len(pend)
            for k, (q, ts, c) in enumerate(pend):
                tv = p.stat(b, c - c0, w, q.ap, ts, col, True, True, n=n)
                q.done(tv)
            t = p.dve([tv, st_free, base], lambda e: e.tensor_copy(
                ST[:, :, c0:c0 + w], b.ap[:, 0:4 * w].rearrange("p (a n) -> p a n", a=4)))
            b.done(t)
            st_t.append(t)
            pend.clear()

        def squared(b, tok, col):
            q = p.tmp.get()
            ts = p.act([tok, q.w], lambda e: e.activation(q.ap, b.ap, ACT.Square))
            b.done(ts)
            pend.append((q, ts, col))

        def fproj(idx, dst, key, col, stat=True, eager=False):
            ch = p.take("w_in_e", idx)
            flush()
            for t, (b, tok) in enumerate(p.feat2(ch, 8, H, p.ht, eager)):
                raw[key, t] = p.copy_out(dst[t], b, tok, base)
                if stat:
                    squared(b, tok, col + 2 * t)
                else:
                    b.done(raw[key, t])
            p.release(ch, tok)
            return tok

        def group(n, tiles):
            y, t, read = p.rsqrt(ST[:, :, 0:n], 4 * n, 1e-6, list(st_t))
            st_free[:] = [read]
            st_t.clear()
            yield
            b = p.banks.get()
            for i in range(4):
                tt = p.pe([t, b.w], lambda e, i=i: e.transpose(b.ap[0:n, i * P:(i + 1) * P],
                                                               y.ap[:, i * n:(i + 1) * n], p.ident), sig=(i == 3))
            y.done(tt)
            t_rt = p.dve([tt, list(rt_free)], lambda e: e.tensor_copy(RT[0:n, :], b.ap[0:n, :]))
            b.done(t_rt)
            yield
            prev = None
            for k in range(len(tiles) + 1):
                if k < len(tiles):
                    x, g, tok, put = tiles[k]
                    b = p.banks.get()
                    tb = p.mm([t_rt, b.w, p.c2_t], b.ap, p.c2("sel")[0:n, k * P:(k + 1) * P], RT[0:n, :], sig=True)
                    t = p.dve([tb, tok], lambda e: e.scalar_tensor_tensor(x, x, g, b.ap, ALU.mult, ALU.mult))
                    b.done(t)
                    rt_free[:] = [tb]
                if prev:
                    prev[1](p.rope(prev[0], prev[2], p.perm2, p.COS2, p.SIN2, [p.rope_t]))
                prev = (x, put, t)
                yield

        def putter(lst, n):
            def put(t):
                lst[n] = t
            return put

        ki_t, qi_t = [None], [None, None]
        ch = p.take("w_kiwi", 0)
        b, tok = p.feat(ch, 8, 132, 0, H, p.ht)
        t_ki = p.copy_out(KI[:, :], b, tok, base)
        squared(b, tok, 0)
        b, tok = p.toks(ch, 8, 132, [0, 1, 2, 3], H, p.ht, cols=(128, 4))
        t_wi = p.dve([tok, base], lambda e: e.tensor_scalar(
            WI[:, :, :], b.ap[:, 0:16].rearrange("p (a n) -> p a n", a=4), 1.0 / 16, None, ALU.mult))
        b.done(t_wi)
        p.release(ch, tok)
        ch = p.take("w_in_e", 7)
        flush()
        p.bg.append(group(2, [(KI[:, :], p.vec("g_kidx"), t_ki, putter(ki_t, 0))]))
        for t, (b, tok) in enumerate(p.feat2(ch, 8, H, p.ht)):
            raw["qi", t] = p.copy_out(QI[:, t, :], b, tok, base)
            b.done(raw["qi", t])
        p.release(ch, tok)
        p.until(lambda: ki_t[0])

        bm_at = [None, 0, 256, 640]
        bm_t = [None] * 4

        def index():
            for t in range(2):
                qi_t[t] = p.rope(QI[:, t, :], raw["qi", t], p.perm2, p.COS2, p.SIN2, [p.rope_t])
                yield
            for i in (1, 2, 3):
                n = (i + 1) * P
                w = BM[:, bm_at[i]:bm_at[i] + n]
                tw = None
                for h in range(4):
                    r = slice(64 * (h % 2), 64 * (h % 2) + 64)
                    b = p.banks.get()
                    tok = p.mm([qi_t, ki_t, b.w], b.ap[:, 0:n], QI[r, h // 2, i * P:(i + 1) * P], KI[r, 0:n], sig=True)
                    q = p.tmp.get()
                    t = p.act([tok, q.w], lambda e: e.activation(q.ap[:, 0:n], b.ap[:, 0:n], ACT.Relu))
                    b.done(t)
                    s = WI[:, i, h:h + 1]
                    if h == 0:
                        tw = p.dve([t, base, t_wi], lambda e: e.tensor_scalar(w, q.ap[:, 0:n], s, None, ALU.mult))
                    else:
                        tw = p.dve([t, tw], lambda e: e.scalar_tensor_tensor(w, q.ap[:, 0:n], s, w, ALU.mult, ALU.add))
                    q.done(tw)
                    if h % 2:
                        yield
                tw = p.dve([tw], lambda e: e.tensor_tensor(w, w, p.causal[:, 384 - i * P:S], ALU.add))
                s = p.small.get()
                for r in range(16):
                    tm = p.dve([tw, s.w], lambda e: e.max(s.ap[:, 0:8], w))
                    tw = p.dve([tm], lambda e: e.match_replace(w, s.ap[:, 0:8], w, TAKEN))
                    yield
                s.done(tw)
                bm_t[i] = p.dve([tw], lambda e: e.tensor_scalar(w, w, -2e38, NEG, ALU.is_gt, ALU.mult))

        p.bg.append(index())
        small = p.small.get()
        tg = p.dve([small.w, p.vec_t], lambda e: e.tensor_scalar(small.ap[:, 0:1], p.vec("gq_a"), 0.125, None, ALU.mult))
        tg = p.dve([tg], lambda e: e.tensor_scalar(small.ap[:, 1:2], p.vec("gq_b"), 0.125, None, ALU.mult))
        for i, (X, key) in enumerate(((QA, "qa"), (KA, "ka"))):
            for c in range(2):
                fproj(2 * i + c, [X[:, 2 * c, :], X[:, 2 * c + 1, :]], (key, c), 8 * i + 4 * c)
        qa, ka, qb, kb = ([None] * 4 for _ in range(4))
        va = []
        for c in range(2):
            ch = p.take("w_in_e", 8 + c)
            if c == 0:
                flush()
                order = [(QA, "qa", small.ap[:, 0:1], qa), (KA, "ka", p.vec("gk_a"), ka)]
                p.bg.append(group(16, [(X[:, n, :], g, [raw[(key, n // 2), n % 2], tg], putter(lst, n))
                                       for X, key, g, lst in order for n in range(4)]))
            for i in (0, 2):
                b, tok = p.toks(ch, 8, 256, [i, i + 1], H, p.ht)
                va.append(p.copy_out(VA[:, i:i + 2, 256 * c:256 * c + 256], b, tok, base,
                                     src=b.ap.rearrange("p (a n) -> p a n", a=2)))
                b.done(va[-1])
            p.release(ch, tok)

        lam = p.LAM[:, 0:1]
        o_raw = {}

        def a_unit(h, i, cell):
            n = (i + 1) * P
            sub = []
            for c in range(2):
                r = slice(64 * c, 64 * c + 64)
                b = p.banks.get()
                tok = p.mm([qa[h], ka[h], b.w], b.ap[:, 0:n], QA[r, h, i * P:(i + 1) * P], KA[r, h, 0:n], sig=True)
                sub.append(p.softmax_rows(b, n, p.causal[:, 384 - i * P:S], tok))
            yield
            (q0, s0, t0), (q1, s1, t1) = sub
            e0, e1 = q0.ap[:, 0:n], q1.ap[:, 0:n]
            t0 = p.dve([t0], lambda e: e.reciprocal(s0.ap[:, 3:4], s0.ap[:, 2:3]))
            t1 = p.dve([t1], lambda e: e.reciprocal(s1.ap[:, 3:4], s1.ap[:, 2:3]))
            t0 = p.dve([t0], lambda e: e.tensor_scalar(e0, e0, s0.ap[:, 3:4], None, ALU.mult))
            t1 = p.dve([t1, p.lam_t], lambda e: e.tensor_tensor(s1.ap[:, 4:5], s1.ap[:, 3:4], lam, ALU.mult))
            t = p.dve([t0, t1], lambda e: e.scalar_tensor_tensor(e0, e1, s1.ap[:, 4:5], e0, ALU.mult, ALU.add))
            q1.done(t)
            s0.done(t)
            s1.done(t)
            yield
            b = p.banks.get()
            for j in range(i + 1):
                tt = p.pe([t, b.w], lambda e, j=j: e.transpose(b.ap[:, j * P:(j + 1) * P], e0[:, j * P:(j + 1) * P], p.ident),
                          sig=(j == i))
            q0.done(tt)
            pt = p.tmp.get()
            t = p.act([tt, pt.w], lambda e: e.activation(pt.ap[:, 0:n], b.ap[:, 0:n], ACT.Copy))
            b.done(t)
            yield
            if not cell:
                cell.append(p.held.get())
            o = cell[0]
            for j in range(i + 1):
                to = p.mm([t, o.w, va], o.ap[:, i * P:(i + 1) * P], VA[:, j, h * P:(h + 1) * P], pt.ap[:, j * P:(j + 1) * P],
                          j == 0, j == i, sig=(j == i))
            pt.done(to)
            if i == 3:
                dst = QA[:, h, :]
                t = p.copy_out(dst, o, to)
                o.done(t)
                o_raw[h] = (dst, t)

        def a_units():
            for h in range(4):
                cell = []
                for i in range(4):
                    yield a_unit(h, i, cell)

        p.bg.append(lambda: ka[3])
        p.bg.extend(a_units())
        fproj(6, [KB[:, 0, :], KB[:, 1, :]], ("ckv", 0), 0)
        sq, pend[:] = list(pend), []
        ct = []

        def compressed():
            b = p.banks.get()
            for i in range(4):
                for k in range(2):
                    tv = p.mm([sq[k][1], b.w], b.ap[:, i:i + 1], sq[k][0].ap[:, i * P:(i + 1) * P],
                              p.col256, k == 0, k == 1, sig=(i == 3 and k == 1))
            for k in range(2):
                sq[k][0].done(tv)
            yield
            y, t, read = p.rsqrt(b.ap[:, 0:4], 4, 1e-6, [tv])
            b.done(read)
            yield
            b, tb = p.spread(y.ap, range(4), t)
            y.done(tb)
            cs = []
            for k in range(2):
                q, x = p.tmp.get(), KB[:, k, :]
                t = p.dve([tb, q.w, raw[("ckv", 0), k]], lambda e: e.scalar_tensor_tensor(
                    q.ap, x, p.vec("g_kv_b", k), b.ap, ALU.mult, ALU.mult))
                cs.append((q, t))
            b.done(t)
            yield
            held.extend(cs)

        held = []
        p.bg.insert(0, compressed())
        for c in range(2):
            last = fproj(4 + c, [QB[:, 2 * c, :], QB[:, 2 * c + 1, :]], ("qb", c), 4 * c)
        p.hfree = [last]
        p.until(lambda: held)
        for k, (q, t) in enumerate(held):
            ct.append(p.parts(p.HH[:, k, :], p.HL[:, k, :], q.ap, [t], p.dve, p.hfree))
            q.done(*ct[k])
        ch = p.take("w_kv_up", 0)
        flush()
        for n in range(4):
            b, tok = p.feat(ch, 2, 1024, n, H, ct)
            raw["kb", n] = p.copy_out(KB[:, n, :], b, tok, base)
            squared(b, tok, 8 + 2 * n)
            if n % 2:
                flush()
            p.tick()
        order = [(QB, lambda n: raw[("qb", n // 2), n % 2], small.ap[:, 1:2], qb), (KB, lambda n: raw["kb", n], p.vec("gk_b"), kb)]
        p.bg.insert(0, group(16, [(X[:, n, :], g, [at(n), tg], putter(lst, n))
                                  for X, at, g, lst in order for n in range(4)]))
        vb = []
        for i in range(4):
            b, tok = p.toks(ch, 2, 1024, [i], H, ct, cols=(512, 512))
            vb.append(p.copy_out(VB[:, i, :], b, tok, base))
            b.done(vb[-1])
            p.tick()
        p.release(ch, tok)
        p.hfree = [tok]
        yt = [None] * 8

        def a_norm():
            sg = p.small.get()
            tg = p.dve([sg.w], lambda e: e.tensor_scalar(sg.ap[:, 0:1], p.vec("g_sub_a"), 0.8, None, ALU.mult))
            st = p.banks.get()
            for h in range(4):
                dst, t = o_raw[h]
                q = p.tmp.get()
                ts = p.act([t, q.w], lambda e: e.activation(q.ap, dst, ACT.Square))
                yield
                tv = p.stat(st, h, 4, q.ap, ts, p.col128, True, True)
                q.done(tv)
            y, t, read = p.rsqrt(st.ap[:, 0:16], 16, 1e-6, [tv])
            st.done(read)
            yield
            for h in range(4):
                dst, to = o_raw[h]
                b, tb = p.spread(y.ap, [4 * i + h for i in range(4)], t)
                td = p.dve([tb, to, tg, tv], lambda e: e.scalar_tensor_tensor(dst, dst, sg.ap[:, 0:1], b.ap, ALU.mult, ALU.mult))
                b.done(td)
                yt[h] = p.parts(p.HH[:, h, :], p.HL[:, h, :], dst, [td], p.pool, p.hfree)
                yield
            y.done(tb)
            sg.done(td)

        def emit(n, o, to):
            yt[n] = p.parts(p.HH[:, n, :], p.HL[:, n, :], o.ap, [to], p.dve, p.hfree)
            o.done(*yt[n])

        def b_units():
            for pr in range(4):
                cell = []

                def out(cell=cell):
                    if not cell:
                        cell.append(p.held.get())
                    return cell[0]

                for i in range(4):
                    for c in range(2):
                        n = (i + 1) * P
                        r = slice(64 * c, 64 * c + 64)
                        bias = p.causal[:, 384:S] if i == 0 else BM[:, bm_at[i]:bm_at[i] + n]
                        yield p.attend(
                            QB[r, pr, i * P:(i + 1) * P], KB[r, pr, 0:n],
                            lambda j, pr=pr, c=c: VB[:, j, 64 * (2 * pr + c):64 * (2 * pr + c) + 64],
                            0, i, n, bias, [qb[pr], kb[pr], vb, bm_t[i]], out,
                            lambda o, r=r, i=i: o.ap[r, i * P:(i + 1) * P], i == 0, i == 3 and c == 1,
                            lambda o, to, pr=pr: emit(4 + pr, o, to))

        p.bg.append(lambda: len(o_raw) == 4)
        p.bg.append(a_norm())
        p.bg.append(lambda: kb[3] and bm_t[3])
        p.pipeline(b_units())
        small.done(*qa, *qb)
        p.less_tmp(more)
        p.spare, p.depth = 0, 5
        p.barrier()
        r = p.project_out("w_out_e", 0, 8, 256, H, yt, p.update_plain, "rms")
    p.barrier()
    return r


def odd_mixer(p):
    H = (p.HH, p.HL)
    p.barrier()
    base = p.base
    with ExitStack() as ctx:
        GB, GC = p.alloc(ctx, "gb", [P, 4, S]), p.alloc(ctx, "gc", [P, 4, S])
        U = p.alloc(ctx, "u", [P, 4, S + 2])
        Z = p.alloc(ctx, "z", [P, 4, S + 16])
        SA, SB = p.alloc(ctx, "sa", [P, S + 16]), p.alloc(ctx, "sbb", [P, S + 16])
        tz = p.pool([base], lambda e: e.memset(U[:, :, 0:2], 0.0))
        tz2 = p.pool([base], lambda e: e.memset(Z[:, :, 0:16], 0.0))
        tz3 = p.pool([base], lambda e: e.memset(SA[:, 0:16], 0.0))
        tz4 = p.pool([base], lambda e: e.memset(SB[:, 0:16], 0.0))
        zt = [tz, tz2, tz3, tz4]
        gb, gc, u, zd = [], [], [], []
        for i in range(8):
            ch = p.take("w_in_o", i)
            for t, (b, tok) in enumerate(p.feat2(ch, 8, H, p.ht, i == 0)):
                n = 2 * (i % 2) + t
                if i < 2:
                    gb.append(p.copy_out(GB[:, n, :], b, tok, base))
                    b.done(gb[-1])
                elif i < 4:
                    gc.append(p.copy_out(GC[:, n, :], b, tok, base))
                    b.done(gc[-1])
                elif i < 6:
                    u.append(p.dve([tok, gc[n], zt], lambda e, n=n, b=b: e.tensor_tensor(U[:, n, 2:S + 2], GC[:, n, :], b.ap, ALU.mult)))
                    b.done(u[-1])
                else:
                    zd.append(p.copy_out(Z[:, n, 16:S + 16], b, tok, [zt]))
                    b.done(zd[-1])
            p.release(ch, tok)
        p.hfree = [tok]
        yt = [None] * 8
        for n in range(4):
            acc = GC[:, n, :]
            w = [p.vec("conv_w", 4 * k + n) for k in range(3)]
            t = p.dve([u[n]], lambda e, n=n, w=w, acc=acc: e.tensor_scalar(acc, U[:, n, 0:S], w[0], None, ALU.mult))
            for k in (1, 2):
                t = p.dve([t], lambda e, n=n, w=w, acc=acc, k=k: e.scalar_tensor_tensor(acc, U[:, n, k:k + S], w[k], acc, ALU.mult, ALU.add))
            t = p.dve([t, gb[n]], lambda e, n=n, acc=acc: e.tensor_tensor(acc, acc, GB[:, n, :], ALU.mult))
            yt[n] = p.parts(p.HH[:, n, :], p.HL[:, n, :], acc, [t], p.pool, p.hfree)
        ch = p.take("w_pool", 0)
        pv = []
        prev = list(zt)
        for g, wd in enumerate((2, 4, 8, 16)):
            src, t, k = Z[:, g, :], zd[g], 1
            bufs = [SA[:, :], SB[:, :]]
            while k < wd:
                dst = bufs[0]
                t = p.dve([t, prev], lambda e, dst=dst, src=src, k=k: e.tensor_tensor(
                    dst[:, 16:S + 16], src[:, 16:S + 16], src[:, 16 - k:S + 16 - k], ALU.add))
                src, bufs, k = dst, bufs[::-1], 2 * k
            q = p.tmp.get()
            t1 = p.dve([t, q.w], lambda e, q=q, src=src, wd=wd: e.tensor_scalar(q.ap, src[:, 16:S + 16], 1.0 / wd, None, ALU.mult))
            t1 = p.dve([t1, p.c2_t], lambda e, q=q, src=src, g=g: e.tensor_tensor(
                q.ap[:, 0:16], src[:, 16:32], p.c2("count")[:, g * 16:(g + 1) * 16], ALU.mult))
            prev = [t1]
            t1 = p.dve([t1], lambda e, q=q, g=g: e.tensor_tensor(q.ap, q.ap, Z[:, g, 16:S + 16], ALU.subtract))
            hi, lo = p.HH[:, 4 + g, :], p.HL[:, 4 + g, :]
            pt = p.parts(hi, lo, q.ap, [t1], p.dve, p.hfree)
            q.done(*pt)
            _, wh, wl, toks, _ = ch
            b = p.banks.get()
            tok = p.mm3([toks, pt, b.w], b.ap, wh[:, g * P:(g + 1) * P], wl[:, g * P:(g + 1) * P], hi, lo, True, True, sig=True)
            q = p.tmp.get()
            t = p.act([tok, q.w], lambda e, q=q, b=b, g=g: e.activation(q.ap, b.ap, ACT.Identity, scale=p.vec("pool_scale", g)))
            b.done(t)
            yt[4 + g] = p.parts(hi, lo, q.ap, [t], p.dve)
            q.done(*yt[4 + g])
        p.release(ch, tok)
        r = p.project_out("w_out_o", 0, 8, 256, H, yt, p.update_plain, "rms")
    p.barrier()
    return r


def cross(p, l, sums):
    H = (p.HH, p.HL)
    p.barrier()
    base = p.base
    M = 256
    with ExitStack() as ctx:
        MT = p.alloc(ctx, "mt", [P, 8, M])
        MH, ML = p.alloc(ctx, "mh", [P, 8, M], F32R), p.alloc(ctx, "ml", [P, 8, M], F32R)
        QX, KX, VX = p.alloc(ctx, "qx", [P, 4, S]), p.alloc(ctx, "kx", [P, 4, M]), p.alloc(ctx, "vx", [P, 2, S])
        tl = p.load("mem", MT[:, :, :], p.dram["memT"], base)
        st = p.held.get()
        for k in range(8):
            q = p.tmp.get()
            ts = p.act([tl, q.w], lambda e, q=q, k=k: e.activation(q.ap[:, 0:M], MT[:, k, :], ACT.Square))
            tv = p.stat(st, 0, 1, q.ap, ts, p.col1024, k == 0, k == 7, tiles=2)
            q.done(tv)
        y, t, read = p.rsqrt(st.ap[:, 0:2], 2, 1e-6, [tv])
        st.done(read)
        b, tb = p.spread(y.ap, range(2), t, tiles=2)
        y.done(tb)
        mt = []
        for k in range(8):
            g = p.vec("g_mem", l * 8 + k)
            q = p.tmp.get()
            t = p.dve([tb, tl, q.w], lambda e, k=k, g=g, q=q, b=b: e.scalar_tensor_tensor(
                q.ap[:, 0:M], MT[:, k, :], g, b.ap[:, 0:M], ALU.mult, ALU.mult))
            mt.append(p.parts(MH[:, k, :], ML[:, k, :], q.ap[:, 0:M], [t], p.pool if k % 2 else p.dve, base))
            q.done(*mt[k])
        b.done(t)
        stk = p.held.get()
        kr = []
        for c in range(2):
            ch = p.take("wkv_x", l * 4 + c)
            for t in range(2):
                n = 2 * c + t
                b, tok = p.feat(ch, 8, 256, t, (MH, ML), mt, N=M)
                kr.append(p.copy_out(KX[:, n, :], b, tok, base, src=b.ap[:, 0:M]))
                q = p.tmp.get()
                ts = p.act([tok, q.w], lambda e, q=q, b=b: e.activation(q.ap[:, 0:M], b.ap[:, 0:M], ACT.Square))
                b.done(ts)
                tvk = p.stat(stk, n, 4, q.ap, ts, p.col128, True, True, tiles=2)
                q.done(tvk)
            p.release(ch, tok)
        vx = []
        for c in range(2):
            ch = p.take("wkv_x", l * 4 + 2 + c)
            b, tok = p.toks(ch, 8, 256, [0, 1], (MH, ML), mt)
            vx.append(p.copy_out(VX[:, :, 256 * c:256 * c + 256], b, tok, base, src=b.ap.rearrange("p (a n) -> p a n", a=2)))
            b.done(vx[-1])
            p.release(ch, tok)
        y, t, read = p.rsqrt(stk.ap[:, 0:8], 8, 1e-6, [tvk])
        stk.done(read)
        kx = []
        for n in range(4):
            b, tb = p.spread(y.ap, [n, 4 + n], t, tiles=2)
            kx.append(p.dve([tb, kr[n]], lambda e, n=n, b=b: e.scalar_tensor_tensor(
                KX[:, n, :], KX[:, n, :], p.vec("gk_x", l), b.ap[:, 0:M], ALU.mult, ALU.mult)))
            b.done(kx[-1])
        y.done(tb)
        p.rms_norm("g_xattn", l, sums)
        stq = p.held.get()
        qr = []
        pend = []
        for c in range(2):
            ch = p.take("wq_x", l * 2 + c)
            for t, (b, tok) in enumerate(p.feat2(ch, 8, H, p.ht, c == 0)):
                n = 2 * c + t
                qr.append(p.copy_out(QX[:, n, :], b, tok, base))
                q = p.tmp.get()
                ts = p.act([tok, q.w], lambda e, q=q, b=b: e.activation(q.ap, b.ap, ACT.Square))
                b.done(ts)
                pend.append((n, q, ts))
            p.release(ch, tok)
        p.hfree = [tok]
        for n, q, ts in pend:
            tvq = p.stat(stq, n, 4, q.ap, ts, p.col128, True, True)
            q.done(tvq)
        y, t, read = p.rsqrt(stq.ap[:, 0:16], 16, 1e-6, [tvq])
        stq.done(read)
        sg = p.small.get()
        tg = p.dve([sg.w], lambda e: e.tensor_scalar(sg.ap[:, 0:1], p.vec("gq_x", l), 128.0 ** -0.5, None, ALU.mult))
        qx = []
        for n in range(4):
            b, tb = p.spread(y.ap, [4 * i + n for i in range(4)], t)
            qx.append(p.dve([tb, qr[n], tg], lambda e, n=n, b=b: e.scalar_tensor_tensor(
                QX[:, n, :], QX[:, n, :], sg.ap[:, 0:1], b.ap, ALU.mult, ALU.mult)))
            b.done(qx[-1])
        y.done(tb)
        sg.done(qx[-1])
        yt = [None] * 4

        def emit(n, o, to):
            yt[n] = p.parts(p.HH[:, n, :], p.HL[:, n, :], o.ap, [to], p.dve, p.hfree)
            o.done(*yt[n])

        def units():
            for h in range(4):
                cell = []

                def out(cell=cell):
                    if not cell:
                        cell.append(p.held.get())
                    return cell[0]

                for i in range(4):
                    yield p.attend(QX[:, h, i * P:(i + 1) * P], KX[:, h, :],
                                   lambda j, h=h: VX[:, j, h * P:(h + 1) * P], 0, i, M, None, [qx[h], kx[h], vx], out,
                                   lambda o, i=i: o.ap[:, i * P:(i + 1) * P], i == 0, i == 3,
                                   lambda o, to, h=h: emit(h, o, to))

        p.pipeline(units())
        r = p.project_out("wo_x", l * 2, 4, 512, H, yt, p.update_plain, "rms")
    p.barrier()
    return r


def rope_tables(p):
    q = [p.tmp.get() for _ in range(3)]
    ang, n, r = (x.ap for x in q)
    w = [x.w for x in q]
    tr = p.load("misc", p.POSI, p.dram["positions"], p.base)
    t = p.dve([tr, w], lambda e: e.tensor_copy(r[0:1, :], p.POSI))
    b = p.banks.get()
    tb = p.mm([t, b.w, p.cc_t], b.ap, p.one[0:1, :].to_broadcast([1, P]), r[0:1, :], sig=True)
    ta = p.dve([tb], lambda e: e.tensor_scalar(ang, b.ap, p.inv, None, ALU.mult))
    b.done(ta)
    toks = []
    t = ta
    for dst, shift in ((p.SIN2, 0.0), (p.COS2, 0.25)):
        t = p.dve([t], lambda e: e.tensor_scalar(n, ang, 1.0 / TWO_PI, shift, ALU.mult, ALU.add))
        t = p.dve([t], lambda e: e.tensor_scalar(n, n, MAGIC, None, ALU.add))
        t = p.dve([t], lambda e: e.tensor_scalar(n, n, -MAGIC, None, ALU.add))
        t = p.dve([t] + toks, lambda e: e.scalar_tensor_tensor(r, n, -C1, ang, ALU.mult, ALU.add))
        t = p.dve([t], lambda e: e.scalar_tensor_tensor(r, n, -C2, r, ALU.mult, ALU.add))
        t = p.dve([t], lambda e: e.scalar_tensor_tensor(r, n, -C3, r, ALU.mult, ALU.add))
        t = p.dve([t], lambda e, shift=shift: e.tensor_scalar(r, r, shift * TWO_PI, PI_LOW, ALU.add, ALU.min))
        t = p.dve([t], lambda e: e.tensor_scalar(r, r, -PI_LOW, None, ALU.max))
        ts = p.act([t, p.base], lambda e, dst=dst: e.activation(dst, r, ACT.Sin))
        toks.append(ts)
    for x in q:
        x.done(*toks)
    p.rope_t = toks
    s = p.small.get()
    lv = p.vec("lam", 0, 4)
    t = p.dve([s.w], lambda e: e.tensor_tensor(s.ap[0:64, 0:2], lv[0:64, 0:2], lv[0:64, 2:4], ALU.mult))
    b = p.banks.get()
    tb = p.mm([t, b.w], b.ap[:, 0:2], p.one[0:64, :].to_broadcast([64, P]), s.ap[0:64, 0:2], sig=True)
    t = p.act([tb], lambda e: e.activation(s.ap[:, 2:4], b.ap[:, 0:2], ACT.Exp))
    b.done(t)
    t = p.dve([t], lambda e: e.tensor_tensor(s.ap[:, 4:5], s.ap[:, 3:4], s.ap[:, 2:3], ALU.subtract))
    p.lam_t = p.dve([t], lambda e: e.tensor_scalar(p.LAM[:, 0:1], s.ap[:, 4:5], -(0.8 - 0.6), None, ALU.add))
    s.done(p.lam_t)


def whole(p):
    p.mod_t = {}
    p.vec_t = p.load("vec", p.VEC[:, :], p.dram["vecs"])
    p.cond_t = p.act([p.vec_t], lambda e: e.activation(p.COND[:, :], p.vec("c", 0, 8), ACT.Silu))
    tx = p.ada_first(8)
    p.pe([p.cc_t], lambda e: e.nop(), sig=False)
    p.dve([p.cc_t, p.vec_t], lambda e: e.nop(), sig=False)
    p.x_t = [tx] * NT
    p.fill = [(0, c) for c in range(8, 36)] + [(1, c) for c in range(36)]
    p.modulate_first()
    ffn1 = {"gate": "ffn1_w_gate", "up": "ffn1_w_up", "down": ["ffn1_down0", "ffn1_down1", "ffn1_down2"], "n_up": 11}
    ffn2 = {"gate": "ffn2_w_gate", "up": "ffn2_w_up", "down": ["ffn2_down0", "ffn2_down1", "ffn2_down2"], "n_up": 11}
    for l in range(2):
        gt = {}

        def gated(which):
            def update(n, b, tok):
                if which not in gt:
                    gt[which] = p.gate(l, which, 0.5)
                p.update_gated(n, b, tok, *gt[which])
            return update

        p.every = 2
        mean = p.ffn("swiglu", ffn1, l, FFN_GROUPS, gated(2), "ln")
        gt[2][0].done(p.x_t[7])
        p.layer_norm(l, 0, mean, (l, 3, 4))
        p.every = 1
        mean = first_mixer(p, l)
        p.every = 2
        p.layer_norm(l, 1, mean, (l, 6, 7))
        mean = p.ffn("swiglu", ffn2, l, FFN_GROUPS, gated(8), "ln")
        gt[8][0].done(p.x_t[7])
        p.layer_norm(l, 2, mean, (1, 0, 1) if l == 0 else None)
    assert not p.fill
    p.barrier()
    p.c2_t = p.load("c2", p.C[:, 1024:1024 + p.c2n], p.dram["c2"], p.base)
    rope_tables(p)
    mlp = {"up": "w_up", "down": ["down_m0", "down_m1", "down_m2", "down_m3"], "n_up": 16}
    sums = None
    for l in range(2):
        p.rms_norm("g_mix", l, sums)
        sums = even_mixer(p) if l == 0 else odd_mixer(p)
        sums = cross(p, l, sums)
        p.rms_norm("g_mlp", l, sums)
        sums = p.ffn("relu2", mlp, l, MLP_GROUPS, p.update_plain, "rms" if l == 0 else None)
    for n in range(NT):
        p.load("out", p.out[:, n, :], p.XR[:, n, :], [p.x_t[n]])
    p.sp([("out", 16 * NT)], lambda e: e.nop(), sig=False)


def build(nc, dram, out, tables):
    ctx = ExitStack()
    with ctx:
        def sb(name, shape, dt=F32):
            return ctx.enter_context(nc.sbuf_tensor("s_" + name, shape, dt))

        (cc, ccw), (c1, c1w), (c2, c2w) = tables
        mem = {"NS": 3, "NW": 2}
        mem["psum"] = [ctx.enter_context(nc.psum_tensor(f"ps{i}", [P, S], F32)) for i in range(8)]
        mem["XR"] = sb("xr", [P, NT, S])
        mem["HH"], mem["HL"] = sb("hh", [P, NT, S], F32R), sb("hl", [P, NT, S], F32R)
        mem["STAGE"] = sb("stage", [P, 3, 2048])
        mem["WH"], mem["WL"] = sb("wh", [P, 2, 2048], F32R), sb("wl", [P, 2, 2048], F32R)
        mem["TMP"] = sb("tmp", [P, 6, S])
        mem["CC"] = CC = sb("cc", [P, cc.shape[1]])
        mem["C"] = C = sb("c", [P, c1.shape[1]])
        mem["VEC"] = sb("vec", [P, NVEC])
        mem["MOD"] = sb("mod", [P, 144])
        mem["COND"] = sb("cond", [P, 8])
        mem["SM"] = sb("sm", [P, 8, 32])
        mem["NY"] = sb("ny", [P, 2, 112])
        mem["NV"], mem["NA"] = sb("nv", [P, 112]), sb("na", [P, 112])
        mem["NU"] = sb("nu", [P, 112], I32)
        mem["NG"] = mem["NU"][:, :].bitcast(F32)
        mem["LAM"] = sb("lam", [P, 1])
        for k, (at, n) in ccw.items():
            mem[k] = CC[:, at:at + n]
        mem["c1"] = lambda k: C[:, c1w[k][0]:c1w[k][0] + c1w[k][1]]
        mem["COS2"], mem["SIN2"] = C[:, 0:512], C[:, 512:1024]
        mem["c2"] = lambda k: C[:, 1024 + c2w[k][0]:1024 + c2w[k][0] + c2w[k][1]]
        mem["POSI"] = C[0:1, 4096:4608].bitcast(I32)
        mem["c2n"] = c2.shape[1]
        mem["sems"] = {k: ctx.enter_context(nc.semaphore("q_" + k)) for k in SEMS}
        dry = Prog(nc, dram, out, None, mem, "a")
        whole(dry)
        p = Prog(nc, dram, out, dry.order, mem, "b")
        whole(p)
        assert p.taken == len(p.plan)


def _tiles(w, nc_):
    k, n = w.shape
    a = w.reshape(k // P, P, n // nc_, nc_).transpose(2, 1, 0, 3)
    return a.reshape(n // nc_, P, (k // P) * nc_)


def _cols(v):
    return v.reshape(-1, P).T


def kernel(**inputs):
    import concourse.bacc as _bacc
    from concourse import mybir as _mybir
    from concourse.bass_utils import run_bass_kernel_spmd as _run

    a = {k: np.asarray(v) for k, v in inputs.items()}
    arr = {}

    def put(name, parts):
        arr[name] = np.ascontiguousarray(np.concatenate(parts, 0))

    put("w_ada", [_tiles(a["w_ada"][l], 256) for l in range(2)])
    for f in ("ffn1", "ffn2"):
        for g in ("gate", "up"):
            put(f"{f}_w_{g}", [_tiles(a[f"{f}_w_{g}"][l], 256) for l in range(2)])
        for gi, (g0, G) in enumerate(FFN_GROUPS):
            put(f"{f}_down{gi}", [_tiles(a[f"{f}_w_down"][l][g0 * P:(g0 + G) * P], 256) for l in range(2)])
    put("w_in", [_tiles(a["w_in"][l], 256) for l in range(2)])
    put("w_out", [_tiles(a["w_out"][l], 256) for l in range(2)])
    e = a["w_in_e_2"][0]
    order = [e[:, 0:1024], e[:, 1536:2048], e[:, 2048:2560], e[:, 1024:1536]]
    put("w_in_e", [_tiles(w, 256) for w in order])
    ki, wi = e[:, 2560:2624], e[:, 2624:2628]
    put("w_kiwi", [_tiles(np.concatenate([ki, ki, wi], 1), 132)])
    put("w_kv_up", [_tiles(a["w_kv_up_b_2"][0], 1024)])
    put("w_out_e", [_tiles(a["w_out_e_2"][0], 256)])
    put("w_in_o", [_tiles(a["w_in_o_2"][0], 256)])
    put("w_pool", [a["w_pool_2"][0].transpose(1, 0, 2).reshape(1, P, 512)])
    put("w_out_o", [_tiles(a["w_out_o_2"][0], 256)])
    put("wq_x", [_tiles(a["wq_x_2"][l], 256) for l in range(2)])
    put("wkv_x", [_tiles(a["wkv_x_2"][l], 256) for l in range(2)])
    put("wo_x", [_tiles(a["wo_x_2"][l], 512) for l in range(2)])
    put("w_up", [_tiles(a["w_up_2"][l], 256) for l in range(2)])
    for gi, (g0, G) in enumerate(MLP_GROUPS):
        put(f"down_m{gi}", [_tiles(a["w_down_2"][l][g0 * P:(g0 + G) * P], 256) for l in range(2)])
    arr["xT"] = np.ascontiguousarray(a["x"][0].T.reshape(NT, P, S).transpose(1, 0, 2))
    arr["memT"] = np.ascontiguousarray(a["mem_2"][0].T.reshape(8, P, 256).transpose(1, 0, 2))
    arr["positions"] = np.ascontiguousarray(a["positions_2"])
    two = lambda v: np.concatenate([v, v])[:, None]
    lam = np.zeros((P, 4), np.float32)
    for i, n in enumerate(("lam_q1_2", "lam_q2_2", "lam_k1_2", "lam_k2_2")):
        lam[0:64, i] = a[n][0]
    arr["vecs"] = np.ascontiguousarray(np.concatenate([
        _cols(a["c"][0]), _cols(a["b_ada"].reshape(-1)), _cols(a["ln_gain"].reshape(-1)),
        _cols(a["ln_bias"].reshape(-1)), _cols(a["g_mix_2"].reshape(-1)), _cols(a["g_xattn_2"].reshape(-1)),
        _cols(a["g_mem_2"].reshape(-1)), _cols(a["g_mlp_2"].reshape(-1)), _cols(a["gq_x_2"].reshape(-1)),
        _cols(a["gk_x_2"].reshape(-1)), two(a["gq_a_2"][0]), two(a["gk_a_2"][0]), two(a["gq_b_2"][0]),
        two(a["gk_b_2"][0]), two(a["g_kidx_2"][0]), _cols(a["g_sub_a_2"].reshape(-1)),
        _cols(a["g_kv_b_2"].reshape(-1)), _cols(a["conv_w_2"].reshape(-1)),
        _cols(a["pool_scale_2"].reshape(-1)), lam], 1))
    tables = consts()
    arr["cc"], arr["c1"], arr["c2"] = (t[0] for t in tables)

    nc = _bacc.Bacc("TRN2", target_bir_lowering=False, num_devices=1)
    dram = {}
    for name, v in arr.items():
        dram[name] = nc.dram_tensor(f"in_{name}", v.shape, _mybir.dt.from_np(v.dtype), kind="ExternalInput").ap()
    out = nc.dram_tensor("out_0", (P, NT, S), F32, kind="ExternalOutput").ap()
    build(nc, dram, out, tables)
    r = _run(nc, [{f"in_{k}": v for k, v in arr.items()}], core_ids=[0])
    got = r.results[0]["out_0"]
    return np.ascontiguousarray(got.transpose(1, 0, 2).reshape(D, S).T).reshape(1, S, D)
```

```python
from contextlib import ExitStack

import numpy as np

import concourse.bass as bass
from concourse import mybir

F32 = mybir.dt.float32
F32R = mybir.dt.float32r
I32 = mybir.dt.int32
ALU = mybir.AluOpType
ACT = mybir.ActivationFunctionType
AXX = mybir.AxisListType.X

P = 128
S = 512
D = 1024
NT = D // P
ALPHA = 4.0 ** 0.25
NEG = -1e30
TAKEN = -3e38
MAGIC = 12582912.0
TWO_PI = 6.283185307179586
C1 = 6.28125
C2 = float(np.float32(TWO_PI - C1))
C3 = float(np.float32(TWO_PI - C1 - C2))
PI_LOW = float(np.nextafter(np.float32(np.pi), np.float32(0)))
FFN_GROUPS = [(0, 8), (8, 8), (16, 6)]
ODD_ORDER = (4, 5, 0, 6, 1, 7, 2, 3)
MLP_GROUPS = [(0, 8), (8, 8), (16, 8), (24, 8)]

VEC = {}


def _vec_layout():
    at = 0
    for name, n in (("c", 8), ("b_ada", 144), ("ln_gain", 48), ("ln_bias", 48), ("g_mix", 16),
                    ("g_xattn", 16), ("g_mem", 16), ("g_mlp", 16), ("gq_x", 2), ("gk_x", 2),
                    ("gq_a", 1), ("gk_a", 1), ("gq_b", 1), ("gk_b", 1), ("g_kidx", 1),
                    ("g_sub_a", 1), ("g_kv_b", 2), ("conv_w", 12), ("pool_scale", 4),
                    ("lam", 4)):
        VEC[name] = (at, n)
        at += n
    return at


NVEC = _vec_layout()
SEMS = ["pe", "act", "dve", "pool", "st0", "st1", "st2", "cc", "vec", "x", "c1", "c2", "a0", "a1", "a2", "a3", "a4", "a5", "a6", "a7", "misc", "mem", "out"]


def flat(ws):
    for w in ws:
        if w is None:
            continue
        if isinstance(w, list):
            yield from flat(w)
        else:
            yield w


class Queue:

    def __init__(self, key, eng, sems):
        self.key, self.eng, self.sems = key, eng, sems
        self.n, self.seen = 0, {}

    def __call__(self, waits, fn, sig=True, sem=None):
        need = []
        for k, v in flat(waits):
            if self.seen.get(k, 0) < v:
                self.seen[k] = v
                need = [x for x in need if x[0] != k] + [(k, v)]
        if sig and sem is None:
            self.n += 1
        if self.eng is not None:
            for k, v in need:
                self.eng.wait_ge(self.sems[k], v)
            ins = fn(self.eng)
            if sem is not None:
                ins.then_inc(self.sems[sem], 16)
            elif sig:
                ins.then_inc(self.sems[self.key], 1)
        return (self.key, self.n)


class Slot:

    def __init__(self, ap):
        self.ap, self.w, self.busy = ap, [], False

    def done(self, *tokens):
        self.w = list(tokens)
        self.busy = False


class Ring:
    def __init__(self, aps):
        self.slots, self.i = [Slot(a) for a in aps], 0

    def free(self):
        return sum(not s.busy for s in self.slots)

    def get(self, first=None):
        for _ in self.slots:
            i = self.i % len(self.slots)
            s = self.slots[i]
            self.i += 1
            if not s.busy and i < (first or len(self.slots)):
                break
        assert not s.busy
        s.busy = True
        return s


class Prog:
    def __init__(self, nc, dram, out, plan, mem, tag):
        self.nc, self.dram, self.out, self.plan, self.tag = nc, dram, out, plan, tag
        live = plan is not None
        sems = mem["sems"]
        self.pe = Queue("pe", nc.tensor if live else None, sems)
        self.act = Queue("act", nc.scalar if live else None, sems)
        self.dve = Queue("dve", nc.vector if live else None, sems)
        self.pool = Queue("pool", nc.gpsimd if live else None, sems)
        self.sp = Queue("sp", nc.sync if live else None, sems)
        self.psum = mem["psum"]
        self.XR = mem["XR"]
        self.HH = mem["HH"]
        self.HL = mem["HL"]
        self.STAGE = mem["STAGE"]
        self.WH = mem["WH"]
        self.WL = mem["WL"]
        self.TMP = mem["TMP"]
        self.CC = mem["CC"]
        self.C = mem["C"]
        self.VEC = mem["VEC"]
        self.MOD = mem["MOD"]
        self.COND = mem["COND"]
        self.SM = mem["SM"]
        self.NY = mem["NY"]
        self.NV = mem["NV"]
        self.NA = mem["NA"]
        self.NU = mem["NU"]
        self.NG = mem["NG"]
        self.LAM = mem["LAM"]
        self.POSI = mem["POSI"]
        self.COS2 = mem["COS2"]
        self.SIN2 = mem["SIN2"]
        self.c1 = mem["c1"]
        self.c2 = mem["c2"]
        self.c2n = mem["c2n"]
        self.NS = mem["NS"]
        self.NW = mem["NW"]
        self.ident = mem["ident"]
        self.one = mem["one"]
        self.later = mem["later"]
        self.perm1 = mem["perm1"]
        self.perm2 = mem["perm2"]
        self.causal = mem["causal"]
        self.strict = mem["strict"]
        self.blk = mem["blk"]
        self.col1024 = mem["col1024"]
        self.col256 = mem["col256"]
        self.col128 = mem["col128"]
        self.inv = mem["inv"]
        self.nalloc = 0
        self.order = []
        self.banks = Ring([b[:, :] for b in self.psum[0:6]])
        self.held = Ring([b[:, :] for b in self.psum[6:8]])
        self.tmp = Ring([self.TMP[:, i, :] for i in range(self.TMP.shape[1])])
        self.small = Ring([self.SM[:, i, :] for i in range(self.SM.shape[1])])
        self.newt = Slot(None)
        self.yr = Ring([self.NY[:, i, :] for i in range(2)])
        self.ndma = {}
        self.taken = 0
        self.nload = 0
        self.nsplit = 0
        self.stage_w = {}
        self.landed = {}
        self.split_of = {}
        self.wslot = [[], []]
        self.nw = 0
        self.base = []
        self.fill = []
        self.hfree = []
        self.ada_acc, self.ada_sum = None, None
        self.every, self.since, self.age = 0, 0, 0
        self.bg, self.active, self.depth, self.spare = [], [], 6, 0
        self.pace, self.rest, self.burst = 1, 0, 1

    def alloc(self, ctx, name, shape, dt=F32):
        self.nalloc += 1
        return ctx.enter_context(self.nc.sbuf_tensor(f"{name}_{self.tag}{self.nalloc}", shape, dt))

    def more_tmp(self, ctx, n):
        t = self.alloc(ctx, "xt", [P, n, S])
        new = [Slot(t[:, i, :]) for i in range(n)]
        for x in new:
            x.w = self.base
        self.tmp.slots.extend(new)
        return new

    def less_tmp(self, new):
        assert not any(x.busy for x in new)
        self.tmp.slots = [x for x in self.tmp.slots if x not in new]

    def barrier(self):
        self.base = [(q.key, q.n) for q in (self.pe, self.act, self.dve, self.pool) if q.n]

    def load(self, key, dst, src, waits=()):
        n = self.ndma.get(key, 0) + 1
        self.ndma[key] = n
        self.sp(list(waits), lambda e: e.dma_start(dst, src), sem=key)
        return (key, 16 * n)

    def issue(self, j):
        if j >= len(self.plan):
            return
        name, idx, raw = self.plan[j]
        src = self.dram[name][idx]
        n = src.shape[-1]
        slot = j % self.NS
        self.landed[j] = self.load(f"st{slot}", self.STAGE[:, slot, 0:n], src,
                                   self.stage_w.get(j - self.NS, []))

    def ahead(self):
        if self.plan is not None:
            i = self.taken + 1
            if self.taken < self.nsplit <= i < len(self.plan) and not self.plan[i][2] and i in self.landed:
                self.split(i, 1.0)
                self.nsplit = i + 1

    def split(self, j, share=0.5):
        name, idx, raw = self.plan[j]
        n = self.dram[name][idx].shape[-1]
        slot, ws = j % self.NS, self.nw % self.NW
        self.nw += 1
        src, wh, wl = self.STAGE[:, slot, 0:n], self.WH[:, ws, 0:n], self.WL[:, ws, 0:n]
        free = self.wslot[ws]
        th = self.act([self.landed[j], free], lambda e: e.activation(wh, src, ACT.Copy))
        cut = int(n * share)
        t1 = self.pool([self.landed[j], th, free], lambda e: e.tensor_tensor(
            wl[:, 0:cut], src[:, 0:cut], wh[:, 0:cut].bitcast(F32), ALU.subtract))
        t2 = t1 if cut == n else self.dve([self.landed[j], th, free], lambda e: e.tensor_tensor(
            wl[:, cut:n], src[:, cut:n], wh[:, cut:n].bitcast(F32), ALU.subtract))
        self.stage_w[j] = [t1, t2]
        self.split_of[j] = (wh, wl, [th, t1, t2], ws)
        self.issue(j + self.NS)

    def take(self, name, idx, raw=False):
        j = self.taken
        self.taken += 1
        self.order.append((name, idx, raw))
        if self.plan is None:
            a = self.WH[:, 0, :]
            if raw:
                return j, self.STAGE[:, 0, :], [], 0
            self.ada_step()
            return j, a, a, [], 0
        assert self.plan[j] == (name, idx, raw)
        if raw:
            return j, self.STAGE[:, j % self.NS, :], self.landed[j], 0
        done = 0
        for i in range(j, len(self.plan)):
            if i > j:
                done += 1
            if done > self.NW - 1 or i >= j + self.NS:
                break
            if self.plan[i][2]:
                if i > j:
                    done -= 1
                continue
            if i > j and (i not in self.landed):
                break
            if i >= self.nsplit:
                self.split(i)
                self.nsplit = i + 1
        wh, wl, toks, ws = self.split_of[j]
        self.ada_step()
        return j, wh, wl, toks, ws

    def release(self, ch, token):
        self.age += 1
        if self.age == 2:
            self.ada_flush()
        if self.plan is not None:
            self.wslot[ch[-1]] = [token]

    def release_raw(self, ch, token):
        if self.plan is not None:
            self.stage_w[ch[0]] = [token]
            self.issue(ch[0] + self.NS)

    def mm(self, waits, out, lhsT, rhs, start=True, stop=True, sig=False):
        return self.pe(waits, lambda e: e.matmul(out, lhsT, rhs, start=start, stop=stop,
                                                 skip_group_check=True), sig=sig)

    def mm3(self, waits, out, ah, al, bh, bl, start, stop, sig=False):
        self.mm(waits, out, ah, bh, start, False)
        self.mm([], out, ah, bl, False, False)
        return self.mm([], out, al, bh, False, stop, sig)

    def feat(self, ch, kt, nc_, t, X, xt, N=S, M=P, off=None):
        _, wh, wl, toks, _ = ch
        whv = wh[:, 0:kt * nc_].rearrange("p (k n) -> p k n", k=kt)
        wlv = wl[:, 0:kt * nc_].rearrange("p (k n) -> p k n", k=kt)
        a = t * P if off is None else off
        b = self.banks.get()
        for k in range(kt):
            tok = self.mm3([toks, xt[k], b.w], b.ap[0:M, 0:N], whv[:, k, a:a + M], wlv[:, k, a:a + M],
                           X[0][:, k, 0:N], X[1][:, k, 0:N], k == 0, k == kt - 1, sig=(k == kt - 1))
            if k % 4 == 3:
                self.tick()
        return b, tok

    def feat2(self, ch, kt, X, xt, eager=False, N=S, order=None):
        if not eager:
            for t in range(2):
                yield self.feat(ch, kt, 256, t, X, xt, N)
            return
        _, wh, wl, toks, _ = ch
        whv = wh[:, 0:kt * 256].rearrange("p (k n) -> p k n", k=kt)
        wlv = wl[:, 0:kt * 256].rearrange("p (k n) -> p k n", k=kt)
        bs = [self.banks.get(), self.banks.get()]
        tok = [None, None]
        for i, k in enumerate(order or range(kt)):
            for t in range(2):
                tok[t] = self.mm3([toks, xt[k], bs[t].w], bs[t].ap[:, 0:N], whv[:, k, t * P:(t + 1) * P],
                                  wlv[:, k, t * P:(t + 1) * P], X[0][:, k, 0:N], X[1][:, k, 0:N],
                                  i == 0, i == kt - 1, sig=(i == kt - 1))
            if i % 2 == 1:
                self.tick()
        yield bs[0], tok[0]
        yield bs[1], tok[1]

    def toks(self, ch, kt, nc_, tiles, X, xt, cols=None, n=None, view=None):
        _, wh, wl, toks, _ = ch
        whv = wh[:, 0:kt * nc_].rearrange("p (k n) -> p k n", k=kt)
        wlv = wl[:, 0:kt * nc_].rearrange("p (k n) -> p k n", k=kt)
        c0, n = (0, nc_) if cols is None else cols
        b = self.banks.get()
        for q, i in enumerate(tiles):
            for k in range(kt):
                tok = self.mm3([toks, xt[k], b.w], b.ap[:, q * n:(q + 1) * n],
                               X[0][:, k, i * P:(i + 1) * P], X[1][:, k, i * P:(i + 1) * P],
                               whv[:, k, c0:c0 + n], wlv[:, k, c0:c0 + n],
                               k == 0, k == kt - 1, sig=(k == kt - 1 and i == tiles[-1]))
            if n == 256:
                self.tick()
        return b, tok

    def parts(self, hi, lo, src, waits, lo_on=None, free=()):
        th = self.act([waits, list(free)], lambda e: e.activation(hi, src, ACT.Copy))
        q = lo_on or self.pool
        tl = q([waits, th, list(free)], lambda e: e.tensor_tensor(lo, src, hi.bitcast(F32), ALU.subtract))
        return [th, tl]

    def stat(self, b, col, step, src, tok, rhs, start, stop, n=1, tiles=4):
        for i in range(tiles):
            t = self.mm([tok, b.w], b.ap[:, i * step + col:i * step + col + n], src[:, i * P:(i + 1) * P],
                        rhs, start if i == 0 else False, stop, sig=(i == tiles - 1))
        return t

    def rsqrt(self, src, n, eps, waits):
        y = self.yr.get()
        d, v, u, a, g, yy = self.dve, self.NV[:, 0:n], self.NU[:, 0:n], self.NA[:, 0:n], self.NG[:, 0:n], y.ap[:, 0:n]
        t = d([waits, (d.key, d.n)], lambda e: e.tensor_scalar(v, src, eps, None, ALU.add))
        read = t
        t = d([t], lambda e: e.tensor_scalar(u, v.bitcast(I32), 1, None, ALU.logical_shift_right))
        t = d([t, y.w], lambda e: e.tensor_scalar(yy.bitcast(I32), u, -1.0, float(0x5F3759DF), ALU.mult, ALU.add))
        for _ in range(3):
            t = d([t], lambda e: e.tensor_tensor(a, yy, yy, ALU.mult))
            t = d([t], lambda e: e.scalar_tensor_tensor(g, a, -0.5, v, ALU.mult, ALU.mult))
            t = d([t], lambda e: e.scalar_tensor_tensor(yy, g, 1.5, yy, ALU.add, ALU.mult))
        return y, t, read

    def spread(self, y, cols, tok, ring=None, tiles=4):
        b = (ring or self.banks).get()
        for i in range(tiles):
            c = cols[i]
            t = self.mm([tok, b.w], b.ap[:, i * P:(i + 1) * P], y[:, c:c + 1].to_broadcast([P, P]),
                        self.ident, sig=(i == tiles - 1))
        return b, t

    def ada(self):
        if not self.fill:
            return
        l, c = self.fill.pop(0)
        ch = self.take("w_ada", l * 36 + c, raw=True)
        w = ch[1].rearrange("p (k n) -> p k n", k=8)
        if self.ada_acc is None:
            self.ada_acc = self.tmp.get()
        acc = self.ada_acc
        ts, last = self.ada_rows(w, c, acc, ch[2])
        self.release_raw(ch, last)
        if c % 2 == 0:
            return
        self.ada_acc = None
        self.ada_sum, self.age = lambda: self.ada_mod(l, c, acc, ts), 0

    def ada_flush(self):
        if self.ada_sum:
            self.ada_sum()
        self.ada_sum = None

    def ada_rows(self, w, c, acc, loaded):
        q = self.tmp.get()
        a0, a1 = acc.ap[:, (c % 2) * 256:(c % 2) * 256 + 256], q.ap[:, 0:256]
        t = [None, None]
        for k in range(8):
            dst, cond = (a0, a1)[k % 2], self.COND[:, k:k + 1]
            if k < 2:
                t[k] = self.dve([loaded, self.cond_t, acc.w, q.w], lambda e: e.tensor_scalar(
                    dst, w[:, k, :], cond, None, ALU.mult))
            else:
                t[k % 2] = self.dve([t[k % 2]], lambda e: e.scalar_tensor_tensor(
                    dst, w[:, k, :], cond, dst, ALU.mult, ALU.add))
        ts = self.dve(t, lambda e: e.tensor_tensor(a0, a0, a1, ALU.add))
        q.done(ts)
        return ts, t[1]

    def ada_step(self):
        self.since += 1
        if self.every and self.since >= self.every:
            self.since = 0
            self.ada()

    def ada_mod(self, l, c, acc, ts):
        b = self.banks.get()
        for j in range(4):
            tok = self.mm([ts, b.w, self.cc_t], b.ap[:, j:j + 1], acc.ap[:, j * P:(j + 1) * P], self.one, sig=(j == 3))
        acc.done(tok)
        self.add_bias(l, c - 1, 2, b, tok)

    def add_bias(self, l, c, n, b, tok):
        at = l * 72 + 2 * c
        dst, bias = self.MOD[:, at:at + 2 * n], self.vec("b_ada", at, 2 * n)
        tm = self.dve([tok, self.vec_t], lambda e: e.tensor_tensor(dst, b.ap[:, 0:2 * n], bias, ALU.add))
        b.done(tm)
        for i in range(n):
            self.mod_t[l, c + i] = tm

    def ada_first(self, n):
        with ExitStack() as ctx:
            W = self.alloc(ctx, "wa", [P, n, 2048])
            tl = {}
            for c in (0, 2, 1, 3, 4, 6, 5, 7):
                tl[c] = self.load(f"a{c}", W[:, c, :], self.dram["w_ada"][c])
                if c == 3:
                    self.cc_t = self.load("cc", self.CC[:, :], self.dram["cc"])
            tx = self.load("x", self.XR[:, :, :], self.dram["xT"])
            self.begin()
            self.c1_t = self.load("c1", self.C[:, :], self.dram["c1"])
            rows = []
            for c in (2, 3, 6, 7):
                if c % 2 == 0:
                    acc = self.tmp.get()
                ts = self.ada_rows(W[:, c, :].rearrange("p (k n) -> p k n", k=8), c, acc, tl[c])[0]
                if c % 2:
                    rows.append((c, acc, ts))
            for c in (0, 1, 4, 5):
                b = self.banks.get()
                for j in range(2):
                    for k in range(8):
                        tok = self.mm([tl[c], self.cond_t, b.w], b.ap[:, j:j + 1],
                                      W[:, c, k * 256 + j * P:k * 256 + j * P + P], self.COND[:, k:k + 1],
                                      k == 0, k == 7, sig=(j == 1 and k == 7))
                self.add_bias(0, c, 1, b, tok)
            for c, acc, ts in rows:
                self.ada_mod(0, c, acc, ts)
            if self.plan:
                self.split(0)
                self.nsplit = 1
        return tx

    def begin(self):
        for i in range(self.NS if self.plan else 0):
            self.issue(i)

    def vec(self, name, i=0, n=1):
        at = VEC[name][0] + i
        return self.VEC[:, at:at + n]

    def mod(self, l, which):
        if (l, which * 4 + 3) not in self.mod_t:
            self.ada_flush()
        return (self.MOD[:, l * 72 + which * 8:l * 72 + which * 8 + 8],
                [self.mod_t[l, which * 4 + c] for c in range(4)])

    def modulate_first(self):
        sc, tsc = self.mod(0, 1)
        sh, tsh = self.mod(0, 0)
        s = self.small.get()
        t = self.dve([tsc, tsh, s.w], lambda e: e.tensor_scalar(s.ap[:, 0:8], sc, 1.0, None, ALU.add))
        self.ht = self.to_h(lambda n: [t, tsh, self.x_t[n]], s.ap, sh)
        for n in range(NT):
            x = self.XR[:, n, :]
            self.x_t[n] = self.act([self.ht[n]], lambda e: e.activation(x, x, ACT.Copy, scale=ALPHA))
        s.done(*flat(self.ht))

    def to_h(self, before, a, b):
        ht, prev = [], None
        for n in range(NT + 1):
            if n < NT:
                x, hi, q = self.XR[:, n, :], self.HH[:, n, :], self.tmp.get()
                w, an, bn = before(n), a[:, n:n + 1], b[:, n:n + 1]
                t1 = self.dve([w, self.hfree], lambda e: e.tensor_scalar(hi, x, an, bn, ALU.mult, ALU.add))
                t2 = self.act([w, q.w], lambda e: e.activation(q.ap, x, ACT.Identity, bias=bn, scale=an))
            if prev:
                m, qm, tm = prev
                him, lom = self.HH[:, m, :], self.HL[:, m, :]
                t3 = (self.pool, self.dve)[m % 2]([tm, self.hfree], lambda e: e.tensor_tensor(
                    lom, qm.ap, him.bitcast(F32), ALU.subtract))
                qm.done(t3)
                ht.append([*tm, t3])
            prev = (n, q, [t1, t2])
        return ht

    def gate(self, l, which, w):
        g, tg = self.mod(l, which)
        s = self.small.get()
        t = self.dve([tg, s.w], lambda e: e.tensor_scalar(s.ap[:, 0:8], g, w, w, ALU.mult, ALU.add))
        return s, t

    def update_gated(self, n, b, tok, s, ts):
        x, c = self.XR[:, n, :], s.ap[:, n:n + 1]
        t = self.dve([tok, ts, self.x_t[n]], lambda e: e.scalar_tensor_tensor(x, b.ap, c, x, ALU.mult, ALU.add))
        b.done(t)
        self.x_t[n] = t

    def update_plain(self, n, b, tok):
        x = self.XR[:, n, :]
        t = self.dve([tok, self.x_t[n]], lambda e: e.tensor_tensor(x, b.ap, x, ALU.add))
        b.done(t)
        self.x_t[n] = t

    def layer_norm(self, l, idx, mean, nxt):
        gain, beta = self.vec("ln_gain", l * 24 + idx * 8, 8), self.vec("ln_bias", l * 24 + idx * 8, 8)
        s = self.small.get()
        A, B, AG, AB = (s.ap[:, 8 * i:8 * i + 8] for i in range(4))
        if nxt is not None:
            sc, tsc = self.mod(nxt[0], nxt[2])
            sh, tsh = self.mod(nxt[0], nxt[1])
            t = self.dve([tsc, s.w, self.vec_t], lambda e: e.tensor_scalar(AG, sc, 1.0, None, ALU.add))
            ta = self.dve([t], lambda e: e.tensor_tensor(A, gain, AG, ALU.mult))
            tb = self.dve([t], lambda e: e.tensor_tensor(AB, beta, AG, ALU.mult))
            tb = self.dve([tb, tsh], lambda e: e.tensor_tensor(B, AB, sh, ALU.add))
            t1 = self.dve([ta, tb], lambda e: e.tensor_scalar(AG, gain, ALPHA, None, ALU.mult))
            t2 = self.dve([tb], lambda e: e.tensor_scalar(AB, beta, ALPHA, None, ALU.mult))
            small = [ta, tb, t1, t2]
        acc, ta = mean.w
        b = self.banks.get()
        tb_ = self.mm([ta, b.w], b.ap, self.col1024.to_broadcast([P, P]), acc.ap, sig=True)
        acc.done(tb_)
        rd, sq = [], []
        for n in range(NT):
            x = self.XR[:, n, :]
            td = self.dve([tb_, self.x_t[n]], lambda e: e.tensor_tensor(x, x, b.ap, ALU.subtract))
            if n == NT - 1:
                b.done(td)
            if n >= 6:
                self.fold(self.dve, sq, n - 1)
            q = self.tmp.get()
            ts = self.act([td, q.w], lambda e: e.activation(q.ap, x, ACT.Square))
            rd.append([td, ts])
            sq.append([q, ts])
            if n in (1, 3):
                self.fold(self.pool, sq, n)
        self.fold(self.dve, sq, 7)
        var = self.held.get()
        for i, n in enumerate((1, 3, 7)):
            q, ts = sq[n]
            tv = self.stat(var, 0, 1, q.ap, ts, self.col1024, i == 0, i == 2)
            q.done(tv)
        self.ahead()
        y, t, read = self.rsqrt(var.ap[:, 0:4], 4, 1e-5, [tv])
        var.done(read)
        b, tb_ = self.spread(y.ap, range(4), t)
        y.done(tb_)
        last = []

        def scaled(n):
            x = self.XR[:, n, :]
            t = self.dve([tb_, rd[n]], lambda e: e.tensor_tensor(x, x, b.ap, ALU.mult))
            b.done(t)
            return [t, small] if nxt is not None else t

        if nxt is not None:
            self.ht = self.to_h(scaled, A, B)
        else:
            sq = []
            for n in range(NT):
                x, g, c, q = self.XR[:, n, :], gain[:, n:n + 1], beta[:, n:n + 1], self.tmp.get()
                t = self.dve([tb_, rd[n]], lambda e: e.scalar_tensor_tensor(x, x, g, b.ap, ALU.mult, ALU.mult))
                if n == NT - 1:
                    b.done(t)
                if n >= 6:
                    self.fold(self.dve, sq, n - 1)
                sq.append([q, self.act([t, q.w], lambda e: e.activation(q.ap, x, ACT.Square, bias=c))])
                if 1 <= n <= 3:
                    self.fold(self.pool, sq, n)
            self.fold(self.dve, sq, 7)
            self.fold(self.dve, [sq[3], sq[7]], 1)
            for n in range(NT):
                x, c = self.XR[:, n, :], beta[:, n:n + 1]
                self.x_t[n] = self.act([sq[n][1]], lambda e: e.activation(x, x, ACT.Identity, bias=c))
                last.append(self.x_t[n])
            s.done()
            sums = Slot(None)
            sums.w = sq[7]
            return sums
        if nxt is not None:
            for n in range(NT):
                x, g, c = self.XR[:, n, :], AG[:, n:n + 1], AB[:, n:n + 1]
                self.x_t[n] = self.act([self.ht[n], small], lambda e: e.activation(x, x, ACT.Identity, bias=c, scale=g))
                last.append(self.x_t[n])
        s.done(*last)

    def square_of(self, stats, tiles):
        tv = None
        for n in tiles:
            x, q = self.XR[:, n, :], self.tmp.get()
            ts = self.act([self.x_t[n], q.w], lambda e: e.activation(q.ap, x, ACT.Square))
            tv = self.stat(stats, 0, 1, q.ap, ts, self.col1024, n == 0, n == NT - 1)
            q.done(tv)
        return tv

    def fold(self, eng, sq, n):
        (q, t), (r, u) = sq[n], sq[n - 1]
        sq[n][1] = eng([t, u], lambda e: e.tensor_tensor(q.ap, q.ap, r.ap, ALU.add))
        r.done(sq[n][1])

    def rms_norm(self, name, l, sums=None, meanwhile=None):
        if sums is None:
            sums = Slot(None)
            self.square_of(sums, range(NT))
        acc, ta = sums.w
        st = self.held.get()
        tv = self.stat(st, 0, 1, acc.ap, ta, self.col1024, True, True)
        acc.done(tv)
        if not meanwhile:
            self.ahead()
        y, t, read = self.rsqrt(st.ap[:, 0:4], 4, 1e-6, [tv])
        st.done(read)
        if meanwhile:
            meanwhile[0]()
        b, tb = self.spread(y.ap, range(4), t)
        y.done(tb)
        self.ht = []
        for n in range(NT):
            x, g, q = self.XR[:, n, :], self.vec(name, l * 8 + n), self.tmp.get()
            t = self.dve([tb, q.w, self.x_t[n], self.vec_t], lambda e: e.scalar_tensor_tensor(q.ap, x, g, b.ap, ALU.mult, ALU.mult))
            self.ht.append(self.parts(self.HH[:, n, :], self.HL[:, n, :], q.ap, [t],
                                      self.dve if n % 2 else self.pool, self.hfree))
            q.done(*self.ht[n])
        b.done(t)
        if meanwhile:
            meanwhile[1]()

    def ffn(self, kind, names, l, groups, update, mean):
        H = (self.HH, self.HL)
        self.barrier()
        base = self.base
        sums = Slot(None)
        with ExitStack() as ctx:
            A = [(self.alloc(ctx, "ah", [P, 8, S], F32R), self.alloc(ctx, "al", [P, 8, S], F32R)) for _ in range(2)]
            afree = [base, base]
            up_n = names["n_up"]
            for gi, (g0, G) in enumerate(groups):
                AH, AL = A[gi % 2]
                at = []
                for m in range(G // 2):
                    idx = l * up_n + g0 // 2 + m
                    if kind == "swiglu":
                        ch = self.take(names["gate"], idx)
                        sl = []
                        for b, tok in self.feat2(ch, 8, H, self.ht, gi == 0 and m == 0):
                            q = self.tmp.get()
                            ts = self.act([tok, q.w], lambda e, q=q, b=b: e.activation(q.ap, b.ap, ACT.Silu))
                            b.done(ts)
                            sl.append((q, ts))
                        self.release(ch, tok)
                        ch = self.take(names["up"], idx)
                        for t in range(2):
                            b, tok = self.feat(ch, 8, 256, t, H, self.ht)
                            q, ts = sl[t]
                            ta = self.dve([tok, ts], lambda e, q=q, b=b: e.tensor_tensor(q.ap, q.ap, b.ap, ALU.mult))
                            b.done(ta)
                            k = 2 * m + t
                            at.append(self.parts(AH[:, k, :], AL[:, k, :], q.ap, [ta], free=afree[gi % 2]))
                            q.done(*at[k])
                        self.release(ch, tok)
                    else:
                        ch = self.take(names["up"], idx)
                        for t, (b, tok) in enumerate(self.feat2(ch, 8, H, self.ht, gi == 0 and m == 0)):
                            q = self.tmp.get()
                            ts = self.act([tok, q.w], lambda e, q=q, b=b: e.activation(q.ap, b.ap, ACT.Relu))
                            b.done(ts)
                            ta = self.dve([ts], lambda e, q=q: e.tensor_tensor(q.ap, q.ap, q.ap, ALU.mult))
                            k = 2 * m + t
                            at.append(self.parts(AH[:, k, :], AL[:, k, :], q.ap, [ta], free=afree[gi % 2]))
                            q.done(*at[k])
                        self.release(ch, tok)
                if gi == len(groups) - 1:
                    self.hfree = [tok]
                final = gi == len(groups) - 1 and mean
                done = []
                for c in range(4):
                    ch = self.take(names["down"][gi], l * 4 + c)
                    for t in range(2):
                        b, tok = self.feat(ch, G, 256, t, (AH, AL), at)
                        update(2 * c + t, b, tok)
                        done.append(2 * c + t)
                    self.release(ch, tok)
                    afree[gi % 2] = [tok]
                    if final:
                        f = self.mean_of if mean == "ln" else self.square_of
                        f(sums, done[:-2] if c < 3 else done)
                        done = done[-2:] if c < 3 else []
        self.barrier()
        return sums

    def mean_of(self, sums, tiles):
        for n in tiles:
            x = self.XR[:, n, :]
            if n == 0:
                sums.w = [self.tmp.get(6)]
            elif n == 1:
                a = sums.w[0]
                sums.w.append(self.pool([self.x_t[0], self.x_t[1], a.w], lambda e: e.tensor_tensor(
                    a.ap, self.XR[:, 0, :], x, ALU.add)))
            else:
                a, t = sums.w
                q = self.dve if n == NT - 1 else self.pool
                sums.w[1] = q([self.x_t[n], t], lambda e: e.tensor_tensor(a.ap, a.ap, x, ALU.add))

    def square_of(self, sums, tiles):
        for n in tiles:
            x, q = self.XR[:, n, :], self.tmp.get()
            ts = self.act([self.x_t[n], q.w], lambda e: e.activation(q.ap, x, ACT.Square))
            if n == 0:
                sums.w = [q, ts]
            else:
                a, t = sums.w
                eng = self.dve if n == NT - 1 else self.pool
                sums.w[1] = eng([ts, t], lambda e: e.tensor_tensor(a.ap, a.ap, q.ap, ALU.add))
                q.done(sums.w[1])

    def project_out(self, name, idx0, kt, nc_, Y, yt, update, mean, order=None):
        sums, done = Slot(None), []
        per = nc_ // P
        for c in range(NT // per):
            ch = self.take(name, idx0 + c)
            tiles = (self.feat2(ch, kt, Y, yt, True, order=order) if per == 2 and c == 0 else
                     (self.feat(ch, kt, nc_, t, Y, yt) for t in range(per)))
            for t, (b, tok) in enumerate(tiles):
                update(per * c + t, b, tok)
                done.append(per * c + t)
            self.release(ch, tok)
            if mean:
                last = c == NT // per - 1
                f = self.mean_of if mean == "ln" else self.square_of
                f(sums, done if last else done[:-2])
                done = done[-2:]
        self.hfree = [tok]
        return sums

    def copy_out(self, dst, b, tok, waits=(), scale=None, q=None, src=None):
        src = b.ap if src is None else src
        q = q or self.act
        if q is self.act:
            if scale is None:
                t = q([tok, list(waits)], lambda e: e.activation(dst, src, ACT.Copy))
            else:
                t = q([tok, list(waits)], lambda e: e.activation(dst, src, ACT.Copy, scale=scale))
        else:
            t = q([tok, list(waits)], lambda e: e.tensor_copy(dst, src))
        return t

    def rope(self, x, tok, perm, cos, sin, ctok=()):
        b = self.banks.get()
        tp = self.mm([tok, b.w, list(ctok)], b.ap, perm, x, sig=True)
        q = self.tmp.get()
        t1 = self.dve([tp, q.w, list(ctok)], lambda e: e.tensor_tensor(q.ap, b.ap, sin, ALU.mult))
        b.done(t1)
        t2 = self.pool([tok, tp, list(ctok)], lambda e: e.tensor_tensor(x, x, cos, ALU.mult))
        t3 = self.dve([t1, t2], lambda e: e.tensor_tensor(x, x, q.ap, ALU.add))
        q.done(t3)
        return t3

    def tick(self):
        while self.bg and callable(self.bg[0]) and self.bg[0]():
            self.bg.pop(0)
        self.rest = max(self.rest - 1, 0)
        for _ in range(self.burst):
            if (not self.bg or callable(self.bg[0]) or len(self.active) >= self.depth or self.rest
                    or self.tmp.free() < self.spare):
                break
            self.active.append(self.bg.pop(0))
        else:
            self.rest = self.pace
        keep = []
        for u in self.active:
            if next(u, "end") != "end":
                keep.append(u)
        self.active = keep

    def until(self, ready):
        while not ready():
            self.tick()

    def pipeline(self, units=()):
        self.bg.extend(units)
        while self.bg or self.active:
            self.tick()

    def softmax_rows(self, src, n, bias, tok, extra=(), mask_from=None):
        q, sm = self.tmp.get(), self.small.get()
        e_, mx, nm, sm_, rc = q.ap[:, 0:n], sm.ap[:, 0:1], sm.ap[:, 1:2], sm.ap[:, 2:3], sm.ap[:, 3:4]
        if bias is not None:
            t = self.dve([tok, q.w, sm.w, list(extra)], lambda e: e.tensor_tensor_reduce(
                e_, src.ap[:, 0:n], bias, 1.0, -3e38, ALU.add, ALU.max, mx))
            src.done(t)
            t = self.dve([t], lambda e: e.tensor_scalar(nm, mx, -1.0, None, ALU.mult))
            t = self.act([t], lambda e: e.activation(e_, e_, ACT.Exp, bias=nm, accum_out=sm_))
        else:
            t = self.dve([tok, sm.w], lambda e: e.tensor_reduce(mx, src.ap[:, 0:n], AXX, ALU.max))
            t = self.dve([t], lambda e: e.tensor_scalar(nm, mx, -1.0, None, ALU.mult))
            t = self.act([t, q.w], lambda e: e.activation(e_, src.ap[:, 0:n], ACT.Exp, bias=nm, accum_out=sm_))
            src.done(t)
        return q, sm, t

    def attend(self, Q, K, V, lo, i, n, bias, extra, out, osl, first, last, finish):
        extra = extra()
        b = self.banks.get()
        tok = self.mm([extra, b.w], b.ap[:, 0:n], Q, K, sig=True)
        q, sm, t = self.softmax_rows(b, n, bias, tok, extra)
        yield
        e_, rc = q.ap[:, 0:n], sm.ap[:, 3:4]
        t = self.dve([t], lambda e: e.reciprocal(rc, sm.ap[:, 2:3]))
        t = self.dve([t], lambda e: e.tensor_scalar(e_, e_, rc, None, ALU.mult))
        sm.done(t)
        yield
        b = self.banks.get()
        for j in range(n // P):
            tt = self.pe([t, b.w], lambda e, j=j: e.transpose(b.ap[:, j * P:(j + 1) * P], e_[:, j * P:(j + 1) * P], self.ident),
                         sig=(j == n // P - 1))
        q.done(tt)
        p = self.tmp.get()
        t = self.act([tt, p.w], lambda e: e.activation(p.ap[:, 0:n], b.ap[:, 0:n], ACT.Copy))
        b.done(t)
        yield
        yield
        o = out()
        for j in range(n // P):
            to = self.mm([t, o.w, extra], osl(o), V(j), p.ap[:, j * P:(j + 1) * P], j == 0, j == n // P - 1,
                         sig=(j == n // P - 1))
        p.done(to)
        if last:
            finish(o, to)


def consts():
    f = np.float32
    i = np.arange(P)
    cc = {}
    cc["ident"] = np.eye(P, dtype=f)
    cc["one"] = np.ones((P, 1), f)
    cc["later"] = (i[:, None] > i[None, :]).astype(f)

    def perm(half, width):
        m = np.zeros((P, P), f)
        for a in range(0, P, 64):
            for r in range(half):
                m[a + half + r, a + r] = -1.0
                m[a + r, a + half + r] = 1.0
        return m

    cc["perm1"] = perm(32, 64)
    cc["perm2"] = perm(8, 16)
    w = np.arange(S)
    diff = i[:, None] + 384 - w[None, :]
    cc["causal"] = np.where(diff >= 0, 0.0, NEG).astype(f)
    cc["strict"] = (i[:, None] < i[None, :]).astype(f)
    blk = np.zeros((P, 2), f)
    blk[0:64, 0] = blk[64:, 1] = 1.0 / 64
    cc["blk"] = blk
    cc["col1024"] = np.full((P, 1), 1.0 / 1024, f)
    cc["col256"] = np.full((P, 1), 1.0 / 256, f)
    cc["col128"] = np.full((P, 1), 1.0 / 128, f)
    inv = (np.float64(500000.0) ** (-np.arange(0, 16, 2, dtype=np.float64) / 16)).astype(f)
    col = np.zeros((P, 1), f)
    for a in (0, 64):
        col[a:a + 8, 0] = inv
        col[a + 8:a + 16, 0] = inv
    cc["inv"] = col
    c1 = {}
    t = np.arange(S, dtype=f)
    for name, freq in (("ret", 1.0 / (10000.0 ** np.linspace(0.0, 1.0, 32))),
                       ("dil", 1.0 / (10000.0 ** (np.arange(0, 64, 2) / 64)))):
        ang = (t[None, :] * freq.astype(f)[:, None]).astype(f).astype(np.float64)
        c1[name + "_cos"] = np.tile(np.cos(ang), (4, 1)).astype(f)
        c1[name + "_sin"] = np.tile(np.sin(ang), (4, 1)).astype(f)
    for h in range(4):
        lg = np.log1p(-(2.0 ** (-5.0 - h)))
        d = w[None, :] - i[:, None]
        c1[f"decay{h}"] = (np.where(d >= 0, np.exp(lg * np.maximum(d, 0)), 0.0) * 0.125).astype(f)
    cnt = (diff >= 0).astype(np.int64) * ((diff <= 128).astype(np.int64) + (diff % 4 == 0) + (diff % 16 == 0))
    c1["dil_mask"] = np.where(cnt > 0, np.log(np.maximum(cnt, 1)), NEG).astype(f)
    sel = np.zeros((P, 13 * P), f)
    for v in range(13 * P):
        sel[v // 64, v] = 1.0
    ct = np.zeros((P, 64), f)
    for g, wd in enumerate((2, 4, 8, 16)):
        ct[:, g * 16:(g + 1) * 16] = 1.0 / np.minimum(np.arange(16) + 1, wd)
    c2 = {"sel": sel, "count": ct}
    out = []
    for d in (cc, c1, c2):
        at, where = 0, {}
        for k, v in d.items():
            where[k] = (at, v.shape[1])
            at += v.shape[1]
        out.append((np.ascontiguousarray(np.concatenate(list(d.values()), 1)), where))
    return out


def first_mixer(p, l):
    H = (p.HH, p.HL)
    p.barrier()
    base = p.base
    with ExitStack() as ctx:
        RQ, RK = p.alloc(ctx, "rq", [P, 2, S]), p.alloc(ctx, "rk", [P, 2, S])
        RV, RG = p.alloc(ctx, "rv", [P, 4, S]), p.alloc(ctx, "rg", [P, 4, S])
        DQ, DK, DV = p.alloc(ctx, "dq", [P, 2, S]), p.alloc(ctx, "dk", [P, 2, S]), p.alloc(ctx, "dv", [P, 4, 256])
        SQ, SK, SV = p.alloc(ctx, "sq", [P, 2, S]), p.alloc(ctx, "sk", [P, 2, S]), p.alloc(ctx, "sv", [P, 4, 256])
        NK = p.alloc(ctx, "nk", [P, 2, 1280])
        extra = p.more_tmp(ctx, 3)
        yt = [None] * 8
        kept = {}
        tk = {}

        p.dve([p.c1_t], lambda e: e.nop(), sig=False)

        def fproj(idx, dst, key, scale=None, eager=False, after=None):
            ch = p.take("w_in", l * 12 + idx)
            r = []
            for t, (b, tok) in enumerate(p.feat2(ch, 8, H, p.ht, eager)):
                r.append(p.copy_out(dst[:, t, :], b, tok, base, scale))
                b.done(r[-1])
            p.release(ch, tok)
            tk[key] = r

        def tproj(idx, dst, c0, key):
            ch = p.take("w_in", l * 12 + idx)
            for i in (0, 2):
                b, tok = p.toks(ch, 8, 256, [i, i + 1], H, p.ht)
                tk.setdefault(key, []).append(p.copy_out(dst[:, i:i + 2, c0:c0 + 256], b, tok, base,
                                                         src=b.ap.rearrange("p (a n) -> p a n", a=2)))
                b.done(tk[key][-1])
            p.release(ch, tok)
            return tok

        def roped(X, key, kind):
            tk[key] = [p.rope(X[:, t, :], tk[key][t], p.perm1, p.c1(kind + "_cos"), p.c1(kind + "_sin"), [p.c1_t])
                       for t in range(2)]

        def keep(n, o, to, dst, waits=()):
            t = p.copy_out(dst, o, to, waits)
            o.done(t)
            kept[n] = (dst, t)

        offs = [0, 512, 896, 1152]
        nk_t = {}
        nkfree = [[], []]
        sb_last = []

        def sb_unit(pr, j, cell):
            n = S - j * P
            st = []
            for c in range(2):
                r = slice(64 * c, 64 * c + 64)
                b = p.banks.get()
                tok = p.mm([tk["sq"], tk["sk"], b.w], b.ap[:, 0:n], SK[r, pr, j * P:(j + 1) * P], SQ[r, pr, j * P:S], sig=True)
                q = p.tmp.get()
                t = p.act([tok, q.w], lambda e: e.activation(q.ap[:, 0:n], b.ap[:, 0:n], ACT.Abs))
                t = p.act([t], lambda e: e.activation(q.ap[:, 0:n], q.ap[:, 0:n], ACT.Exp, scale=-1.0))
                st.append([b, q, q.ap[:, 0:n], NK[:, c, offs[j]:offs[j] + n], t])
            for s in st:
                b, q, a, nk, t = s
                s[4] = p.act([t], lambda e: e.activation(a, a, ACT.Ln, bias=1.0))
            yield
            for c, s in enumerate(st):
                b, q, a, nk, t = s
                z = b.ap[:, 0:n]
                t1 = p.dve([t, base, nkfree[c]], lambda e: e.scalar_tensor_tensor(nk, z, 0.0, a, ALU.max, ALU.add))
                s[4] = p.dve([t1], lambda e: e.tensor_tensor(a, z, nk, ALU.subtract))
                b.done(s[4])
                nk_t[c, j] = p.pool([s[4]], lambda e: e.tensor_tensor(nk[:, 0:P], nk[:, 0:P], p.strict, ALU.mult))
            yield
            for c, s in enumerate(st):
                _, q, a, nk, t2 = s
                b = p.banks.get()
                bt = p.mm([nk_t[c, j], b.w], b.ap[:, 0:n], p.later, nk, True, j == 3, sig=(j == 3))
                for jj in range(j + 1, 4):
                    m = S - jj * P
                    bt = p.mm([nk_t[c, jj]], b.ap[:, n - m:n], p.one.to_broadcast([P, P]), NK[:, c, offs[jj]:offs[jj] + m],
                              False, jj == 3, sig=(jj == 3))
                if j == 0:
                    nkfree[c] = [bt]
                t = p.dve([bt, t2], lambda e: e.tensor_tensor(a, a, b.ap[:, 0:n], ALU.subtract))
                b.done(t)
                s[4] = p.act([t], lambda e: e.activation(a, a, ACT.Exp))
            yield
            for s in st:
                a, t = s[2], s[4]
                s[4] = p.pool([t], lambda e: e.tensor_tensor(a[:, 0:P], a[:, 0:P], p.strict, ALU.mult))
            if not cell:
                cell.append(p.held.get())
            o = cell[0]
            yield
            for c, (_, q, a, _, t) in enumerate(st):
                h, r = 2 * pr + c, slice(64 * c, 64 * c + 64)
                to = p.mm([t, o.w, tk["sv"]], o.ap[r, j * P:S], SV[:, j, 64 * h:64 * h + 64], a, j == 3, j == 0, sig=True)
                q.done(to)
            if j == 0:
                keep(6 + pr, o, to, SQ[:, pr, :])
                sb_last.append(to)

        def sb_units():
            for pr in range(2):
                cell = []
                for j in (3, 2, 1, 0):
                    yield sb_unit(pr, j, cell)

        NKF = NK[:, :, :].rearrange("p a n -> p (a n)")
        oh = {}

        def ret_unit(h, j, cell):
            r = slice(64 * (h % 2), 64 * (h % 2) + 64)
            n = S - j * P
            b = p.banks.get()
            tok = p.mm([tk["rq"], tk["rk"], b.w], b.ap[:, 0:n], RK[r, h // 2, j * P:(j + 1) * P], RQ[r, h // 2, j * P:S], sig=True)
            q = p.tmp.get()
            t = p.dve([tok, q.w], lambda e: e.tensor_tensor(q.ap[:, 0:n], b.ap[:, 0:n], p.c1(f"decay{h}")[:, 0:n], ALU.mult))
            b.done(t)
            yield
            if j == 0:
                cell.append(p.held.get())
            o = cell[0]
            to = p.mm([t, o.w, tk["rv"]], o.ap[:, j * P:S], RV[:, j, h * P:(h + 1) * P], q.ap[:, 0:n], j == 0, j == 3, sig=True)
            q.done(to)
            if j == 3:
                dst = NKF[:, h * S:(h + 1) * S]
                t = p.copy_out(dst, o, to, sb_last)
                o.done(t)
                oh[h] = (dst, t)

        def ret_norm():
            yield
            yield
            st = p.held.get()
            for h in range(4):
                dst, t = oh[h]
                tm = p.stat(st, h, 4, dst, t, p.col128, True, True)
            yield
            y = p.yr.get()
            t = p.dve([tm, y.w], lambda e: e.tensor_copy(y.ap[:, 0:16], st.ap[:, 0:16]))
            st.done(t)
            st = p.held.get()
            prev = None
            for h in range(5):
                if h < 4:
                    dst, to = oh[h]
                    b, tb = p.spread(y.ap, [4 * i + h for i in range(4)], t)
                    td = p.dve([tb, to], lambda e: e.tensor_tensor(dst, dst, b.ap, ALU.subtract))
                    b.done(td)
                    q = p.tmp.get()
                    ts = p.act([td, q.w], lambda e: e.activation(q.ap, dst, ACT.Square))
                    oh[h] = (dst, [td, ts])
                if prev is not None:
                    q0, ts0 = prev
                    tv = p.stat(st, h - 1, 4, q0.ap, ts0, p.col128, True, True)
                    q0.done(tv)
                prev = (q, ts)
                yield
            y.done(tb)
            y, t, read = p.rsqrt(st.ap[:, 0:16], 16, 1e-6, [tv])
            st.done(read)
            yield
            for h in range(4):
                dst, to = oh[h]
                b, tb = p.spread(y.ap, [4 * i + h for i in range(4)], t)
                g = RG[:, h, :]
                tg = p.pool([tk["rg"][h], to], lambda e: e.tensor_tensor(g, dst, g, ALU.mult))
                td = p.dve([tb, tg], lambda e: e.tensor_tensor(g, g, b.ap, ALU.mult))
                b.done(td)
                kept[h] = (g, td)
                yield
            y.done(tb)

        def setpace(n):
            p.pace = n
            return True

        def ret_units():
            for h in range(4):
                cell = []
                for j in range(4):
                    yield ret_unit(h, j, cell)
            yield ret_norm()

        def emit(n, o, to):
            yt[n] = p.parts(p.HH[:, n, :], p.HL[:, n, :], o.ap, [to], p.dve, p.hfree)
            o.done(*yt[n])

        def dil_units():
            for pr in range(2):
                cell = []

                def out(cell=cell):
                    if not cell:
                        cell.append(p.held.get())
                    return cell[0]

                for i in range(4):
                    for c in range(2):
                        n = (i + 1) * P
                        r = slice(64 * c, 64 * c + 64)
                        yield p.attend(
                            DQ[r, pr, i * P:(i + 1) * P], DK[r, pr, 0:n],
                            lambda j, pr=pr, c=c: DV[:, j, 64 * (2 * pr + c):64 * (2 * pr + c) + 64],
                            0, i, n, p.c1("dil_mask")[:, 384 - i * P:S], lambda: [tk["dq"], tk["dk"], tk["dv"], p.c1_t], out,
                            lambda o, r=r, i=i: o.ap[r, i * P:(i + 1) * P], i == 0, i == 3 and c == 1,
                            lambda o, to, pr=pr: emit(4 + pr, o, to))

        fproj(9, SQ, "sq", 0.125, eager=True)
        fproj(10, SK, "sk")
        tproj(11, SV, 0, "sv")
        p.bg.extend(sb_units())
        p.pace = 2
        fproj(0, RQ, "rq")
        fproj(1, RK, "rk")
        roped(RQ, "rq", "ret")
        roped(RK, "rk", "ret")
        tproj(2, RV, 0, "rv")
        tproj(3, RV, 256, "rv")
        p.bg.append(lambda: setpace(1))
        p.bg.extend(ret_units())
        tk["rg"] = []
        for c in range(2):
            ch = p.take("w_in", l * 12 + 4 + c)
            for t, (b, tok) in enumerate(p.feat2(ch, 8, H, p.ht)):
                dst = RG[:, 2 * c + t, :]
                tk["rg"].append(p.act([tok, base], lambda e: e.activation(dst, b.ap, ACT.Silu)))
                b.done(tk["rg"][-1])
            p.release(ch, tok)
        fproj(6, DQ, "dq", 0.125)
        fproj(7, DK, "dk")
        roped(DQ, "dq", "dil")
        roped(DK, "dk", "dil")
        last = tproj(8, DV, 0, "dv")
        p.hfree = [last]
        p.burst, p.depth = 2, 8
        p.pipeline(dil_units())
        p.burst, p.depth = 1, 6
        order = (6, 7, 0, 1, 2, 3, 4, 5)
        for i, n in enumerate(order[:6]):
            src, t = kept[n]
            yt[n] = p.parts(p.HH[:, n, :], p.HL[:, n, :], src, [t], (p.pool, p.dve)[i % 2], p.hfree)
        s, ts = p.gate(l, 5, 1.0)
        r = p.project_out("w_out", l * 4, 8, 256, H, yt, lambda n, b, tok: p.update_gated(n, b, tok, s, ts), "ln", order)
        s.done(p.x_t[7])
        p.less_tmp(extra)
    p.barrier()
    return r


def even_mixer(p):
    H = (p.HH, p.HL)
    p.barrier()
    base = p.base
    with ExitStack() as ctx:
        QA, KA, VA = (p.alloc(ctx, n, [P, 4, S]) for n in ("qa", "ka", "va"))
        QB, KB, VB = (p.alloc(ctx, n, [P, 4, S]) for n in ("qb", "kb", "vb"))
        QI, KI = p.alloc(ctx, "qi", [P, 2, S]), p.alloc(ctx, "ki", [P, S])
        BM = p.alloc(ctx, "bm", [P, 1152])
        RT = p.alloc(ctx, "rt", [32, S])
        WI = p.alloc(ctx, "wi", [P, 4, 4])
        ST = p.alloc(ctx, "stt", [P, 4, 16])
        more = p.more_tmp(ctx, 1)
        p.spare, p.depth = 3, 7
        p.dve([p.c2_t, p.rope_t, p.lam_t], lambda e: e.nop(), sig=False)
        raw = {}
        st_t, st_free = [], []
        rt_free = list(base)
        pend = []

        def flush(col=p.blk, n=2):
            if not pend:
                return
            b = p.banks.get()
            c0 = pend[0][2]
            w = n * len(pend)
            for k, (q, ts, c) in enumerate(pend):
                tv = p.stat(b, c - c0, w, q.ap, ts, col, True, True, n=n)
                q.done(tv)
            t = p.dve([tv, st_free, base], lambda e: e.tensor_copy(
                ST[:, :, c0:c0 + w], b.ap[:, 0:4 * w].rearrange("p (a n) -> p a n", a=4)))
            b.done(t)
            st_t.append(t)
            pend.clear()

        def squared(b, tok, col):
            q = p.tmp.get()
            ts = p.act([tok, q.w], lambda e: e.activation(q.ap, b.ap, ACT.Square))
            b.done(ts)
            pend.append((q, ts, col))

        def fproj(idx, dst, key, col, stat=True, eager=False):
            ch = p.take("w_in_e", idx)
            for t, (b, tok) in enumerate(p.feat2(ch, 8, H, p.ht, eager)):
                if t == 0:
                    flush()
                raw[key, t] = p.copy_out(dst[t], b, tok, base)
                if stat:
                    squared(b, tok, col + 2 * t)
                else:
                    b.done(raw[key, t])
            p.release(ch, tok)
            return tok

        def group(n, tiles):
            y, t, read = p.rsqrt(ST[:, :, 0:n], 4 * n, 1e-6, list(st_t))
            st_free[:] = [read]
            st_t.clear()
            yield
            b = p.banks.get()
            for i in range(4):
                tt = p.pe([t, b.w], lambda e, i=i: e.transpose(b.ap[0:n, i * P:(i + 1) * P],
                                                               y.ap[:, i * n:(i + 1) * n], p.ident), sig=(i == 3))
            y.done(tt)
            t_rt = p.dve([tt, list(rt_free)], lambda e: e.tensor_copy(RT[0:n, :], b.ap[0:n, :]))
            b.done(t_rt)
            yield
            prev = None
            for k in range(len(tiles) + 1):
                if k < len(tiles):
                    x, g, tok, put = tiles[k]
                    b = p.banks.get()
                    tb = p.mm([t_rt, b.w, p.c2_t], b.ap, p.c2("sel")[0:n, k * P:(k + 1) * P], RT[0:n, :], sig=True)
                    t = p.dve([tb, tok], lambda e: e.scalar_tensor_tensor(x, x, g, b.ap, ALU.mult, ALU.mult))
                    b.done(t)
                    rt_free[:] = [tb]
                if prev:
                    prev[1](p.rope(prev[0], prev[2], p.perm2, p.COS2, p.SIN2, [p.rope_t]))
                prev = (x, put, t)
                yield

        def putter(lst, n):
            def put(t):
                lst[n] = t
            return put

        ki_t, qi_t = [None], [None, None]
        ch = p.take("w_kiwi", 0)
        b, tok = p.feat(ch, 8, 132, 0, H, p.ht)
        t_ki = p.copy_out(KI[:, :], b, tok, base)
        squared(b, tok, 0)
        b, tok = p.feat(ch, 8, 132, 0, H, p.ht, M=4, off=128)
        p.release(ch, tok)
        wi = p.tmp.get()
        t = p.act([tok, wi.w], lambda e: e.activation(wi.ap[0:4, :], b.ap[0:4, :], ACT.Copy, scale=1.0 / 16))
        b.done(t)
        wi_t = [t]
        ch = p.take("w_in_e", 7)
        for t, (b, tok) in enumerate(p.feat2(ch, 8, H, p.ht)):
            if t == 0:
                flush()
                b1 = p.banks.get()
                for i in range(4):
                    tt = p.pe([wi_t, b1.w], lambda e, i=i: e.transpose(
                        b1.ap[:, 4 * i:4 * i + 4], wi.ap[0:4, i * P:(i + 1) * P], p.ident[0:4, 0:4]), sig=(i == 3))
                wi.done(tt)
                t_wi = p.dve([tt, base], lambda e: e.tensor_copy(
                    WI[:, :, :], b1.ap[:, 0:16].rearrange("p (a n) -> p a n", a=4)))
                b1.done(t_wi)
                p.bg.append(group(2, [(KI[:, :], p.vec("g_kidx"), t_ki, putter(ki_t, 0))]))
            raw["qi", t] = p.copy_out(QI[:, t, :], b, tok, base)
            b.done(raw["qi", t])
        p.release(ch, tok)
        p.until(lambda: ki_t[0])

        bm_at = [None, 0, 256, 640]
        bm_t = [None] * 4

        def index():
            for t in range(2):
                qi_t[t] = p.rope(QI[:, t, :], raw["qi", t], p.perm2, p.COS2, p.SIN2, [p.rope_t])
                yield
            for i in (1, 2, 3):
                n = (i + 1) * P
                w = BM[:, bm_at[i]:bm_at[i] + n]
                tw = None
                for h in range(4):
                    r = slice(64 * (h % 2), 64 * (h % 2) + 64)
                    b = p.banks.get()
                    tok = p.mm([qi_t, ki_t, b.w], b.ap[:, 0:n], QI[r, h // 2, i * P:(i + 1) * P], KI[r, 0:n], sig=True)
                    q = p.tmp.get()
                    t = p.act([tok, q.w], lambda e: e.activation(q.ap[:, 0:n], b.ap[:, 0:n], ACT.Relu))
                    b.done(t)
                    s = WI[:, i, h:h + 1]
                    if h == 0:
                        tw = p.dve([t, base, t_wi], lambda e: e.tensor_scalar(w, q.ap[:, 0:n], s, None, ALU.mult))
                    else:
                        tw = p.dve([t, tw], lambda e: e.scalar_tensor_tensor(w, q.ap[:, 0:n], s, w, ALU.mult, ALU.add))
                    q.done(tw)
                    if h % 2:
                        yield
                tw = p.dve([tw], lambda e: e.tensor_tensor(w, w, p.causal[:, 384 - i * P:S], ALU.add))
                s = p.small.get()
                for r in range(16):
                    tm = p.dve([tw, s.w], lambda e: e.max(s.ap[:, 0:8], w))
                    tw = p.dve([tm], lambda e: e.match_replace(w, s.ap[:, 0:8], w, TAKEN))
                    yield
                s.done(tw)
                bm_t[i] = p.dve([tw], lambda e: e.tensor_scalar(w, w, -2e38, NEG, ALU.is_gt, ALU.mult))

        p.bg.append(index())
        small = p.small.get()
        tg = p.dve([small.w, p.vec_t], lambda e: e.tensor_scalar(small.ap[:, 0:1], p.vec("gq_a"), 0.125, None, ALU.mult))
        tg = p.dve([tg], lambda e: e.tensor_scalar(small.ap[:, 1:2], p.vec("gq_b"), 0.125, None, ALU.mult))
        for i, (X, key) in enumerate(((QA, "qa"), (KA, "ka"))):
            for c in range(2):
                fproj(2 * i + c, [X[:, 2 * c, :], X[:, 2 * c + 1, :]], (key, c), 8 * i + 4 * c)
        qa, ka, qb, kb = ([None] * 4 for _ in range(4))
        va = []
        for c in range(2):
            ch = p.take("w_in_e", 8 + c)
            for i in (0, 2):
                b, tok = p.toks(ch, 8, 256, [i, i + 1], H, p.ht)
                va.append(p.copy_out(VA[:, i:i + 2, 256 * c:256 * c + 256], b, tok, base,
                                     src=b.ap.rearrange("p (a n) -> p a n", a=2)))
                b.done(va[-1])
                if i + c:
                    continue
                flush()
                order = [(QA, "qa", small.ap[:, 0:1], qa), (KA, "ka", p.vec("gk_a"), ka)]
                p.bg.append(group(16, [(X[:, n, :], g, [raw[(key, n // 2), n % 2], tg], putter(lst, n))
                                       for X, key, g, lst in order for n in range(4)]))
            p.release(ch, tok)

        lam = p.LAM[:, 0:1]
        o_raw = {}

        def a_unit(h, i, cell):
            n = (i + 1) * P
            sub = []
            for c in range(2):
                r = slice(64 * c, 64 * c + 64)
                b = p.banks.get()
                tok = p.mm([qa[h], ka[h], b.w], b.ap[:, 0:n], QA[r, h, i * P:(i + 1) * P], KA[r, h, 0:n], sig=True)
                sub.append(p.softmax_rows(b, n, p.causal[:, 384 - i * P:S], tok))
            yield
            (q0, s0, t0), (q1, s1, t1) = sub
            e0, e1 = q0.ap[:, 0:n], q1.ap[:, 0:n]
            t0 = p.dve([t0], lambda e: e.reciprocal(s0.ap[:, 3:4], s0.ap[:, 2:3]))
            t1 = p.dve([t1], lambda e: e.reciprocal(s1.ap[:, 3:4], s1.ap[:, 2:3]))
            t0 = p.dve([t0], lambda e: e.tensor_scalar(e0, e0, s0.ap[:, 3:4], None, ALU.mult))
            t1 = p.dve([t1, p.lam_t], lambda e: e.tensor_tensor(s1.ap[:, 4:5], s1.ap[:, 3:4], lam, ALU.mult))
            t = p.dve([t0, t1], lambda e: e.scalar_tensor_tensor(e0, e1, s1.ap[:, 4:5], e0, ALU.mult, ALU.add))
            q1.done(t)
            s0.done(t)
            s1.done(t)
            yield
            b = p.banks.get()
            for j in range(i + 1):
                tt = p.pe([t, b.w], lambda e, j=j: e.transpose(b.ap[:, j * P:(j + 1) * P], e0[:, j * P:(j + 1) * P], p.ident),
                          sig=(j == i))
            q0.done(tt)
            pt = p.tmp.get()
            t = p.act([tt, pt.w], lambda e: e.activation(pt.ap[:, 0:n], b.ap[:, 0:n], ACT.Copy))
            b.done(t)
            yield
            yield
            if not cell:
                cell.append(p.held.get())
            o = cell[0]
            for j in range(i + 1):
                to = p.mm([t, o.w, va], o.ap[:, i * P:(i + 1) * P], VA[:, j, h * P:(h + 1) * P], pt.ap[:, j * P:(j + 1) * P],
                          j == 0, j == i, sig=(j == i))
            pt.done(to)
            if i == 3:
                dst = QA[:, h, :]
                t = p.copy_out(dst, o, to)
                o.done(t)
                o_raw[h] = (dst, t)

        def a_units():
            for h in range(4):
                cell = []
                for i in range(4):
                    yield a_unit(h, i, cell)

        p.bg.append(lambda: ka[3])
        p.bg.extend(a_units())
        fproj(6, [KB[:, 0, :], KB[:, 1, :]], ("ckv", 0), 0)
        sq, pend[:] = list(pend), []
        ct = []

        def compressed():
            b = p.banks.get()
            for i in range(4):
                for k in range(2):
                    tv = p.mm([sq[k][1], b.w], b.ap[:, i:i + 1], sq[k][0].ap[:, i * P:(i + 1) * P],
                              p.col256, k == 0, k == 1, sig=(i == 3 and k == 1))
            for k in range(2):
                sq[k][0].done(tv)
            yield
            y, t, read = p.rsqrt(b.ap[:, 0:4], 4, 1e-6, [tv])
            b.done(read)
            yield
            b, tb = p.spread(y.ap, range(4), t)
            y.done(tb)
            cs = []
            for k in range(2):
                q, x = p.tmp.get(), KB[:, k, :]
                t = p.dve([tb, q.w, raw[("ckv", 0), k]], lambda e: e.scalar_tensor_tensor(
                    q.ap, x, p.vec("g_kv_b", k), b.ap, ALU.mult, ALU.mult))
                cs.append((q, t))
            b.done(t)
            yield
            held.extend(cs)

        held = []
        p.bg.insert(0, compressed())
        for c in range(2):
            last = fproj(4 + c, [QB[:, 2 * c, :], QB[:, 2 * c + 1, :]], ("qb", c), 4 * c)
        p.hfree = [last]
        p.until(lambda: held)
        for k, (q, t) in enumerate(held):
            ct.append(p.parts(p.HH[:, k, :], p.HL[:, k, :], q.ap, [t], p.dve, p.hfree))
            q.done(*ct[k])
        ch = p.take("w_kv_up", 0)
        vb = []

        def vup(i):
            b, tok = p.toks(ch, 2, 1024, [i], H, ct, cols=(512, 512))
            vb.append(p.copy_out(VB[:, i, :], b, tok, base))
            b.done(vb[-1])
            p.tick()
            return tok

        for n in range(4):
            b, tok = p.feat(ch, 2, 1024, n, H, ct)
            raw["kb", n] = p.copy_out(KB[:, n, :], b, tok, base)
            if n % 2 == 0:
                flush()
            squared(b, tok, 8 + 2 * n)
            p.tick()
        vup(0)
        flush()
        order = [(QB, lambda n: raw[("qb", n // 2), n % 2], small.ap[:, 1:2], qb), (KB, lambda n: raw["kb", n], p.vec("gk_b"), kb)]
        p.bg.insert(0, group(16, [(X[:, n, :], g, [at(n), tg], putter(lst, n))
                                  for X, at, g, lst in order for n in range(4)]))
        for i in (1, 2, 3):
            tok = vup(i)
        p.release(ch, tok)
        p.hfree = [tok]
        yt = [None] * 8

        def a_norm():
            sg = p.small.get()
            tg = p.dve([sg.w], lambda e: e.tensor_scalar(sg.ap[:, 0:1], p.vec("g_sub_a"), 0.8, None, ALU.mult))
            st = p.banks.get()
            for h in range(4):
                dst, t = o_raw[h]
                q = p.tmp.get()
                ts = p.act([t, q.w], lambda e: e.activation(q.ap, dst, ACT.Square))
                yield
                tv = p.stat(st, h, 4, q.ap, ts, p.col128, True, True)
                q.done(tv)
            y, t, read = p.rsqrt(st.ap[:, 0:16], 16, 1e-6, [tv])
            st.done(read)
            yield
            for h in range(4):
                dst, to = o_raw[h]
                b, tb = p.spread(y.ap, [4 * i + h for i in range(4)], t)
                td = p.dve([tb, to, tg, tv], lambda e: e.scalar_tensor_tensor(dst, dst, sg.ap[:, 0:1], b.ap, ALU.mult, ALU.mult))
                b.done(td)
                yt[h] = p.parts(p.HH[:, h, :], p.HL[:, h, :], dst, [td], p.pool, p.hfree)
                yield
            y.done(tb)
            sg.done(td)

        def emit(n, o, to):
            yt[n] = p.parts(p.HH[:, n, :], p.HL[:, n, :], o.ap, [to], p.dve, p.hfree)
            o.done(*yt[n])

        def b_units():
            for pr in range(4):
                cell = []

                def out(cell=cell):
                    if not cell:
                        cell.append(p.held.get())
                    return cell[0]

                for i in range(4):
                    for c in range(2):
                        n = (i + 1) * P
                        r = slice(64 * c, 64 * c + 64)
                        bias = p.causal[:, 384:S] if i == 0 else BM[:, bm_at[i]:bm_at[i] + n]
                        yield p.attend(
                            QB[r, pr, i * P:(i + 1) * P], KB[r, pr, 0:n],
                            lambda j, pr=pr, c=c: VB[:, j, 64 * (2 * pr + c):64 * (2 * pr + c) + 64],
                            0, i, n, bias, lambda pr=pr, i=i: [qb[pr], kb[pr], vb, bm_t[i]], out,
                            lambda o, r=r, i=i: o.ap[r, i * P:(i + 1) * P], i == 0, i == 3 and c == 1,
                            lambda o, to, pr=pr: emit(4 + pr, o, to))

        p.bg.append(lambda: len(o_raw) == 4)
        p.bg.append(a_norm())
        p.bg.append(lambda: kb[3] and bm_t[3])
        p.burst = 2
        p.pipeline(b_units())
        p.burst = 1
        small.done(*qa, *qb)
        p.less_tmp(more)
        p.spare, p.depth = 0, 6
    return yt


def odd_mixer(p):
    H = (p.HH, p.HL)
    p.barrier()
    base = p.base
    with ExitStack() as ctx:
        GB, GC = p.alloc(ctx, "gb", [P, 4, S]), p.alloc(ctx, "gc", [P, 4, S])
        U = p.alloc(ctx, "u", [P, 4, S + 2])
        Z = p.alloc(ctx, "z", [P, 4, S + 16])
        SA, SB = p.alloc(ctx, "sa", [P, S + 16]), p.alloc(ctx, "sbb", [P, S + 16])
        PO = p.alloc(ctx, "po", [P, 4, S])
        PH, PL = p.alloc(ctx, "ph", [P, 512], F32R), p.alloc(ctx, "pl", [P, 512], F32R)
        WP = p.alloc(ctx, "wp", [P, 2, 512], F32R)
        more = p.more_tmp(ctx, 2)
        tz = p.pool([base], lambda e: e.memset(U[:, :, 0:2], 0.0))
        tz2 = p.pool([base], lambda e: e.memset(Z[:, :, 0:16], 0.0))
        tz3 = p.pool([base], lambda e: e.memset(SA[:, 0:16], 0.0))
        tz4 = p.pool([base], lambda e: e.memset(SB[:, 0:16], 0.0))
        zt = [tz, tz2, tz3, tz4]
        gb, gc, u, zd = [], [], [], []
        out = [None] * 8
        wp = []

        def conv(n):
            acc = GC[:, n, :]
            w = [p.vec("conv_w", 4 * k + n) for k in range(3)]
            t = p.dve([u[n]], lambda e: e.tensor_scalar(acc, U[:, n, 0:S], w[0], None, ALU.mult))
            yield
            for k in (1, 2):
                t = p.dve([t], lambda e: e.scalar_tensor_tensor(acc, U[:, n, k:k + S], w[k], acc, ALU.mult, ALU.add))
            yield
            t = p.dve([t, gb[n]], lambda e: e.tensor_tensor(acc, acc, GB[:, n, :], ALU.mult))
            out[n] = (acc, t)

        def pool():
            prev, pfree = list(zt), list(base)
            for g, wd in enumerate((2, 4, 8, 16)):
                src, t, k = Z[:, g, :], zd[g], 1
                bufs = [SA[:, :], SB[:, :]]
                while k < wd:
                    dst = bufs[0]
                    t = p.dve([t, prev], lambda e: e.tensor_tensor(
                        dst[:, 16:S + 16], src[:, 16:S + 16], src[:, 16 - k:S + 16 - k], ALU.add))
                    src, bufs, k = dst, bufs[::-1], 2 * k
                    yield
                q = p.tmp.get()
                t1 = p.dve([t, q.w], lambda e: e.tensor_scalar(q.ap, src[:, 16:S + 16], 1.0 / wd, None, ALU.mult))
                t1 = p.dve([t1, p.c2_t], lambda e: e.tensor_tensor(
                    q.ap[:, 0:16], src[:, 16:32], p.c2("count")[:, g * 16:(g + 1) * 16], ALU.mult))
                prev = [t1]
                t1 = p.dve([t1], lambda e: e.tensor_tensor(q.ap, q.ap, Z[:, g, 16:S + 16], ALU.subtract))
                pt = p.parts(PH[:, :], PL[:, :], q.ap, [t1], p.pool, pfree)
                q.done(*pt)
                yield
                yield
                b = p.banks.get()
                tok = p.mm3([wp, pt, b.w], b.ap, WP[:, 0, g * P:(g + 1) * P], WP[:, 1, g * P:(g + 1) * P], PH[:, :],
                            PL[:, :], True, True, sig=True)
                pfree = [tok]
                dst = PO[:, g, :]
                t = p.act([tok, base], lambda e: e.activation(dst, b.ap, ACT.Identity, scale=p.vec("pool_scale", g)))
                b.done(t)
                out[4 + g] = (dst, t)
                yield

        for step, i in enumerate((6, 7, 2, 3, 4, 5, 0, 1)):
            ch = p.take("w_in_o", i)
            for t, (b, tok) in enumerate(p.feat2(ch, 8, H, p.ht, step == 0)):
                n = 2 * (i % 2) + t
                if i < 2:
                    gb.append(p.copy_out(GB[:, n, :], b, tok, base))
                    b.done(gb[-1])
                elif i < 4:
                    gc.append(p.copy_out(GC[:, n, :], b, tok, base))
                    b.done(gc[-1])
                elif i < 6:
                    u.append(p.dve([tok, gc[n], zt], lambda e, n=n, b=b: e.tensor_tensor(U[:, n, 2:S + 2], GC[:, n, :], b.ap, ALU.mult)))
                    b.done(u[-1])
                else:
                    zd.append(p.copy_out(Z[:, n, 16:S + 16], b, tok, [zt]))
                    b.done(zd[-1])
            p.release(ch, tok)
            if i == 7:
                ch = p.take("w_pool", 0)
                _, wh, wl, toks, _ = ch
                for k, w in enumerate((wh, wl)):
                    wp.append(p.act([toks, base], lambda e: e.activation(WP[:, k, :], w[:, 0:512].bitcast(F32), ACT.Copy)))
                p.release(ch, wp[-1])
                p.bg.append(pool())
            if i == 0:
                p.bg.extend([conv(0), conv(1)])
        p.hfree = [tok]
        p.pipeline([conv(2), conv(3)])
        yt = [None] * 8
        for i, n in enumerate(ODD_ORDER):
            src, t = out[n]
            yt[n] = p.parts(p.HH[:, n, :], p.HL[:, n, :], src, [t], (p.pool, p.dve)[i % 2], p.hfree)
        p.less_tmp(more)
    return yt


def cross(p, l, name, yt):
    H = (p.HH, p.HL)
    p.barrier()
    base = p.base
    M = 256
    with ExitStack() as ctx:
        MT = p.alloc(ctx, "mt", [P, 8, M])
        MH, ML = p.alloc(ctx, "mh", [P, 8, M], F32R), p.alloc(ctx, "ml", [P, 8, M], F32R)
        QX, KX, VX = p.alloc(ctx, "qx", [P, 4, S]), p.alloc(ctx, "kx", [P, 4, M]), p.alloc(ctx, "vx", [P, 2, S])
        more = p.more_tmp(ctx, 6)
        tl = p.load("mem", MT[:, :, :], p.dram["memT"], base)
        mt = []

        def memory():
            sq = []
            for k in range(8):
                q = p.tmp.get()
                ts = p.act([tl, q.w], lambda e: e.activation(q.ap[:, 0:M], MT[:, k, :], ACT.Square))
                if not sq:
                    sq = [q, ts]
                else:
                    a, ta = sq
                    sq[1] = p.pool([ts, ta], lambda e: e.tensor_tensor(a.ap[:, 0:M], a.ap[:, 0:M], q.ap[:, 0:M], ALU.add))
                    q.done(sq[1])
                if k % 2:
                    yield
            b = p.banks.get()
            tv = p.stat(b, 0, 1, sq[0].ap, sq[1], p.col1024, True, True, tiles=2)
            sq[0].done(tv)
            yield
            y, t, read = p.rsqrt(b.ap[:, 0:2], 2, 1e-6, [tv])
            b.done(read)
            yield
            b, tb = p.spread(y.ap, range(2), t, tiles=2)
            y.done(tb)
            for k in range(8):
                q = p.tmp.get()
                t = p.dve([tb, tl, q.w], lambda e: e.scalar_tensor_tensor(
                    q.ap[:, 0:M], MT[:, k, :], p.vec("g_mem", l * 8 + k), b.ap[:, 0:M], ALU.mult, ALU.mult))
                mt.append(p.parts(MH[:, k, :], ML[:, k, :], q.ap[:, 0:M], [t], p.pool, base))
                q.done(*mt[k])
                if k % 2:
                    yield
            b.done(t)

        def head_norm(X, n, heads, sq, raw, gain, out):
            w, nt = len(heads), n // P
            yield
            b = p.banks.get()
            for i, (q, ts) in enumerate(sq):
                tv = p.stat(b, i, w, q.ap, ts, p.col128, True, True, tiles=nt)
                q.done(tv)
            y, t, read = p.rsqrt(b.ap[:, 0:w * nt], w * nt, 1e-6, [tv])
            b.done(read)
            yield
            yield
            for i, h in enumerate(heads):
                b, tb = p.spread(y.ap, [w * j + i for j in range(nt)], t, tiles=nt)
                out[h] = p.dve([tb, raw[i]], lambda e: e.scalar_tensor_tensor(
                    X[:, h, :], X[:, h, :], gain, b.ap[:, 0:n], ALU.mult, ALU.mult))
                b.done(out[h])
            y.done(tb)

        def tiles_of(ch, X, xt, dst, n0, n, eager=False):
            raw, sq = [], []
            for t, (b, tok) in enumerate(p.feat2(ch, 8, X, xt, eager, N=n)):
                raw.append(p.copy_out(dst[:, n0 + t, :], b, tok, base, src=b.ap[:, 0:n]))
                q = p.tmp.get()
                ts = p.act([tok, q.w], lambda e: e.activation(q.ap[:, 0:n], b.ap[:, 0:n], ACT.Square))
                b.done(ts)
                sq.append((q, ts))
            p.release(ch, tok)
            return raw, sq, tok

        def kproj(c):
            raw, sq, _ = tiles_of(p.take("wkv_x", l * 4 + c), (MH, ML), mt, KX, 2 * c, M)
            later.append(head_norm(KX, M, [2 * c, 2 * c + 1], sq, raw, p.vec("gk_x", l), kx))

        def vproj(c, ch=None):
            ch = ch or p.take("wkv_x", l * 4 + 2 + c)
            b, tok = p.toks(ch, 8, 256, [0, 1], (MH, ML), mt)
            vx.append(p.copy_out(VX[:, :, 256 * c:256 * c + 256], b, tok, base, src=b.ap.rearrange("p (a n) -> p a n", a=2)))
            b.done(vx[-1])
            p.release(ch, tok)

        sg = p.small.get()
        tg = p.dve([sg.w], lambda e: e.tensor_scalar(sg.ap[:, 0:1], p.vec("gq_x", l), 128.0 ** -0.5, None, ALU.mult))

        def qproj(c):
            raw, sq, tok = tiles_of(p.take("wq_x", l * 2 + c), H, p.ht, QX, 2 * c, S, c == 0)
            p.hfree = [tok]
            p.bg.append(head_norm(QX, S, [2 * c, 2 * c + 1], sq, [[r, tg] for r in raw], sg.ap[:, 0:1], qx))

        kx, qx, vx, later = [None] * 4, [None] * 4, [], []
        p.bg.append(memory())
        sums = p.project_out(name, 0, 8, 256, H, yt, p.update_plain, "rms", ODD_ORDER if l else None)
        p.until(lambda: len(mt) == 8)
        kproj(0)
        taken = []

        def between():
            kproj(1)
            taken.append(p.take("wkv_x", l * 4 + 2))

        p.rms_norm("g_xattn", l, sums, (between, lambda: vproj(0, taken[0])))
        p.bg.extend(later)
        qproj(0)
        vproj(1)
        yt, kept = [None] * 4, {}

        def emit(n, o, to):
            kept[n] = p.copy_out(QX[:, n, :], o, to)
            o.done(kept[n])

        def units(heads):
            for h in heads:
                cell = []

                def out(cell=cell):
                    if not cell:
                        cell.append(p.held.get())
                    return cell[0]

                for i in range(4):
                    yield p.attend(QX[:, h, i * P:(i + 1) * P], KX[:, h, :],
                                   lambda j, h=h: VX[:, j, h * P:(h + 1) * P], 0, i, M, None, lambda h=h: [qx[h], kx[h], vx], out,
                                   lambda o, i=i: o.ap[:, i * P:(i + 1) * P], i == 0, i == 3,
                                   lambda o, to, h=h: emit(h, o, to))

        p.bg.append(lambda: qx[1] and kx[3])
        p.bg.extend(units((0, 1)))
        qproj(1)
        p.bg.append(lambda: qx[3])
        p.burst, p.depth = 2, 10
        p.pipeline(units((2, 3)))
        p.burst, p.depth = 1, 6
        for n in range(4):
            yt[n] = p.parts(p.HH[:, n, :], p.HL[:, n, :], QX[:, n, :], [kept[n]], p.dve, p.hfree)
        sg.done(*qx)
        p.less_tmp(more)
        r = p.project_out("wo_x", l * 2, 4, 512, H, yt, p.update_plain, "rms")
    p.barrier()
    return r


def rope_tables(p):
    ang, n = p.C[:, 2816:3328], p.C[:, 3328:3840]
    base = p.base
    tr = p.load("misc", p.POSI, p.dram["positions"], base)
    for _ in range(24):
        yield
    t = p.dve([tr, base], lambda e: e.tensor_copy(n[0:1, :], p.POSI))
    yield
    b = p.banks.get()
    tb = p.mm([t, b.w, p.cc_t], b.ap, p.one[0:1, :].to_broadcast([1, P]), n[0:1, :], sig=True)
    yield
    ta = p.dve([tb], lambda e: e.tensor_scalar(ang, b.ap, p.inv, None, ALU.mult))
    b.done(ta)
    p.rope_t = []
    t = ta
    for r, shift in ((p.SIN2, 0.0), (p.COS2, 0.25)):
        t = p.dve([t], lambda e: e.tensor_scalar(n, ang, 1.0 / TWO_PI, shift, ALU.mult, ALU.add))
        t = p.dve([t], lambda e: e.tensor_scalar(n, n, MAGIC, None, ALU.add))
        yield
        t = p.dve([t], lambda e: e.tensor_scalar(n, n, -MAGIC, None, ALU.add))
        t = p.dve([t], lambda e: e.scalar_tensor_tensor(r, n, -C1, ang, ALU.mult, ALU.add))
        yield
        t = p.dve([t], lambda e: e.scalar_tensor_tensor(r, n, -C2, r, ALU.mult, ALU.add))
        t = p.dve([t], lambda e: e.scalar_tensor_tensor(r, n, -C3, r, ALU.mult, ALU.add))
        yield
        t = p.dve([t], lambda e: e.tensor_scalar(r, r, shift * TWO_PI, PI_LOW, ALU.add, ALU.min))
        t = p.dve([t], lambda e: e.tensor_scalar(r, r, -PI_LOW, None, ALU.max))
        yield
        p.rope_t.append(p.act([t], lambda e: e.activation(r, r, ACT.Sin)))
        yield
    s = p.small.get()
    lv = p.vec("lam", 0, 4)
    t = p.dve([s.w], lambda e: e.tensor_tensor(s.ap[0:64, 0:2], lv[0:64, 0:2], lv[0:64, 2:4], ALU.mult))
    b = p.banks.get()
    tb = p.mm([t, b.w], b.ap[:, 0:2], p.one[0:64, :].to_broadcast([64, P]), s.ap[0:64, 0:2], sig=True)
    t = p.act([tb], lambda e: e.activation(s.ap[:, 2:4], b.ap[:, 0:2], ACT.Exp))
    b.done(t)
    t = p.dve([t], lambda e: e.tensor_tensor(s.ap[:, 4:5], s.ap[:, 3:4], s.ap[:, 2:3], ALU.subtract))
    p.lam_t = p.dve([t], lambda e: e.tensor_scalar(p.LAM[:, 0:1], s.ap[:, 4:5], -(0.8 - 0.6), None, ALU.add))
    s.done(p.lam_t)


def whole(p):
    p.mod_t = {}
    p.vec_t = p.load("vec", p.VEC[:, :], p.dram["vecs"])
    p.cond_t = p.act([p.vec_t], lambda e: e.activation(p.COND[:, :], p.vec("c", 0, 8), ACT.Silu))
    tx = p.ada_first(8)
    p.pe([p.cc_t], lambda e: e.nop(), sig=False)
    p.dve([p.cc_t, p.vec_t], lambda e: e.nop(), sig=False)
    p.x_t = [tx] * NT
    p.fill = [(0, c) for c in range(8, 36)] + [(1, c) for c in range(36)]
    p.modulate_first()
    ffn1 = {"gate": "ffn1_w_gate", "up": "ffn1_w_up", "down": ["ffn1_down0", "ffn1_down1", "ffn1_down2"], "n_up": 11}
    ffn2 = {"gate": "ffn2_w_gate", "up": "ffn2_w_up", "down": ["ffn2_down0", "ffn2_down1", "ffn2_down2"], "n_up": 11}
    for l in range(2):
        gt = {}

        def gated(which):
            def update(n, b, tok):
                if which not in gt:
                    gt[which] = p.gate(l, which, 0.5)
                p.update_gated(n, b, tok, *gt[which])
            return update

        p.every = 2
        mean = p.ffn("swiglu", ffn1, l, FFN_GROUPS, gated(2), "ln")
        gt[2][0].done(p.x_t[7])
        p.layer_norm(l, 0, mean, (l, 3, 4))
        mean = first_mixer(p, l)
        p.layer_norm(l, 1, mean, (l, 6, 7))
        if l == 1:
            p.barrier()
            p.c2_t = p.load("c2", p.C[:, 1024:1024 + p.c2n], p.dram["c2"], p.base)
            p.bg.append(rope_tables(p))
        mean = p.ffn("swiglu", ffn2, l, FFN_GROUPS, gated(8), "ln")
        gt[8][0].done(p.x_t[7])
        sums = p.layer_norm(l, 2, mean, (1, 0, 1) if l == 0 else None)
    assert not p.fill
    p.pipeline()
    mlp = {"up": "w_up", "down": ["down_m0", "down_m1", "down_m2", "down_m3"], "n_up": 16}
    for l in range(2):
        p.rms_norm("g_mix", l, sums)
        yt = even_mixer(p) if l == 0 else odd_mixer(p)
        sums = cross(p, l, ("w_out_e", "w_out_o")[l], yt)
        p.rms_norm("g_mlp", l, sums)
        sums = p.ffn("relu2", mlp, l, MLP_GROUPS, p.update_plain, "rms" if l == 0 else None)
    for n in range(NT):
        p.load("out", p.out[:, n, :], p.XR[:, n, :], [p.x_t[n]])
    p.sp([("out", 16 * NT)], lambda e: e.nop(), sig=False)


def build(nc, dram, out, tables):
    ctx = ExitStack()
    with ctx:
        def sb(name, shape, dt=F32):
            return ctx.enter_context(nc.sbuf_tensor("s_" + name, shape, dt))

        (cc, ccw), (c1, c1w), (c2, c2w) = tables
        mem = {"NS": 3, "NW": 2}
        mem["psum"] = [ctx.enter_context(nc.psum_tensor(f"ps{i}", [P, S], F32)) for i in range(8)]
        mem["XR"] = sb("xr", [P, NT, S])
        mem["HH"], mem["HL"] = sb("hh", [P, NT, S], F32R), sb("hl", [P, NT, S], F32R)
        mem["STAGE"] = sb("stage", [P, 3, 2048])
        mem["WH"], mem["WL"] = sb("wh", [P, 2, 2048], F32R), sb("wl", [P, 2, 2048], F32R)
        mem["TMP"] = sb("tmp", [P, 6, S])
        mem["CC"] = CC = sb("cc", [P, cc.shape[1]])
        mem["C"] = C = sb("c", [P, c1.shape[1]])
        mem["VEC"] = sb("vec", [P, NVEC])
        mem["MOD"] = sb("mod", [P, 144])
        mem["COND"] = sb("cond", [P, 8])
        mem["SM"] = sb("sm", [P, 8, 32])
        mem["NY"] = sb("ny", [P, 2, 112])
        mem["NV"], mem["NA"] = sb("nv", [P, 112]), sb("na", [P, 112])
        mem["NU"] = sb("nu", [P, 112], I32)
        mem["NG"] = mem["NU"][:, :].bitcast(F32)
        mem["LAM"] = sb("lam", [P, 1])
        for k, (at, n) in ccw.items():
            mem[k] = CC[:, at:at + n]
        mem["c1"] = lambda k: C[:, c1w[k][0]:c1w[k][0] + c1w[k][1]]
        mem["COS2"], mem["SIN2"] = C[:, 0:512], C[:, 512:1024]
        mem["c2"] = lambda k: C[:, 1024 + c2w[k][0]:1024 + c2w[k][0] + c2w[k][1]]
        mem["POSI"] = C[0:1, 4096:4608].bitcast(I32)
        mem["c2n"] = c2.shape[1]
        mem["sems"] = {k: ctx.enter_context(nc.semaphore("q_" + k)) for k in SEMS}
        dry = Prog(nc, dram, out, None, mem, "a")
        whole(dry)
        p = Prog(nc, dram, out, dry.order, mem, "b")
        whole(p)
        assert p.taken == len(p.plan)


def _tiles(w, nc_):
    k, n = w.shape
    a = w.reshape(k // P, P, n // nc_, nc_).transpose(2, 1, 0, 3)
    return a.reshape(n // nc_, P, (k // P) * nc_)


def _cols(v):
    return v.reshape(-1, P).T


def kernel(**inputs):
    import concourse.bacc as _bacc
    from concourse import mybir as _mybir
    from concourse.bass_utils import run_bass_kernel_spmd as _run

    a = {k: np.asarray(v) for k, v in inputs.items()}
    arr = {}

    def put(name, parts):
        arr[name] = np.ascontiguousarray(np.concatenate(parts, 0))

    put("w_ada", [_tiles(a["w_ada"][l], 256) for l in range(2)])
    for f in ("ffn1", "ffn2"):
        for g in ("gate", "up"):
            put(f"{f}_w_{g}", [_tiles(a[f"{f}_w_{g}"][l], 256) for l in range(2)])
        for gi, (g0, G) in enumerate(FFN_GROUPS):
            put(f"{f}_down{gi}", [_tiles(a[f"{f}_w_down"][l][g0 * P:(g0 + G) * P], 256) for l in range(2)])
    put("w_in", [_tiles(a["w_in"][l], 256) for l in range(2)])
    put("w_out", [_tiles(a["w_out"][l], 256) for l in range(2)])
    e = a["w_in_e_2"][0]
    order = [e[:, 0:1024], e[:, 1536:2048], e[:, 2048:2560], e[:, 1024:1536]]
    put("w_in_e", [_tiles(w, 256) for w in order])
    ki, wi = e[:, 2560:2624], e[:, 2624:2628]
    put("w_kiwi", [_tiles(np.concatenate([ki, ki, wi], 1), 132)])
    put("w_kv_up", [_tiles(a["w_kv_up_b_2"][0], 1024)])
    put("w_out_e", [_tiles(a["w_out_e_2"][0], 256)])
    put("w_in_o", [_tiles(a["w_in_o_2"][0], 256)])
    put("w_pool", [a["w_pool_2"][0].transpose(1, 0, 2).reshape(1, P, 512)])
    put("w_out_o", [_tiles(a["w_out_o_2"][0], 256)])
    put("wq_x", [_tiles(a["wq_x_2"][l], 256) for l in range(2)])
    put("wkv_x", [_tiles(a["wkv_x_2"][l], 256) for l in range(2)])
    put("wo_x", [_tiles(a["wo_x_2"][l], 512) for l in range(2)])
    put("w_up", [_tiles(a["w_up_2"][l], 256) for l in range(2)])
    for gi, (g0, G) in enumerate(MLP_GROUPS):
        put(f"down_m{gi}", [_tiles(a["w_down_2"][l][g0 * P:(g0 + G) * P], 256) for l in range(2)])
    arr["xT"] = np.ascontiguousarray(a["x"][0].T.reshape(NT, P, S).transpose(1, 0, 2))
    arr["memT"] = np.ascontiguousarray(a["mem_2"][0].T.reshape(8, P, 256).transpose(1, 0, 2))
    arr["positions"] = np.ascontiguousarray(a["positions_2"])
    two = lambda v: np.concatenate([v, v])[:, None]
    lam = np.zeros((P, 4), np.float32)
    for i, n in enumerate(("lam_q1_2", "lam_q2_2", "lam_k1_2", "lam_k2_2")):
        lam[0:64, i] = a[n][0]
    arr["vecs"] = np.ascontiguousarray(np.concatenate([
        _cols(a["c"][0]), _cols(a["b_ada"].reshape(-1)), _cols(a["ln_gain"].reshape(-1)),
        _cols(a["ln_bias"].reshape(-1)), _cols(a["g_mix_2"].reshape(-1)), _cols(a["g_xattn_2"].reshape(-1)),
        _cols(a["g_mem_2"].reshape(-1)), _cols(a["g_mlp_2"].reshape(-1)), _cols(a["gq_x_2"].reshape(-1)),
        _cols(a["gk_x_2"].reshape(-1)), two(a["gq_a_2"][0]), two(a["gk_a_2"][0]), two(a["gq_b_2"][0]),
        two(a["gk_b_2"][0]), two(a["g_kidx_2"][0]), _cols(a["g_sub_a_2"].reshape(-1)),
        _cols(a["g_kv_b_2"].reshape(-1)), _cols(a["conv_w_2"].reshape(-1)),
        _cols(a["pool_scale_2"].reshape(-1)), lam], 1))
    tables = consts()
    arr["cc"], arr["c1"], arr["c2"] = (t[0] for t in tables)

    nc = _bacc.Bacc("TRN2", target_bir_lowering=False, num_devices=1)
    dram = {}
    for name, v in arr.items():
        dram[name] = nc.dram_tensor(f"in_{name}", v.shape, _mybir.dt.from_np(v.dtype), kind="ExternalInput").ap()
    out = nc.dram_tensor("out_0", (P, NT, S), F32, kind="ExternalOutput").ap()
    build(nc, dram, out, tables)
    r = _run(nc, [{f"in_{k}": v for k, v in arr.items()}], core_ids=[0])
    got = r.results[0]["out_0"]
    return np.ascontiguousarray(got.transpose(1, 0, 2).reshape(D, S).T).reshape(1, S, D)
```
